# Optimizing a Trainium2 kernel written in Bass

```python
import math
import jax
import jax.numpy as jnp
from jax import lax
import numpy as np

D_MODEL = 1024
BATCH = 1
SEQ = 1024
DEPTH = 1

HY_WIDTH = 768
HY_ORDER = 2
HY_SHORT_CONV = 3
HY_EMB_DIM = 33
HY_FILTER_HIDDEN = 64
HY_FAST_DECAY = 0.3
HY_SLOW_DECAY = 1.5
HY_DECAY_TARGET = 1e-2
HY_MOD_SHIFT = 0.0
HEAD_DIM = 64
HEADS_PER_GROUP = 8
DILATED_GROUPS = ((128, 1), (512, 4), (2048, 16))
N_GROUPS = 3
AT_HEADS = N_GROUPS * HEADS_PER_GROUP
AT_QKV = AT_HEADS * HEAD_DIM
AT_WIDTH = HEADS_PER_GROUP * HEAD_DIM
BAND_BLOCK = 64
NORM_EPS = 1e-6
NEG_INF = -1e30
IN_COLS = 3 * HY_WIDTH + HY_WIDTH + 3 * AT_QKV + AT_WIDTH + 2 * D_MODEL

kernel_name = 'hybrid_hyena_dilated_attn_encoder_block'

def _rmsnorm(x, g):
    xf = x.astype(jnp.float32)
    y = xf * lax.rsqrt(jnp.mean(xf * xf, axis=-1, keepdims=True) + NORM_EPS)
    return (y * g.astype(jnp.float32)).astype(x.dtype)

def _alibi_slopes(n):
    return 2.0 ** (-8.0 * jnp.arange(1, n + 1, dtype=jnp.float32) / n)

def _short_conv(z, w, b):
    L = z.shape[1]
    p = HY_SHORT_CONV // 2
    zp = jnp.pad(z, ((0, 0), (p, p), (0, 0)))
    out = b
    for j in range(HY_SHORT_CONV):
        out = out + zp[:, j:j + L] * w[j]
    return out

def _hyena_filters(L, w1, b1, w2, b2, w3, b3, w4, freq):
    f32 = jnp.float32
    t = jnp.linspace(0.0, 1.0, L, dtype=f32)[:, None]
    bands = (HY_EMB_DIM - 1) // 2
    w = 2.0 * math.pi * jnp.arange(L, dtype=f32)[:, None] / L
    f = jnp.linspace(1e-4, bands - 1, bands, dtype=f32)[None, :]
    z = jnp.concatenate([t, jnp.cos(f * w), -jnp.sin(f * w)], axis=-1)
    fr = freq.astype(f32)
    h = jnp.sin(fr * (z @ w1.astype(f32) + b1.astype(f32)))
    h = jnp.sin(fr * (h @ w2.astype(f32) + b2.astype(f32)))
    h = jnp.sin(fr * (h @ w3.astype(f32) + b3.astype(f32)))
    h = (h @ w4.astype(f32)).reshape(L, HY_ORDER, 2, HY_WIDTH)
    max_decay = math.log(HY_DECAY_TARGET) / HY_FAST_DECAY
    min_decay = math.log(HY_DECAY_TARGET) / HY_SLOW_DECAY
    deltas = jnp.linspace(min_decay, max_decay, HY_WIDTH, dtype=f32)
    decay = jnp.exp(-t * jnp.abs(deltas)[None, :])
    h = h * (decay + HY_MOD_SHIFT)[:, None, None, :]
    h_fwd, h_bwd = h[:, :, 0], h[:, :, 1]
    k_circ = jnp.concatenate([h_fwd, jnp.zeros((1, HY_ORDER, HY_WIDTH), f32), h_bwd[1:][::-1]], axis=0)
    return jnp.fft.rfft(k_circ, axis=0)

def _fft_conv(u, k_f, skip):
    L = u.shape[1]
    U = jnp.fft.rfft(u, n=2 * L, axis=1)
    y = jnp.fft.irfft(U * k_f[None], n=2 * L, axis=1)[:, :L]
    return y + u * skip.astype(jnp.float32)

def _hyena(z_in, conv_w, conv_b, w1, b1, w2, b2, w3, b3, w4, freq, skip):
    L = z_in.shape[1]
    zc = _short_conv(z_in, conv_w, conv_b).astype(jnp.float32)
    v, x1, x2 = jnp.split(zc, 3, axis=-1)
    k_f = _hyena_filters(L, w1, b1, w2, b2, w3, b3, w4, freq)
    y = x1 * _fft_conv(v, k_f[:, 0], skip[0])
    y = x2 * _fft_conv(y, k_f[:, 1], skip[1])
    return y

def _band_group(q, k, v, window, dilation, slopes):
    B, H, S, Dh = q.shape
    half = window // (2 * dilation)
    n = S // dilation
    nb = -(-n // BAND_BLOCK)
    pad = nb * BAND_BLOCK - n

    def to_blocks(t):
        t = t.reshape(B, H, n, dilation, Dh).transpose(0, 1, 3, 2, 4)
        t = jnp.pad(t, ((0, 0), (0, 0), (0, 0), (0, pad), (0, 0)))
        return t.reshape(B, H, dilation, nb, BAND_BLOCK, Dh)

    def band(t):
        tp = jnp.pad(t, ((0, 0), (0, 0), (0, 0), (1, 1), (0, 0), (0, 0)))
        return jnp.concatenate([tp[:, :, :, :-2], tp[:, :, :, 1:-1], tp[:, :, :, 2:]], axis=4)

    qb = to_blocks(q)
    kw = band(to_blocks(k))
    vw = band(to_blocks(v))
    qi = jnp.arange(nb)[:, None] * BAND_BLOCK + jnp.arange(BAND_BLOCK)[None, :]
    ki = (jnp.arange(nb)[:, None] - 1) * BAND_BLOCK + jnp.arange(3 * BAND_BLOCK)[None, :]
    rel = qi[:, :, None] - ki[:, None, :]
    valid = (jnp.abs(rel) <= half) & (ki[:, None, :] >= 0) & (ki[:, None, :] < n)
    dist = (dilation * jnp.abs(rel)).astype(jnp.float32)
    s = jnp.einsum('bhrnqd,bhrnkd->bhrnqk', qb, kw) * (HEAD_DIM ** -0.5)
    s = s - slopes[None, :, None, None, None, None] * dist[None, None, None]
    s = jnp.where(valid[None, None, None], s, NEG_INF)
    m = jnp.max(s, axis=-1)
    p = jnp.exp(s - m[..., None])
    den = jnp.sum(p, axis=-1)
    o = jnp.einsum('bhrnqk,bhrnkd->bhrnqd', p, vw) / den[..., None]
    lse = m + jnp.log(den)
    o = o.reshape(B, H, dilation, nb * BAND_BLOCK, Dh)[:, :, :, :n].transpose(0, 1, 3, 2, 4).reshape(B, H, S, Dh)
    lse = lse.reshape(B, H, dilation, nb * BAND_BLOCK)[:, :, :, :n].transpose(0, 1, 3, 2).reshape(B, H, S)
    return o, lse

def _dilated_attention(q, k, v, slopes):
    outs, lses = [], []
    for g, (window, dilation) in enumerate(DILATED_GROUPS):
        o, lse = _band_group(q[:, :, g].transpose(0, 2, 1, 3), k[:, :, g].transpose(0, 2, 1, 3),
                             v[:, :, g].transpose(0, 2, 1, 3), window, dilation, slopes)
        outs.append(o)
        lses.append(lse)
    wts = jax.nn.softmax(jnp.stack(lses, axis=0), axis=0)
    return jnp.sum(wts[..., None] * jnp.stack(outs, axis=0), axis=0)

def setup_inputs(seed: int = 0) -> dict:
    key = jax.random.key(seed)
    ks = jax.random.split(key, 20)
    f32 = jnp.float32

    def nrm(k, shape, scale):
        return jax.random.normal(k, shape, f32) * scale

    return {
        'x': nrm(ks[0], (BATCH, SEQ, D_MODEL), 1.0),
        'norm_g': 1.0 + nrm(ks[1], (DEPTH, D_MODEL), 0.05),
        'w_in': nrm(ks[2], (DEPTH, D_MODEL, IN_COLS), D_MODEL ** -0.5),
        'b_in': nrm(ks[3], (DEPTH, IN_COLS), 0.02),
        'conv_w': nrm(ks[4], (DEPTH, HY_SHORT_CONV, 3 * HY_WIDTH), HY_SHORT_CONV ** -0.5),
        'conv_b': nrm(ks[5], (DEPTH, 3 * HY_WIDTH), 0.02),
        'hf_w1': nrm(ks[6], (DEPTH, HY_EMB_DIM, HY_FILTER_HIDDEN), HY_EMB_DIM ** -0.5),
        'hf_b1': nrm(ks[7], (DEPTH, HY_FILTER_HIDDEN), 0.02),
        'hf_w2': nrm(ks[8], (DEPTH, HY_FILTER_HIDDEN, HY_FILTER_HIDDEN), HY_FILTER_HIDDEN ** -0.5),
        'hf_b2': nrm(ks[9], (DEPTH, HY_FILTER_HIDDEN), 0.02),
        'hf_w3': nrm(ks[10], (DEPTH, HY_FILTER_HIDDEN, HY_FILTER_HIDDEN), HY_FILTER_HIDDEN ** -0.5),
        'hf_b3': nrm(ks[11], (DEPTH, HY_FILTER_HIDDEN), 0.02),
        'hf_w4': nrm(ks[12], (DEPTH, HY_FILTER_HIDDEN, HY_ORDER * 2 * HY_WIDTH), 0.02),
        'hf_freq': 1.0 + nrm(ks[13], (DEPTH, HY_FILTER_HIDDEN), 0.05),
        'hy_skip': nrm(ks[14], (DEPTH, HY_ORDER, HY_WIDTH), 0.1),
        'q_norm_g': 1.0 + nrm(ks[15], (DEPTH, HEAD_DIM), 0.05),
        'k_norm_g': 1.0 + nrm(ks[16], (DEPTH, HEAD_DIM), 0.05),
        'w_hy_out': nrm(ks[17], (DEPTH, HY_WIDTH, D_MODEL), HY_WIDTH ** -0.5),
        'w_at_out': nrm(ks[18], (DEPTH, AT_WIDTH, D_MODEL), AT_WIDTH ** -0.5),
        'w_out': nrm(ks[19], (DEPTH, D_MODEL, D_MODEL), D_MODEL ** -0.5),
    }

def reference(x, norm_g, w_in, b_in, conv_w, conv_b, hf_w1, hf_b1, hf_w2, hf_b2, hf_w3, hf_b3, hf_w4,
              hf_freq, hy_skip, q_norm_g, k_norm_g, w_hy_out, w_at_out, w_out):
    B, S, _ = x.shape
    f32 = jnp.float32
    slopes = _alibi_slopes(HEADS_PER_GROUP)
    o1 = 3 * HY_WIDTH
    o2 = o1 + HY_WIDTH
    o3 = o2 + 3 * AT_QKV
    o4 = o3 + AT_WIDTH
    o5 = o4 + D_MODEL
    for i in range(DEPTH):
        xn = _rmsnorm(x, norm_g[i])
        proj = xn @ w_in[i] + b_in[i]
        hy_in, hy_gate = proj[..., :o1], proj[..., o1:o2]
        qkv, at_gate = proj[..., o2:o3], proj[..., o3:o4]
        mg_h, mg_a = proj[..., o4:o5], proj[..., o5:]
        y_h = _hyena(hy_in, conv_w[i], conv_b[i], hf_w1[i], hf_b1[i], hf_w2[i], hf_b2[i], hf_w3[i], hf_b3[i],
                     hf_w4[i], hf_freq[i], hy_skip[i])
        u_h = (y_h * jax.nn.silu(hy_gate.astype(f32))).astype(x.dtype) @ w_hy_out[i]
        q, k, v = jnp.split(qkv, 3, axis=-1)
        q = _rmsnorm(q.reshape(B, S, N_GROUPS, HEADS_PER_GROUP, HEAD_DIM), q_norm_g[i]).astype(f32)
        k = _rmsnorm(k.reshape(B, S, N_GROUPS, HEADS_PER_GROUP, HEAD_DIM), k_norm_g[i]).astype(f32)
        v = v.reshape(B, S, N_GROUPS, HEADS_PER_GROUP, HEAD_DIM).astype(f32)
        o = _dilated_attention(q, k, v, slopes).transpose(0, 2, 1, 3).reshape(B, S, AT_WIDTH)
        u_a = (o * jax.nn.silu(at_gate.astype(f32))).astype(x.dtype) @ w_at_out[i]
        merged = jax.nn.sigmoid(mg_h) * u_h + jax.nn.sigmoid(mg_a) * u_a
        x = x + merged @ w_out[i]
    return x


_drawn_inputs = setup_inputs


def setup_inputs(seed=0):
    import zlib

    import numpy as np

    out = dict(_drawn_inputs(seed))
    spreads = {}
    factors = {'hf_b1': 4.566,
     'hf_b2': 4.061,
     'hf_b3': 3.887,
     'q_norm_g': 8.0,
     'k_norm_g': 8.0,
     'hf_freq': 2.681}
    for name, (base, spread) in spreads.items():
        noise = np.random.default_rng([zlib.crc32(name.encode()), seed]).standard_normal(out[name].shape)
        drawn = base * np.exp(spread * noise) if base else spread * noise
        out[name] = jnp.asarray(drawn.astype(out[name].dtype))
    for name, factor in factors.items():
        out[name] = (out[name] * factor).astype(out[name].dtype)
    return out
```

```python
from contextlib import ExitStack

import concourse.bass as bass
from concourse import mybir

F32 = mybir.dt.float32
ACT = mybir.ActivationFunctionType
ALU = mybir.AluOpType
AX = mybir.AxisListType
ds = bass.ds

P = 128
D = 1024
S = 1024
KT = D // P
HALF = 512
HY = 768
HYT = HY // P
HD = 64
PAIRS = 4
GROUPS = 3
COL_GATE_HY = 3 * HY
COL_QKV = 4 * HY
COL_GATE_AT = COL_QKV + 9 * 512
COL_MIX = COL_GATE_AT + 512
NB_IN = 80
EPS = 1e-6

ROW_CONV_W, ROW_CONV_B, ROW_QG, ROW_KG, ROW_HF = 0, 54, 72, 73, 74
ROWS_B = 78


def sbuf(ctx, nc, name, shape, dt=F32):
    return ctx.enter_context(nc.sbuf_tensor(name, shape, dt))


def sems(ctx, nc, *names):
    return [ctx.enter_context(nc.semaphore(n)) for n in names]


def count_from_one(nc, *counted):
    with nc.Block() as block:
        @block.sync
        def _(sync):
            for s in counted:
                sync.sem_inc(s, 1)


def wait_alone(eng, passed, sem, value):
    eng.wait_ge(sem, value)
    eng.sem_inc(passed, 1)


def w_view(w, k):
    return w.rearrange("(k p) n -> p k n", p=P) if k > 1 else w


def normalise(nc, ps, keep, x, norm_g, b_in, conv_w, conv_b, hf_b, q_g, k_g, squares):
    xn_t, sq, cols_in, cols_p = keep["xn_t"], keep["squares"], keep["cols_in"], keep["cols_p"]
    with ExitStack() as ctx:
        xt = sbuf(ctx, nc, "x_tok", [P, KT, D])
        xs = sbuf(ctx, nc, "x_scaled", [P, 2, D])
        junk = sbuf(ctx, nc, "x_squares", [P, 2, D])
        stat = sbuf(ctx, nc, "x_stat", [P, 4, KT])
        rows_in = sbuf(ctx, nc, "rows_in", [P, P])
        rows_p = sbuf(ctx, nc, "rows_p", [P, P])
        x_in = sems(ctx, nc, *[f"x_in{t}" for t in range(KT)])
        table_in, rows_clear, rows_ready, cols_done, cols_kept = sems(
            ctx, nc, "table_in", "rows_clear", "rows_ready", "cols_done", "cols_kept")
        squared, mean_done, root_done, rstd_done, scaled, turned, kept = sems(
            ctx, nc, "squared", "mean_done", "root_done", "rstd_done", "scaled", "turned", "kept")
        with nc.Block() as block:
            @block.sync
            def _(sync):
                for t in range(KT):
                    sync.dma_start(xt[:, t, :], x[t * P:(t + 1) * P, :]).then_inc(x_in[t], 16)

            @block.gpsimd
            def _(pool):
                pool.memset(rows_in[:], 0.0).then_inc(rows_clear, 1)
                pool.memset(rows_p[:], 0.0).then_inc(rows_clear, 1)

            @block.scalar
            def _(act):
                act.dma_start(sq[:], squares).then_inc(table_in, 16)
                act.wait_ge(rows_clear, 2)
                act.dma_start(rows_in[0:NB_IN, :], b_in.rearrange("a (c p) -> (a c) p", p=P)).then_inc(rows_ready, 16)
                act.dma_start(rows_in[NB_IN:NB_IN + KT, :], norm_g.rearrange("a (c p) -> (a c) p", p=P)).then_inc(rows_ready, 16)
                act.dma_start(rows_p[0:54, :], conv_w.rearrange("j (c p) -> (j c) p", p=P)).then_inc(rows_ready, 16)
                act.dma_start(rows_p[54:72, :], conv_b.rearrange("a (c p) -> (a c) p", p=P)).then_inc(rows_ready, 16)
                for e in range(2):
                    act.dma_start(rows_p[ROW_QG:ROW_QG + 1, e * HD:(e + 1) * HD], q_g).then_inc(rows_ready, 16)
                    act.dma_start(rows_p[ROW_KG:ROW_KG + 1, e * HD:(e + 1) * HD], k_g).then_inc(rows_ready, 16)
                for n, v in enumerate(hf_b):
                    act.dma_start(rows_p[ROW_HF + n:ROW_HF + n + 1, 0:HD], v).then_inc(rows_ready, 16)
                for t in range(KT):
                    act.wait_ge(x_in[t], 16)
                    if t >= 2:
                        act.wait_ge(squared, t - 1)
                    act.activation(junk[:, t % 2, :], xt[:, t, :], ACT.Square, accum_out=stat[:, 0, t:t + 1]).then_inc(squared, 1)
                act.wait_ge(mean_done, 1)
                act.activation(stat[:, 2, :], stat[:, 1, :], ACT.Sqrt).then_inc(root_done, 1)

            @block.vector
            def _(dve):
                dve.wait_ge(cols_done, 1)
                dve.tensor_copy(cols_in[:], ps[:, 0, 0:P]).then_inc(cols_kept, 1)
                dve.tensor_copy(cols_p[:], ps[:, 1, 0:P]).then_inc(cols_kept, 1)
                dve.wait_ge(squared, KT)
                dve.tensor_scalar(stat[:, 1, :], stat[:, 0, :], 1.0 / D, EPS, ALU.mult, ALU.add).then_inc(mean_done, 1)
                dve.wait_ge(root_done, 1)
                dve.reciprocal(stat[:, 3, :], stat[:, 2, :]).then_inc(rstd_done, 1)
                dve.wait_ge(rstd_done, 1)
                dve.wait_ge(cols_kept, 2)
                gain = cols_in[:, NB_IN:NB_IN + KT].unsqueeze(2).to_broadcast([P, KT, P])
                for t in range(KT):
                    for u in ([0, 1] if t == 0 else [t + 1] if t + 1 < KT else []):
                        if u >= 2:
                            dve.wait_ge(turned, u - 1)
                        dve.tensor_scalar(xs[:, u % 2, :], xt[:, u, :], stat[:, 3, u:u + 1], None, ALU.mult).then_inc(scaled, 1)
                    dve.wait_ge(turned, t + 1)
                    b = 4 * (t % 2)
                    for hh in range(2):
                        dve.tensor_tensor(xn_t[:, 4 * hh:4 * hh + 4, t * P:(t + 1) * P],
                                          ps[:, b + hh, :].rearrange("p (k n) -> p k n", n=P),
                                          gain[:, 4 * hh:4 * hh + 4, :], ALU.mult).then_inc(kept, 1)

            @block.tensor
            def _(pe):
                ident = sq[:, 0, :]
                pe.wait_ge(table_in, 16)
                pe.wait_ge(rows_ready, 16 * 12)
                pe.transpose(ps[:, 0, 0:P], rows_in[:], ident)
                pe.transpose(ps[:, 1, 0:P], rows_p[:], ident).then_inc(cols_done, 1)
                pe.wait_ge(cols_kept, 2)
                for t in range(KT):
                    pe.wait_ge(scaled, t + 1)
                    if t >= 2:
                        pe.wait_ge(kept, 2 * (t - 1))
                    for k in range(KT):
                        last = pe.transpose(ps[:, 4 * (t % 2) + k // 4, (k % 4) * P:(k % 4 + 1) * P],
                                            xs[:, t % 2, k * P:(k + 1) * P], ident)
                    last.then_inc(turned, 1)


def hyena_in(nc, ps, keep, w_in, v_tok, x1_tok, x2_t):
    xn_t, ident, cols_in, cols_p = keep["xn_t"], keep["squares"][:, 0, :], keep["cols_in"], keep["cols_p"]
    w_cols = w_view(w_in, KT)
    with ExitStack() as ctx:
        w = sbuf(ctx, nc, "w_hy", [P, 4, KT, P])
        z = sbuf(ctx, nc, "z_pad", [P, 3, S + 2])
        zc = sbuf(ctx, nc, "z_conv", [P, 3, S])
        gate = sbuf(ctx, nc, "hy_gate", [P, S])
        tok = sbuf(ctx, nc, "z_tok", [P, 2, 8, P])
        w_ready = sems(ctx, nc, *[f"w_ready{s}" for s in range(4)])
        tok_out = sems(ctx, nc, "tok_out0", "tok_out1")
        [x2_out] = sems(ctx, nc, "x2_out")
        proj_done, bank_free, z_ready, z_free, conv_step, conv_done, turned, turn_free, tok_ready, gate_ready, mul_done = sems(
            ctx, nc, "proj_done", "bank_free", "z_ready", "z_free", "conv_step", "conv_done", "turned", "turn_free",
            "tok_ready", "gate_ready", "mul_done")
        count_from_one(nc, *tok_out, turned, x2_out)

        with nc.Block() as block:
            @block.sync
            def _(sync):
                for s in range(4):
                    sync.dma_start(w[:, s], w_cols[:, :, s * HY:s * HY + P]).then_inc(w_ready[s], 16)
                with sync.Fori(1, HYT) as i:
                    for s in range(4):
                        sync.wait_ge(proj_done, i * 4 + (s - 3))
                        sync.dma_start(w[:, s], w_cols[:, :, ds(i * P + s * HY, P)]).then_inc(w_ready[s], 16)
                    sync.wait_ge(mul_done, i)
                    sync.dma_start(x2_t[ds(i * P - P, P), :], zc[:, 2, :]).then_inc(x2_out, 16)
                sync.wait_ge(mul_done, HYT)
                sync.dma_start(x2_t[(HYT - 1) * P:HYT * P, :], zc[:, 2, :]).then_inc(x2_out, 16)
                sync.wait_ge(x2_out, 1 + 16 * HYT)

            @block.tensor
            def _(pe):
                with pe.Fori(0, HYT) as i:
                    for s in range(4):
                        pe.wait_ge(w_ready[s], i * 16 + 16)
                        b = 2 * (s % 2)
                        pe.wait_ge(bank_free, i * 4 + s + 1)
                        for h in range(2):
                            for k in range(KT):
                                last = pe.matmul(ps[:, b + h, :], w[:, s, k, :], xn_t[:, k, h * HALF:(h + 1) * HALF],
                                                 start=(k == 0), stop=(k == KT - 1))
                        last.then_inc(proj_done, 1)
                        if s in (1, 2):
                            r = s - 1
                            pe.wait_ge(conv_done, i * 3 + r + 1)
                            pe.wait_ge(turn_free, i * 2 + r + 1)
                            rows = zc[:, r, :].rearrange("p (s j) -> p j s", j=8)
                            for j in range(8):
                                last = pe.transpose(ps[:, 4 + 2 * r + j // 4, (j % 4) * P:(j % 4 + 1) * P], rows[:, j], ident)
                            last.then_inc(turned, 1)

            @block.scalar
            def _(act):
                act.sem_inc(bank_free, 2)
                with act.Fori(0, HYT) as i:
                    for s in range(4):
                        b = 2 * (s % 2)
                        act.wait_ge(proj_done, i * 4 + s + 1)
                        bias = cols_in[:, ds(i + HYT * s, 1)]
                        src = ps[:, b:b + 2, :].rearrange("p a n -> p (a n)")
                        act.wait_ge(z_free, i * 4 + s + 1)
                        if s < 3:
                            act.activation(z[:, s, 1:S + 1], src, ACT.Identity, bias=bias).then_inc(z_ready, 1)
                            act.wait_ge(z_ready, i * 3 + s + 1)
                        else:
                            act.activation(gate[:], src, ACT.Silu, bias=bias).then_inc(gate_ready, 1)
                            act.wait_ge(gate_ready, i + 1)
                        act.sem_inc(bank_free, 1)
                        if s >= 2:
                            r = s - 2
                            act.wait_ge(turned, 1 + i * 2 + r + 1)
                            act.wait_ge(tok_out[r], 1 + i * 16)
                            act.activation(tok[:, r].rearrange("p j n -> p (j n)"),
                                           ps[:, 4 + 2 * r:6 + 2 * r, :].rearrange("p a n -> p (a n)"), ACT.Copy).then_inc(tok_ready, 1)
                            act.wait_ge(tok_ready, i * 2 + r + 1)
                            act.sem_inc(turn_free, 1)
                            dst = (v_tok, x1_tok)[r]
                            act.dma_start(dst[:, :, ds(i * P, P)].rearrange("j q c -> q j c"), tok[:, r]).then_inc(tok_out[r], 16)
                for r in range(2):
                    act.wait_ge(tok_out[r], 1 + 16 * HYT)

            @block.gpsimd
            def _(pool):
                pool.sem_inc(turn_free, 2)

            @block.vector
            def _(dve):
                dve.memset(z[:], 0.0).then_inc(conv_step, 1)
                dve.wait_ge(conv_step, 1)
                dve.sem_inc(z_free, 4)
                with dve.Fori(0, HYT) as i:
                    for s in range(3):
                        tap = [cols_p[:, ds(i + HYT * s + 18 * j, 1)] for j in range(3)]
                        shift = cols_p[:, ds(i + HYT * s + ROW_CONV_B, 1)]
                        dve.wait_ge(z_ready, i * 3 + s + 1)
                        if s < 2:
                            dve.wait_ge(turned, 1 + i * 2 + s)
                        else:
                            dve.wait_ge(x2_out, 1 + i * 16)
                        dve.tensor_scalar(zc[:, s, :], z[:, s, 0:S], tap[0], shift, ALU.mult, ALU.add).then_inc(conv_step, 1)
                        dve.wait_ge(conv_step, i * 6 + 2 * s + 2)
                        dve.scalar_tensor_tensor(zc[:, s, :], z[:, s, 1:S + 1], tap[1], zc[:, s, :], ALU.mult, ALU.add).then_inc(conv_step, 1)
                        dve.wait_ge(conv_step, i * 6 + 2 * s + 3)
                        dve.scalar_tensor_tensor(zc[:, s, :], z[:, s, 2:S + 2], tap[2], zc[:, s, :], ALU.mult, ALU.add).then_inc(conv_done, 1)
                        dve.wait_ge(conv_done, i * 3 + s + 1)
                        dve.sem_inc(z_free, 1)
                    dve.wait_ge(gate_ready, i + 1)
                    dve.tensor_tensor(zc[:, 2, :], zc[:, 2, :], gate[:], ALU.mult).then_inc(mul_done, 1)
                    dve.wait_ge(mul_done, i + 1)
                    dve.sem_inc(z_free, 1)


CH = 256
CHUNKS = HY // CH
NJ, NM = 8, 16
INV_2PI = 0.15915494309189535
ROUND = 12582912.0
TWO_PI = (6.28125, 0.0019350051879882812, 3.019916050e-07)
PI_BELOW = 3.1415925


def filter_mlp(nc, ps, keep, h_t, work, z_t, hf_w):
    cols_p = keep["cols_p"]
    with ExitStack() as ctx:
        feat = sbuf(ctx, nc, "features", [33, S])
        w = sbuf(ctx, nc, "hf_w", [HD, 3, HD])
        loaded, prod, arg, done = sems(ctx, nc, "mlp_loaded", "mlp_prod", "mlp_arg", "mlp_done")
        arg_x, turns = work[0:HD, 0:S], work[0:HD, S:2 * S]
        with nc.Block() as block:
            @block.sync
            def _(sync):
                sync.dma_start(feat[:], z_t).then_inc(loaded, 16)
                for n, v in enumerate(hf_w):
                    sync.dma_start(w[0:v.shape[0], n, :], v).then_inc(loaded, 16)

            @block.tensor
            def _(pe):
                pe.wait_ge(loaded, 64)
                for n in range(3):
                    if n:
                        pe.wait_ge(done, n)
                    for h in range(2):
                        src = feat[:, h * HALF:(h + 1) * HALF] if n == 0 else h_t[:, h * HALF:(h + 1) * HALF]
                        pe.matmul(ps[0:HD, h, :], w[0:33 if n == 0 else HD, n, :], src, start=True, stop=True).then_inc(prod, 1)

            @block.vector
            def _(dve):
                freq = cols_p[0:HD, ROW_HF + 3:ROW_HF + 4]
                step = 0
                for n in range(3):
                    dve.wait_ge(prod, 2 * n + 2)
                    src = ps[0:HD, 0:2, :].rearrange("p a n -> p (a n)")
                    dve.tensor_scalar(arg_x, src, cols_p[0:HD, ROW_HF + n:ROW_HF + n + 1], freq, ALU.add, ALU.mult).then_inc(arg, 1)
                    step += 1
                    dve.wait_ge(arg, step)
                    dve.tensor_scalar(turns, arg_x, INV_2PI, ROUND, ALU.mult, ALU.add).then_inc(arg, 1)
                    step += 1
                    dve.wait_ge(arg, step)
                    dve.tensor_scalar(turns, turns, -ROUND, None, ALU.add).then_inc(arg, 1)
                    step += 1
                    for part in TWO_PI:
                        dve.wait_ge(arg, step)
                        dve.scalar_tensor_tensor(arg_x, turns, -part, arg_x, ALU.mult, ALU.add).then_inc(arg, 1)
                        step += 1
                    dve.wait_ge(arg, step)
                    dve.tensor_scalar(arg_x, arg_x, PI_BELOW, -PI_BELOW, ALU.min, ALU.max).then_inc(arg, 1)
                    step += 1

            @block.scalar
            def _(act):
                for n in range(3):
                    act.wait_ge(arg, 7 * (n + 1))
                    act.wait_ge(prod, 2 * n + 2)
                    act.activation(h_t[:], arg_x, ACT.Sin).then_inc(done, 1)
                act.wait_ge(done, 3)


def hyena_mix(nc, ps, keep, v_tok, x1_tok, x2_t, y_t, dft, decay, skip, z_t, hf_w, w4):
    with ExitStack() as ctx:
        dft_sb = sbuf(ctx, nc, "dft_sb", [P, 38, P])
        h_t = sbuf(ctx, nc, "h_t", [HD, S])
        v = sbuf(ctx, nc, "v_chunk", [P, NJ, CH])
        x1 = sbuf(ctx, nc, "x1_chunk", [P, NJ, CH])
        x2 = sbuf(ctx, nc, "x2_chunk", [P, 2, S])
        dec = sbuf(ctx, nc, "decay_chunk", [P, NJ, CH])
        w4c = sbuf(ctx, nc, "w4_chunk", [HD, 2, 2, CH])
        skc = sbuf(ctx, nc, "skip_chunk", [1, 2, CH])
        taps = sbuf(ctx, nc, "filter_taps", [P, NJ, 2, CH])
        back = taps[:].rearrange("p j d c -> p (j d) c")
        stage = sbuf(ctx, nc, "stage_one", [P, 2, 2, CH])
        filt = sbuf(ctx, nc, "filter_mid", [P, NM, 2, CH])
        spec = sbuf(ctx, nc, "spectrum", [P, NM, CH])
        spec_x = sbuf(ctx, nc, "spectrum_x", [P, NM, CH])
        mid = sbuf(ctx, nc, "data_mid", [P, NM, CH])
        prod1 = sbuf(ctx, nc, "prod1", [P, 2, CH])
        prod2 = sbuf(ctx, nc, "prod2", [P, 2, CH])
        ybuf = sbuf(ctx, nc, "y_spec", [P, 2, 2, CH])
        filter_mlp(nc, ps, keep, h_t, mid[:].rearrange("p m c -> p (m c)"), z_t, hf_w)

        m1 = lambda j, h: dft_sb[:, 2 * j + h, :]
        m2 = lambda m: dft_sb[:, 16 + (m > 0), :]
        m2c = lambda m: dft_sb[:, 18 + (m > 0), :]
        i1 = lambda m: dft_sb[:, 20 + (m > 0), :]
        i2 = lambda j, h: dft_sb[:, 22 + 2 * j + h, :]

        dft_in, chunk_in, chunk_used, y_ready, y_out = sems(ctx, nc, "dft_in", "chunk_in", "chunk_used", "y_ready", "y_out")
        a_full, a_free, taps_ready, taps_step = sems(ctx, nc, "a_full", "a_free", "taps_ready", "taps_step")
        s_full, s_free, s_kept, s_sent0, s_sent1 = sems(ctx, nc, "s_full", "s_free", "s_kept", "s_sent0", "s_sent1")
        c_full, c_kept, c_multiplied, spec_ready, prod_done, y_done, pair_fixed = sems(
            ctx, nc, "c_full", "c_kept", "c_multiplied", "spec_ready", "prod_done", "y_done", "pair_fixed")
        d_full, mid_ready, back_in, u_ready = sems(ctx, nc, "d_full", "mid_ready", "back_in", "u_ready")
        s_sent = (s_sent0, s_sent1)
        count_from_one(nc, chunk_used, y_out, *s_sent, c_multiplied)
        with nc.Block() as block:
            A_OF, A_CH = (0, 16), 28
            S_Q = 24
            C_Q = 16

            @block.sync
            def _(sync):
                sync.dma_start(dft_sb[:], dft).then_inc(dft_in, 16)
                with sync.Fori(0, CHUNKS) as c:
                    wait_alone(sync, keep["passed"], chunk_used, 1 + c)
                    wait_alone(sync, keep["passed"], y_out, 1 + c * 16)
                    sync.dma_start(w4c[:], w4.rearrange("k (o d c) -> k o d c", o=2, d=2)[:, :, :, ds(c * CH, CH)]).then_inc(chunk_in, 16)
                    sync.dma_start(dec[:], decay[:, :, ds(c * CH, CH)]).then_inc(chunk_in, 16)
                    sync.dma_start(skc[:], skip[:, :, ds(c * CH, CH)]).then_inc(chunk_in, 16)
                    sync.dma_start(v[:], v_tok.rearrange("j q c -> q j c")[:, :, ds(c * CH, CH)]).then_inc(chunk_in, 16)
                    sync.dma_start(x1[:], x1_tok.rearrange("j q c -> q j c")[:, :, ds(c * CH, CH)]).then_inc(chunk_in, 16)
                    sync.dma_start(x2[:], x2_t.rearrange("(t q) n -> q t n", q=P)[:, ds(c * 2, 2), :]).then_inc(chunk_in, 16)
                    for o in range(2):
                        for n in range(16):
                            j, h = n // 2, n % 2
                            sync.wait_ge(s_kept, c * (2 * S_Q) + (o * S_Q + n + 1))
                            sync.dma_start(filt[16 * j:16 * j + 16, 8 * h:8 * h + 8].rearrange("q m d c -> q m (d c)"),
                                           stage[:, n % 2].rearrange("p d c -> p (d c)")).then_inc(s_sent[n % 2], 16)
                        for j in range(NJ):
                            n = 16 + j
                            sync.wait_ge(s_kept, c * (2 * S_Q) + (o * S_Q + n + 1))
                            for h in range(2):
                                sync.dma_start(mid[16 * j:16 * j + 16, 8 * h:8 * h + 8, :], stage[:, n % 2, h, :]).then_inc(s_sent[n % 2], 16)
                        for h in range(2):
                            sync.wait_ge(mid_ready, c * 16 + (8 * o + 4 * h + 4))
                            for j in range(NJ):
                                sync.dma_start(back[:, 2 * j + h, :], mid[16 * j:16 * j + 16, 8 * h:8 * h + 8, :]).then_inc(back_in, 16)
                    sync.wait_ge(y_ready, c * 4 + 4)
                    sync.dma_start(y_t.rearrange("(t q) n -> q t n", q=P)[:, ds(c * 2, 2), :], x2[:]).then_inc(y_out, 16)
                sync.wait_ge(y_out, 1 + 16 * CHUNKS)

            SENT_Q = 16 * 16

            @block.tensor
            def _(pe):
                pe.wait_ge(dft_in, 16)
                with pe.Fori(0, CHUNKS) as c:
                    pe.wait_ge(chunk_in, c * 96 + 96)
                    for o in range(2):
                        a0, s0, c0 = A_OF[o], o * S_Q, o * C_Q
                        for j in range(NJ):
                            pe.wait_ge(a_free, c * A_CH + (a0 + j + 1))
                            pe.matmul(ps[:, j % 2, :], h_t[:, j * P:(j + 1) * P], w4c[:, o].rearrange("k d c -> k (d c)"),
                                      start=True, stop=True).then_inc(a_full, 1)
                        for n in range(16):
                            j, h = n // 2, n % 2
                            if h == 0:
                                pe.wait_ge(taps_ready, c * 16 + (8 * o + j + 1))
                            pe.wait_ge(s_free, c * (2 * S_Q) + (s0 + n + 1))
                            pe.matmul(ps[:, 2 + n % 2, :], m1(j, h), taps[:, j].rearrange("p d c -> p (d c)"),
                                      start=True, stop=True).then_inc(s_full, 1)
                        for j in range(NJ):
                            n = 16 + j
                            if o == 1:
                                pe.wait_ge(u_ready, c * 8 + (j + 1))
                            pe.wait_ge(s_free, c * (2 * S_Q) + (s0 + n + 1))
                            for h in range(2):
                                last = pe.matmul(ps[:, 2 + n % 2, h * CH:(h + 1) * CH], m1(j, h), v[:, j, :], start=True, stop=True)
                            last.then_inc(s_full, 1)
                        for r in range(2):
                            pe.wait_ge(s_sent[r], 1 + c * (2 * SENT_Q) + (o * SENT_Q + 8 * 16))
                        for g in range(8):
                            if g < 2:
                                pe.wait_ge(c_multiplied, 1 + c * 16 + 8 * o)
                            else:
                                pe.wait_ge(c_kept, c * 16 + (8 * o + g - 1))
                            for e in range(2):
                                m = 2 * g + e
                                out = ps[:, 4 + g % 2, e * CH:(e + 1) * CH]
                                pe.matmul(out, m2(m), filt[:, m, 0, :], start=True, stop=False)
                                last = pe.matmul(out, m2c(m), filt[:, m, 1, :], start=False, stop=True)
                            last.then_inc(c_full, 1)
                        for r in range(2):
                            pe.wait_ge(s_sent[r], 1 + c * (2 * SENT_Q) + ((o + 1) * SENT_Q))
                        for g in range(9):
                            if g < 8:
                                if g < 2:
                                    pe.wait_ge(c_kept, c * 16 + (8 * o + 8))
                                else:
                                    pe.wait_ge(c_multiplied, 1 + c * 16 + (8 * o + g - 1))
                                for e in range(2):
                                    m = 2 * g + e
                                    last = pe.matmul(ps[:, 4 + g % 2, e * CH:(e + 1) * CH], m2(m), mid[:, m, :], start=True, stop=True)
                                last.then_inc(c_full, 1)
                            if g > 0:
                                k = g - 1
                                pe.wait_ge(y_done, c * 32 + (16 * o + 2 * k + 2))
                                if k >= 2:
                                    pe.wait_ge(mid_ready, c * 16 + (8 * o + k - 1))
                                for e in range(2):
                                    m = 2 * k + e
                                    last = pe.matmul(ps[:, 6 + k % 2, e * CH:(e + 1) * CH], i1(m), ybuf[:, k % 2, e, :], start=True, stop=True)
                                last.then_inc(d_full, 1)
                        pe.wait_ge(back_in, c * 512 + 256 * (o + 1))
                        if o == 0:
                            for j in range(NJ):
                                pe.wait_ge(a_free, c * A_CH + (8 + j + 1))
                                for h in range(2):
                                    last = pe.matmul(ps[:, j % 2, 0:CH], i2(j, h), back[:, 2 * j + h, :], start=(h == 0), stop=(h == 1))
                                last.then_inc(a_full, 1)
                        else:
                            for n in range(4):
                                t, jj = n // 2, n % 2
                                pe.wait_ge(a_free, c * A_CH + (24 + n + 1))
                                for j in range(4 * jj, 4 * jj + 4):
                                    for h in range(2):
                                        last = pe.matmul(ps[:, n % 2, (j % 4) * P:(j % 4 + 1) * P], back[:, 2 * j + h, t * P:(t + 1) * P],
                                                         i2(j, h), start=(h == 0), stop=(h == 1))
                                last.then_inc(a_full, 1)

            @block.scalar
            def _(act):
                act.sem_inc(s_free, 2)
                with act.Fori(0, CHUNKS) as c:
                    for o in range(2):
                        s0, c0 = o * S_Q, o * C_Q
                        for n in range(S_Q):
                            act.wait_ge(s_full, c * (2 * S_Q) + (s0 + n + 1))
                            before = n // 2 * 16 if n < 16 else 128 + (n - 16) // 2 * 32
                            act.wait_ge(s_sent[n % 2], 1 + c * (2 * SENT_Q) + (o * SENT_Q + before))
                            act.activation(stage[:, n % 2].rearrange("p d c -> p (d c)"), ps[:, 2 + n % 2, :], ACT.Copy).then_inc(s_kept, 1)
                            act.wait_ge(s_kept, c * (2 * S_Q) + (s0 + n + 1))
                            act.sem_inc(s_free, 1)
                        for g in range(8):
                            act.wait_ge(c_full, c * (2 * C_Q) + (c0 + g + 1))
                            bank = ps[:, 4 + g % 2, :]
                            act.activation(spec[:, 2 * g:2 * g + 2].rearrange("p m c -> p (m c)"), bank, ACT.Copy).then_inc(spec_ready, 1)
                            sx = spec_x[:, 2 * g:2 * g + 2].rearrange("p m c -> p (m c)")
                            act.activation(sx[0:64], bank[64:128], ACT.Copy).then_inc(spec_ready, 1)
                            act.activation(sx[64:128], bank[0:64], ACT.Copy).then_inc(spec_ready, 1)
                            if g == 0:
                                act.wait_ge(spec_ready, c * 50 + (25 * o + 3))
                                act.activation(spec_x[64:65, 0, :], bank[64:65, 0:CH], ACT.Copy).then_inc(spec_ready, 1)
                            act.wait_ge(spec_ready, c * 50 + (25 * o + 3 * g + 4))
                            act.sem_inc(c_kept, 1)
                        for k in range(8):
                            act.wait_ge(d_full, c * 16 + (8 * o + k + 1))
                            act.activation(mid[:, 2 * k:2 * k + 2].rearrange("p m c -> p (m c)"), ps[:, 6 + k % 2, :], ACT.Copy).then_inc(mid_ready, 1)

            @block.vector
            def _(dve):
                dve.sem_inc(a_free, 2)
                with dve.Fori(0, CHUNKS) as c:
                    dve.wait_ge(chunk_in, c * 96 + 96)
                    for o in range(2):
                        for j in range(NJ):
                            dve.wait_ge(a_full, c * A_CH + (A_OF[o] + j + 1))
                            dve.tensor_tensor(taps[:, j], ps[:, j % 2, :].rearrange("p (d c) -> p d c", d=2),
                                              dec[:, j, :].unsqueeze(1).to_broadcast([P, 2, CH]), ALU.mult).then_inc(taps_step, 1)
                            dve.wait_ge(taps_step, c * 20 + (10 * o + j + (3 if j else 1)))
                            dve.sem_inc(a_free, 1)
                            if j == 0:
                                dve.memset(taps[0:1, 0, 1, :], 0.0).then_inc(taps_step, 1)
                                dve.tensor_tensor(taps[0:1, 0, 0, :], taps[0:1, 0, 0, :], skc[0:1, o, :], ALU.add).then_inc(taps_step, 1)
                                dve.wait_ge(taps_step, c * 20 + (10 * o + 3))
                            dve.sem_inc(taps_ready, 1)
                        for g in range(8):
                            dve.wait_ge(c_full, c * (2 * C_Q) + (o * C_Q + 8 + g + 1))
                            if g == 0:
                                dve.wait_ge(spec_ready, c * 50 + 25 * (o + 1))
                                dve.memset(spec[64:65, 0, :], 0.0).then_inc(pair_fixed, 1)
                                dve.memset(spec_x[0:1, 0, :], 0.0).then_inc(pair_fixed, 1)
                                dve.wait_ge(pair_fixed, c * 4 + (2 * o + 2))
                            bank = ps[:, 4 + g % 2, :].rearrange("p (m c) -> p m c", m=2)
                            dve.tensor_tensor(prod1[:], bank, spec[:, 2 * g:2 * g + 2, :], ALU.mult).then_inc(prod_done, 1)
                            dve.tensor_tensor(prod2[:], bank, spec_x[:, 2 * g:2 * g + 2, :], ALU.mult).then_inc(prod_done, 1)
                            dve.wait_ge(prod_done, c * 32 + (16 * o + 2 * g + 2))
                            dve.sem_inc(c_multiplied, 1)
                            if g >= 2:
                                dve.wait_ge(d_full, c * 16 + (8 * o + g - 1))
                            dve.tensor_tensor(ybuf[0:64, g % 2], prod1[0:64], prod1[64:128], ALU.subtract).then_inc(y_done, 1)
                            dve.wait_ge(y_done, c * 32 + (16 * o + 2 * g + 1))
                            dve.tensor_tensor(ybuf[64:128, g % 2], prod2[0:64], prod2[64:128], ALU.add).then_inc(y_done, 1)
                            dve.wait_ge(y_done, c * 32 + (16 * o + 2 * g + 2))
                        if o == 0:
                            for j in range(NJ):
                                dve.wait_ge(a_full, c * A_CH + (8 + j + 1))
                                dve.tensor_tensor(v[:, j, :], ps[:, j % 2, 0:CH], x1[:, j, :], ALU.mult).then_inc(u_ready, 1)
                                dve.wait_ge(u_ready, c * 8 + (j + 1))
                                dve.sem_inc(a_free, 1)
                        else:
                            for n in range(4):
                                t, jj = n // 2, n % 2
                                dve.wait_ge(a_full, c * A_CH + (24 + n + 1))
                                out = x2[:, t, :].rearrange("p (s j) -> p j s", j=8)[:, 4 * jj:4 * jj + 4, :]
                                dve.tensor_tensor(out, ps[:, n % 2, :].rearrange("p (j s) -> p j s", j=4), out, ALU.mult).then_inc(y_ready, 1)
                                dve.wait_ge(y_ready, c * 4 + (n + 1))
                                dve.sem_inc(a_free, 1)
                            dve.sem_inc(chunk_used, 1)


NV = 29


def score_tiles():
    tiles = []
    for t in range(8):
        k0, k1 = max(0, P * t - 64), min(S, P * t + 192)
        blocks = [(0, 64, 0), (64, 128, 1)] if t == 0 else [(0, 128, t), (128, 128 if t < 7 else 64, t + 1)]
        tiles.append(dict(g=0, q=(P * t, 1, P), k=(k0, 1, k1 - k0), w=k1 - k0, tab=64 if t == 0 else 0, blocks=blocks))
    for r in range(4):
        for t in range(2):
            blocks = [(0, 64, 9 + 3 * r), (64, 128, 10 + 3 * r)] if t == 0 else [(0, 128, 10 + 3 * r), (128, 64, 11 + 3 * r)]
            tiles.append(dict(g=1, q=(r + 512 * t, 4, P), k=(r + 256 * t, 4, 192), w=192,
                              tab=256 + (64 if t == 0 else 0), blocks=blocks))
    for r in range(8):
        tiles.append(dict(g=2, q=(r, 8, P), k=(r, 8, P), w=P, tab=512, blocks=[(0, P, 21 + r)]))
    off = 0
    for x in tiles:
        x["off"] = off
        off += x["w"]
    return tiles, off


def value_tiles():
    out = [(0, (0, 1, 64))] + [(0, (64 + P * n, 1, P)) for n in range(7)] + [(0, (960, 1, 64))]
    for r in range(4):
        out += [(1, (r, 4, 64)), (1, (r + 256, 4, P)), (1, (r + 768, 4, 64))]
    out += [(2, (r, 8, P)) for r in range(8)]
    return out


def tokens(ap, where):
    first, step, count = where
    return ap[:, first:first + step * (count - 1) + 1:step]


def attention(nc, ps, keep, w_in, alibi):
    xn_t, sq, cols_in, cols_p, att = keep["xn_t"], keep["squares"], keep["cols_in"], keep["cols_p"], keep["att_t"]
    ident, pair_ones = sq[:, 0, :], sq[:, 1, :]
    tiles, width = score_tiles()
    vts = value_tiles()
    NT = len(tiles)
    blocks = [(x, b) for x in tiles for b in x["blocks"]]
    NBLK = len(blocks)
    QUADS = NBLK // 4
    v_batches = [list(range(a, min(a + 4, b))) for a0, b in ((0, 9), (9, 21), (21, 29)) for a in range(a0, b, 4)]
    NVB = len(v_batches)
    w_cols = w_view(w_in, KT)
    with ExitStack() as ctx:
        w = sbuf(ctx, nc, "w_at", [P, 5, KT, P])
        qk = sbuf(ctx, nc, "qk", [P, 6, S])
        sqr = sbuf(ctx, nc, "qk_squares", [P, 4, HALF])
        rs = sbuf(ctx, nc, "qk_root", [P, 2, HALF])
        vt = sbuf(ctx, nc, "v_t", [P, S])
        vx = sbuf(ctx, nc, "v_tok_one", [P, NV, 2, HD + 1])
        gate = sbuf(ctx, nc, "at_gate", [P, S])
        table = sbuf(ctx, nc, "alibi_pair", [P, 2, 640])
        sc = sbuf(ctx, nc, "scores", [P, 2, width])
        mx = sbuf(ctx, nc, "tile_max", [P, 2, NT])
        mrow = sbuf(ctx, nc, "max_row", [1, S])
        nmx = sbuf(ctx, nc, "minus_max", [P, 2, NT])
        pts = sbuf(ctx, nc, "probs_t", [P, 2, 4, P])
        o_s = sbuf(ctx, nc, "out_t", [P, S])
        rden = sbuf(ctx, nc, "rden", [HD + 1, S])
        normed = sbuf(ctx, nc, "out_normed", [P, S])
        small = sbuf(ctx, nc, "small", [P, 66])
        w_ready = sems(ctx, nc, *[f"aw_ready{s}" for s in range(5)])
        consts, table_in, p_full, p_free, evac, v_read, sq_ready, n_full, n_root, n_recip, qk_ready, head_done = sems(
            ctx, nc, "consts", "at_table_in", "at_p_full", "at_p_free", "at_evac", "at_v_read", "at_sq_ready", "at_n_full", "at_n_root",
            "at_n_recip", "at_qk_ready", "at_head_done")
        sc_full, sc_ready, row_full, row_kept, row_ready, neg_full, neg_ready, exp_done = sems(
            ctx, nc, "sc_full", "sc_ready", "row_full", "row_kept", "row_ready", "neg_full", "neg_ready", "exp_done")
        vx_full, vx_ready, pt_full, pt_ready, pv_done, o_kept, rd_ready, bc_full, o_norm, o_done = sems(
            ctx, nc, "vx_full", "vx_ready", "pt_full", "pt_ready", "pv_done", "o_kept", "rd_ready", "bc_full", "o_norm", "o_done")
        count_from_one(nc, n_root, row_kept, vx_ready, pt_ready, o_kept, rd_ready, o_norm, head_done, n_full, vx_full, o_done,
                       n_recip, bc_full)

        TILES10 = [(0, 0), (1, 0), (0, 1), (1, 1), (0, 2), (1, 2), (2, 0), (2, 1), (2, 2), None]

        def first_col(n):
            return COL_GATE_AT if TILES10[n] is None else COL_QKV + TILES10[n][0] * 1536 + TILES10[n][1] * 512

        with nc.Block() as block:
            @block.sync
            def _(sync):
                for n in range(5):
                    sync.dma_start(w[:, n], w_cols[:, :, first_col(n):first_col(n) + P]).then_inc(w_ready[n], 16)
                sync.dma_start(table[:], alibi[0]).then_inc(table_in, 16)
                with sync.Fori(0, PAIRS - 1) as i:
                    for n in range(5, 15):
                        sync.wait_ge(p_full, i * 20 + 2 * (n - 5) + 2)
                        col = ds(i * P + (first_col(n % 10) + (P if n >= 10 else 0)), P)
                        sync.dma_start(w[:, n % 5], w_cols[:, :, col]).then_inc(w_ready[n % 5], 16)
                    sync.wait_ge(sc_ready, i * (2 * NT) + 2 * NT)
                    sync.dma_start(table[:], alibi[ds(i + 1, 1)].rearrange("a p h n -> p (a h) n")).then_inc(table_in, 16)
                for n in range(5, 10):
                    sync.wait_ge(p_full, 20 * (PAIRS - 1) + 2 * (n - 5) + 2)
                    col = (PAIRS - 1) * P + first_col(n)
                    sync.dma_start(w[:, n % 5], w_cols[:, :, col:col + P]).then_inc(w_ready[n % 5], 16)

            @block.gpsimd
            def _(pool):
                pool.memset(small[:, 0:1], EPS).then_inc(consts, 1)
                pool.memset(small[:, 1:65], 1.0).then_inc(consts, 1)
                pool.memset(small[:, 65:66], -1.0).then_inc(consts, 1)
                pool.memset(vx[:, :, :, HD:HD + 1], 1.0).then_inc(consts, 1)

            @block.tensor
            def _(pe):
                pe.wait_ge(consts, 5)
                with pe.Fori(0, PAIRS) as i:
                    def project(n):
                        pe.wait_ge(w_ready[n % 5], i * 32 + (16 if n < 5 else 32))
                        for h in range(2):
                            pe.wait_ge(p_free, i * 20 + 2 * n + h + 1)
                            for k in range(KT):
                                last = pe.matmul(ps[:, h, :], w[:, n % 5, k, :], xn_t[:, k, h * HALF:(h + 1) * HALF],
                                                 start=(k == 0), stop=(k == KT - 1))
                            last.then_inc(p_full, 1)

                    def norm(n):
                        for h in range(2):
                            pe.wait_ge(sq_ready, i * 12 + 2 * n + h + 1)
                            pe.wait_ge(n_root, 1 + i * 12 + 2 * n + h)
                            pe.matmul(ps[:, 2, :], pair_ones, sqr[:, (2 * n + h) % 4, :], start=True, stop=True).then_inc(n_full, 1)

                    def score(e):
                        pe.wait_ge(qk_ready, i * 12 + 12)
                        rows = slice(64 * e, 64 * e + 64)
                        for n, x in enumerate(tiles):
                            done = i * (2 * NT) + (NT * e + n - 1)
                            if n >= 2:
                                pe.wait_ge(sc_ready, done)
                            pe.matmul(ps[:, 4 + n % 2, 0:x["w"]], tokens(qk[rows, 2 * x["g"]], x["q"]),
                                      tokens(qk[rows, 2 * x["g"] + 1], x["k"]), start=True, stop=True).then_inc(sc_full, 1)

                    def max_rows(e):
                        pe.wait_ge(sc_ready, i * (2 * NT) + (NT * e + NT))
                        for g in range(GROUPS):
                            pe.wait_ge(row_kept, 1 + i * 6 + (3 * e + g))
                            for n, x in enumerate(tiles):
                                if x["g"] != g:
                                    continue
                                col = mx[:, e, n:n + 1]
                                if g == 0:
                                    last = pe.matmul(ps[0:1, 4 + n // 4, (n % 4) * P:(n % 4 + 1) * P], col, ident, start=True, stop=True)
                                elif g == 1:
                                    r, t = (n - 8) // 2, n % 2
                                    last = pe.matmul(ps[0:1, 4 + t, r:r + 4 * (P - 1) + 1:4], col, ident, start=True, stop=True)
                                else:
                                    r = n - 16
                                    for t in range(2):
                                        last = pe.matmul(tokens(ps[0:1, 4 + t, :], (r, 8, 64)), col, ident[:, 64 * t:64 * t + 64],
                                                         start=True, stop=True)
                            last.then_inc(row_full, 1)

                    def max_cols(e):
                        pe.wait_ge(row_ready, i * 2 + (e + 1))
                        for n, x in enumerate(tiles):
                            last = pe.matmul(ps[:, 2, n:n + 1], tokens(mrow[:], x["q"]), small[0:1, 65:66], start=True, stop=True)
                        last.then_inc(neg_full, 1)

                    def values(g):
                        pe.wait_ge(evac, i * 20 + (12 + 2 * g + 2))
                        for n, batch in enumerate(v_batches):
                            if vts[batch[0]][0] != g:
                                continue
                            wait_alone(pe, keep["passed"], vx_ready, 1 + i * NVB + n)
                            for b, tile in enumerate(batch):
                                where = vts[tile][1]
                                keys = where[2]
                                last = pe.transpose(ps[0:keys, 2, b * P:(b + 1) * P], tokens(vt[:], where), ident)
                            last.then_inc(vx_full, 1)

                    def weigh(e):
                        def turn(qd):
                            x = blocks[4 * qd + 3][0]
                            wait_alone(pe, keep["passed"], exp_done, i * (2 * NT) + (NT * e + tiles.index(x) + 1))
                            wait_alone(pe, keep["passed"], pt_ready, 1 + i * (2 * QUADS) + (QUADS * e + qd))
                            for b in range(4):
                                x, (c, keys, _) = blocks[4 * qd + b]
                                last = pe.transpose(ps[0:keys, 3, b * P:(b + 1) * P], sc[:, e, x["off"] + c:x["off"] + c + keys], ident)
                            last.then_inc(pt_full, 1)

                        def product(qd):
                            pe.wait_ge(pt_ready, 1 + i * (2 * QUADS) + (QUADS * e + qd + 1))
                            for b in range(4):
                                x, (c, keys, tile) = blocks[4 * qd + b]
                                probs = pts[0:keys, qd % 2, b, :]
                                val = vx[0:keys, tile, e, :]
                                first, step, _ = x["q"]
                                if x["g"] < 2:
                                    lo = first % HALF
                                    last = pe.matmul(ps[0:HD + 1, 6 + first // HALF, lo:lo + step * (P - 1) + 1:step], val, probs,
                                                     start=(x["g"] == 0 and first % HALF == 0 and c == 0), stop=False, skip_group_check=True)
                                else:
                                    for t in range(2):
                                        last = pe.matmul(tokens(ps[0:HD + 1, 6 + t, :], (first, 8, 64)), val, probs[:, 64 * t:64 * t + 64],
                                                         start=False, stop=(qd == QUADS - 1 and b == 3), skip_group_check=True)
                            last.then_inc(pv_done, 1)

                        wait_alone(pe, keep["passed"], o_kept, 1 + i * 2 + e)
                        pe.wait_ge(rd_ready, 1 + i * 2 + e)
                        wait_alone(pe, keep["passed"], vx_ready, 1 + i * NVB + NVB)
                        turn(0)
                        for qd in range(QUADS):
                            product(qd) if qd == 0 else None
                            if qd + 1 < QUADS:
                                turn(qd + 1)
                            if qd:
                                product(qd)

                    def denominators(e):
                        pe.wait_ge(rd_ready, 1 + i * 2 + (e + 1))
                        for h in range(2):
                            pe.wait_ge(o_norm, 1 + i * 4 + (2 * e + h))
                            pe.matmul(ps[0:HD, 2, :], small[64:65, 1:65], rden[64:65, h * HALF:(h + 1) * HALF],
                                      start=True, stop=True).then_inc(bc_full, 1)

                    pe.wait_ge(head_done, 1 + i * 2)
                    project(0)
                    for n in range(1, 6):
                        project(n)
                        norm(n - 1)
                    project(6)
                    norm(5)
                    score(0)
                    max_rows(0)
                    max_cols(0)
                    score(1)
                    max_rows(1)
                    pe.wait_ge(neg_ready, i * 2 + 1)
                    values(0)
                    project(7)
                    values(1)
                    project(8)
                    values(2)
                    project(9)
                    wait_alone(pe, keep["passed"], vx_ready, 1 + i * NVB + NVB)
                    max_cols(1)
                    weigh(0)
                    pe.wait_ge(neg_ready, i * 2 + 2)
                    denominators(0)
                    weigh(1)
                    denominators(1)

            @block.scalar
            def _(act):
                act.sem_inc(p_free, 2)
                with act.Fori(0, PAIRS) as i:
                    def evacuate(n):
                        kind = TILES10[n]
                        for h in range(2):
                            wait_alone(act, keep["passed"], p_full, i * 20 + 2 * n + h + 1)
                            half = slice(h * HALF, (h + 1) * HALF)
                            bias = cols_in[:, ds(i + first_col(n) // P, 1)]
                            if n < 6:
                                act.activation(qk[:, n, half], ps[:, h, :], ACT.Identity, bias=bias).then_inc(evac, 1)
                                wait_alone(act, keep["passed"], n_full, 1 + i * 12 + max(0, 2 * n + h - 3))
                                act.activation(sqr[:, (2 * n + h) % 4, :], ps[:, h, :], ACT.Square, bias=bias).then_inc(sq_ready, 1)
                                act.wait_ge(sq_ready, i * 12 + 2 * n + h + 1)
                            elif kind is not None:
                                if n == 6:
                                    wait_alone(act, keep["passed"], vx_full, 1 + i * NVB)
                                else:
                                    wait_alone(act, keep["passed"], vx_full, 1 + i * NVB + (3 if n == 7 else 6))
                                act.activation(vt[:, half], ps[:, h, :], ACT.Identity, bias=bias).then_inc(evac, 1)
                            else:
                                wait_alone(act, keep["passed"], o_done, 1 + i * 4)
                                act.activation(gate[:, half], ps[:, h, :], ACT.Silu, bias=bias).then_inc(evac, 1)
                            act.wait_ge(evac, i * 20 + 2 * n + h + 1)
                            act.sem_inc(p_free, 1)

                    def roots(n):
                        for h in range(2):
                            act.wait_ge(n_full, 1 + i * 12 + 2 * n + h + 1)
                            act.wait_ge(n_recip, 1 + i * 24 + 2 * max(0, 2 * n + h - 1))
                            act.activation(rs[:, h, :], ps[:, 2, :], ACT.Sqrt, bias=small[:, 0:1], scale=1.0 / HD).then_inc(n_root, 1)

                    def exps(e):
                        act.wait_ge(neg_ready, i * 2 + (e + 1))
                        for n, x in enumerate(tiles):
                            s = sc[:, e, x["off"]:x["off"] + x["w"]]
                            act.activation(s, s, ACT.Exp, bias=nmx[:, e, n:n + 1]).then_inc(exp_done, 1)

                    def keep_out(e):
                        act.wait_ge(pv_done, i * (2 * QUADS) + QUADS * (e + 1))
                        act.wait_ge(o_norm, 1 + i * 4 + 2 * e)
                        act.activation(o_s[0:HD, :], ps[0:HD, 6:8, :].rearrange("p a n -> p (a n)"), ACT.Copy).then_inc(o_kept, 1)

                    act.wait_ge(consts, 5)
                    for n in range(6):
                        evacuate(n)
                        if n:
                            roots(n - 1)
                    evacuate(6)
                    roots(5)
                    exps(0)
                    evacuate(7)
                    evacuate(8)
                    evacuate(9)
                    exps(1)
                    keep_out(0)
                    keep_out(1)

            @block.vector
            def _(dve):
                dve.memset(ps[:, 3, :], 0.0).then_inc(consts, 1)
                with dve.Fori(0, PAIRS) as i:
                    def unit(n):
                        gain = cols_p[:, (ROW_QG, ROW_KG)[n % 2]:(ROW_QG, ROW_KG)[n % 2] + 1]
                        for h in range(2):
                            m = 2 * n + h
                            dve.wait_ge(n_root, 1 + i * 12 + m + 1)
                            dve.reciprocal(rs[:, h, :], rs[:, h, :]).then_inc(n_recip, 1)
                            dve.wait_ge(n_recip, 1 + i * 24 + 2 * m + 1)
                            x = qk[:, n, h * HALF:(h + 1) * HALF]
                            dve.scalar_tensor_tensor(x, x, gain, rs[:, h, :], ALU.mult, ALU.mult).then_inc(n_recip, 1)
                            dve.wait_ge(n_recip, 1 + i * 24 + 2 * m + 2)
                            dve.sem_inc(qk_ready, 1)

                    def add_bias(e):
                        for n, x in enumerate(tiles):
                            wait_alone(dve, keep["passed"], sc_full, i * (2 * NT) + (NT * e + n + 1))
                            dve.tensor_tensor_reduce(sc[:, e, x["off"]:x["off"] + x["w"]], ps[:, 4 + n % 2, 0:x["w"]],
                                                     table[:, e, x["tab"]:x["tab"] + x["w"]], 0.125, -3e38, ALU.add, ALU.max,
                                                     mx[:, e, n:n + 1]).then_inc(sc_ready, 1)

                    def join_max(e):
                        for g in range(GROUPS):
                            src = ps[0:1, 4:6, :].rearrange("p a n -> p (a n)")
                            dve.wait_ge(row_full, i * 6 + (3 * e + g + 1))
                            if g == 0:
                                dve.tensor_copy(mrow[:], src).then_inc(row_kept, 1)
                            else:
                                dve.tensor_tensor(mrow[:], src, mrow[:], ALU.max).then_inc(row_kept, 1)
                            dve.wait_ge(row_kept, 1 + i * 6 + (3 * e + g + 1))
                        dve.sem_inc(row_ready, 1)

                    def keep_neg(e):
                        dve.wait_ge(neg_full, i * 2 + (e + 1))
                        dve.tensor_copy(nmx[:, e, :], ps[:, 2, 0:NT]).then_inc(neg_ready, 1)

                    def keep_values(g):
                        for n, batch in enumerate(v_batches):
                            if vts[batch[0]][0] != g:
                                continue
                            dve.wait_ge(vx_full, 1 + i * NVB + n + 1)
                            dve.tensor_copy(vx[:, batch[0]:batch[-1] + 1, :, 0:HD],
                                            ps[:, 2, 0:P * len(batch)].rearrange("p (b e d) -> p b e d", e=2, d=HD)).then_inc(vx_ready, 1)

                    def keep_probs(e):
                        for qd in range(QUADS):
                            dve.wait_ge(pt_full, i * (2 * QUADS) + (QUADS * e + qd + 1))
                            if qd >= 2:
                                dve.wait_ge(pv_done, i * (2 * QUADS) + (QUADS * e + qd - 1))
                            dve.tensor_copy(pts[:, qd % 2].rearrange("p b n -> p (b n)"), ps[:, 3, :]).then_inc(pt_ready, 1)

                    def finish(e):
                        dve.wait_ge(pv_done, i * (2 * QUADS) + QUADS * (e + 1))
                        dve.wait_ge(bc_full, 1 + i * 4 + 2 * e)
                        dve.reciprocal(rden[64:65, :], ps[64:65, 6:8, :].rearrange("p a n -> p (a n)")).then_inc(rd_ready, 1)
                        dve.wait_ge(o_kept, 1 + i * 2 + (e + 1))
                        rows = slice(64 * e, 64 * e + 64)
                        for h in range(2):
                            half = slice(h * HALF, (h + 1) * HALF)
                            dve.wait_ge(bc_full, 1 + i * 4 + (2 * e + h + 1))
                            dve.tensor_tensor(normed[rows, half], o_s[0:HD, half], ps[0:HD, 2, :], ALU.mult).then_inc(o_norm, 1)
                            dve.wait_ge(o_norm, 1 + i * 4 + (2 * e + h + 1))
                            dve.wait_ge(evac, i * 20 + 20)
                            dve.tensor_tensor(att[rows, ds(i, 1), half], normed[rows, half].unsqueeze(1), gate[rows, half].unsqueeze(1),
                                              ALU.mult).then_inc(o_done, 1)
                        dve.wait_ge(o_done, 1 + i * 4 + 2 * (e + 1))
                        dve.sem_inc(head_done, 1)

                    for n in range(6):
                        unit(n)
                    dve.wait_ge(table_in, i * 16 + 16)
                    add_bias(0)
                    join_max(0)
                    keep_neg(0)
                    add_bias(1)
                    join_max(1)
                    for g in range(GROUPS):
                        keep_values(g)
                    keep_neg(1)
                    keep_probs(0)
                    finish(0)
                    keep_probs(1)
                    finish(1)


def merge(nc, ps, keep, w_in, w_hy, w_at, w_out, y_t, x, out):
    xn_t, cols_in, att = keep["xn_t"], keep["cols_in"], keep["att_t"]
    w_cols, hy_cols, at_cols, out_rows = w_view(w_in, KT), w_view(w_hy, HYT), w_view(w_at, PAIRS), w_view(w_out, KT)
    DT = D // P
    with ExitStack() as ctx:
        y = sbuf(ctx, nc, "y_gated", [P, HYT, S])
        merged = sbuf(ctx, nc, "merged", [P, DT, S])
        wg = sbuf(ctx, nc, "w_gates", [P, 2, 2, KT, P])
        wu = sbuf(ctx, nc, "w_up", [P, 2, HYT + PAIRS, P])
        wo = sbuf(ctx, nc, "w_out_sb", [P, KT, D])
        sig = sbuf(ctx, nc, "sigmoids", [P, 2, 2, HALF])
        part = sbuf(ctx, nc, "parts", [P, 2, HALF])
        xr = sbuf(ctx, nc, "x_again", [P, 2, D])
        w_ready = sems(ctx, nc, "mw_ready0", "mw_ready1")
        x_in = sems(ctx, nc, "xr_in0", "xr_in1")
        stored = sems(ctx, nc, "stored0", "stored1")
        y_in, wo_in, full, free, sig_ready, part_ready, merged_ready, o_full, o_ready = sems(
            ctx, nc, "m_y_in", "wo_in", "m_full", "m_free", "sig_ready", "part_ready", "merged_ready", "o_full", "o_ready")
        count_from_one(nc, part_ready)
        with nc.Block() as block:
            def load(eng, r, c_gate, c_up):
                for g in range(2):
                    eng.dma_start(wg[:, r, g], w_cols[:, :, c_gate(g)]).then_inc(w_ready[r], 16)
                eng.dma_start(wu[:, r, 0:HYT], hy_cols[:, :, c_up]).then_inc(w_ready[r], 16)
                eng.dma_start(wu[:, r, HYT:HYT + PAIRS], at_cols[:, :, c_up]).then_inc(w_ready[r], 16)

            @block.sync
            def _(sync):
                for r in range(2):
                    load(sync, r, lambda g: slice(COL_MIX + g * D + r * P, COL_MIX + g * D + r * P + P), slice(r * P, r * P + P))
                sync.dma_start(y[:], y_t.rearrange("(t q) n -> q t n", q=P)).then_inc(y_in, 16)
                with sync.Fori(1, DT // 2) as i:
                    for r in range(2):
                        sync.wait_ge(full, i * 4 + (2 * r - 2))
                        load(sync, r, lambda g: ds(i * (2 * P) + (COL_MIX + g * D + r * P), P), ds(i * (2 * P) + r * P, P))
                sync.dma_start(wo[:], out_rows).then_inc(wo_in, 16)
                for t in range(2):
                    sync.dma_start(xr[:, t, :], x[t * P:(t + 1) * P, :]).then_inc(x_in[t], 16)
                for t in range(KT):
                    sync.wait_ge(o_ready, 2 * t + 2)
                    sync.dma_start(out[t * P:(t + 1) * P, :], xr[:, t % 2, :]).then_inc(stored[t % 2], 16)
                    if t + 2 < KT:
                        sync.wait_ge(stored[t % 2], 16 * (t // 2 + 1))
                        sync.dma_start(xr[:, t % 2, :], x[(t + 2) * P:(t + 3) * P, :]).then_inc(x_in[t % 2], 16)
                for r in range(2):
                    sync.wait_ge(stored[r], 16 * (KT // 2))

            @block.tensor
            def _(pe):
                with pe.Fori(0, DT // 2) as i:
                    for r in range(2):
                        pe.wait_ge(w_ready[r], i * 64 + 64)
                        for h in range(2):
                            half = slice(h * HALF, (h + 1) * HALF)
                            pe.wait_ge(free, i * 4 + (2 * r + h + 1))
                            for g in range(2):
                                for k in range(KT):
                                    pe.matmul(ps[:, 4 * h + g, :], wg[:, r, g, k, :], xn_t[:, k, half], start=(k == 0), stop=(k == KT - 1))
                            if r == 0:
                                pe.wait_ge(y_in, 16)
                            for k in range(HYT):
                                pe.matmul(ps[:, 4 * h + 2, :], wu[:, r, k, :], y[:, k, half], start=(k == 0), stop=(k == HYT - 1))
                            for k in range(PAIRS):
                                last = pe.matmul(ps[:, 4 * h + 3, :], wu[:, r, HYT + k, :], att[:, k, half], start=(k == 0), stop=(k == PAIRS - 1))
                            last.then_inc(full, 1)
                pe.wait_ge(merged_ready, 2 * DT)
                pe.wait_ge(wo_in, 16)
                for t in range(KT):
                    for h in range(2):
                        n = 2 * t + h
                        if n >= 2:
                            pe.wait_ge(o_ready, n - 1)
                        for k in range(KT):
                            last = pe.matmul(ps[:, n % 2, :], merged[:, k, t * P:(t + 1) * P], wo[:, k, h * HALF:(h + 1) * HALF],
                                             start=(k == 0), stop=(k == KT - 1))
                        last.then_inc(o_full, 1)

            @block.scalar
            def _(act):
                with act.Fori(0, DT // 2) as i:
                    for r in range(2):
                        for h in range(2):
                            wait_alone(act, keep["passed"], full, i * 4 + (2 * r + h + 1))
                            wait_alone(act, keep["passed"], part_ready, 1 + i * 8 + max(0, 4 * r + 2 * h - 2))
                            for g in range(2):
                                bias = cols_in[:, ds(i * 2 + (COL_MIX // P + g * DT + r), 1)]
                                act.activation(sig[:, h, g, :], ps[:, 4 * h + g, :], ACT.Sigmoid, bias=bias).then_inc(sig_ready, 1)

            @block.vector
            def _(dve):
                dve.sem_inc(free, 2)
                with dve.Fori(0, DT // 2) as i:
                    for r in range(2):
                        for h in range(2):
                            n = 2 * r + h
                            for g in range(2):
                                dve.wait_ge(sig_ready, i * 8 + (2 * n + g + 1))
                                dve.tensor_tensor(part[:, g, :], sig[:, h, g, :], ps[:, 4 * h + 2 + g, :], ALU.mult).then_inc(part_ready, 1)
                            dve.wait_ge(part_ready, 1 + i * 8 + (2 * n + 2))
                            dve.sem_inc(free, 1)
                            dve.tensor_tensor(merged[:, ds(i * 2 + r, 1), h * HALF:(h + 1) * HALF], part[:, 0:1, :], part[:, 1:2, :],
                                              ALU.add).then_inc(merged_ready, 1)
                            dve.wait_ge(merged_ready, i * 4 + (n + 1))
                for t in range(KT):
                    dve.wait_ge(x_in[t % 2], 16 * (t // 2 + 1))
                    for h in range(2):
                        dve.wait_ge(o_full, 2 * t + h + 1)
                        dst = xr[:, t % 2, h * HALF:(h + 1) * HALF]
                        dve.tensor_tensor(dst, ps[:, h, :], dst, ALU.add).then_inc(o_ready, 1)


def program(nc, x, norm_g, w_in, b_in, conv_w, conv_b, hf_w1, hf_b1, hf_w2, hf_b2, hf_w3, hf_b3, hf_w4, hf_freq,
            hy_skip, q_norm_g, k_norm_g, w_hy_out, w_at_out, w_out, dft, z_t, decay, alibi, squares, out):
    v_tok = nc.dram_tensor("v_tok_d", (8, P, HY), F32).ap()
    x1_tok = nc.dram_tensor("x1_tok_d", (8, P, HY), F32).ap()
    x2_t = nc.dram_tensor("x2_t_d", (HY, S), F32).ap()
    y_t = nc.dram_tensor("y_t_d", (HY, S), F32).ap()
    with ExitStack() as ctx:
        ps = ctx.enter_context(nc.psum_tensor("psum", [P, 8, HALF], F32))
        keep = {"xn_t": sbuf(ctx, nc, "xn_t", [P, KT, S]), "squares": sbuf(ctx, nc, "squares_sb", [P, 2, P]),
                "cols_in": sbuf(ctx, nc, "cols_in", [P, P]), "cols_p": sbuf(ctx, nc, "cols_p", [P, P])}
        [keep["passed"]] = sems(ctx, nc, "passed")
        w = w_in[0]
        normalise(nc, ps, keep, x[0], norm_g, b_in, conv_w[0], conv_b, (hf_b1, hf_b2, hf_b3, hf_freq), q_norm_g, k_norm_g, squares)
        hyena_in(nc, ps, keep, w, v_tok, x1_tok, x2_t)
        hyena_mix(nc, ps, keep, v_tok, x1_tok, x2_t, y_t, dft, decay, hy_skip, z_t, (hf_w1[0], hf_w2[0], hf_w3[0]), hf_w4[0])
        keep["att_t"] = sbuf(ctx, nc, "att_t", [P, PAIRS, S])
        attention(nc, ps, keep, w, alibi)
        merge(nc, ps, keep, w, w_hy_out[0], w_at_out[0], w_out[0], y_t, x[0], out[0])


def shape_tables():
    import math
    import numpy as np

    f32 = np.float32
    a = np.arange(16)
    bq = np.arange(8)
    tau = 2.0 * np.pi

    def times(j):
        return (64 * a[:, None] + 8 * bq[None, :] + j).reshape(-1)

    col_b, col_c, col_m = (x.reshape(-1) for x in np.meshgrid(bq, np.arange(2), np.arange(8), indexing="ij"))
    m1 = np.zeros((8, 2, 128, 128))
    i2 = np.zeros((8, 2, 128, 128))
    for j in range(8):
        n = times(j)
        same = (n % 64 // 8)[:, None] == col_b[None, :]
        sign = np.where((n // 64) % 2, -1.0, 1.0)[:, None]
        for h in range(2):
            k1 = 8 * h + col_m[None, :]
            c = col_c[None, :]
            angle = tau * k1 * n[:, None] / 2048.0
            fwd = np.where(k1 > 0, np.where(c == 0, np.cos(angle), -np.sin(angle)), np.where(c == 0, 1.0, sign))
            inv = np.where(k1 > 0, np.where(c == 0, 2 * np.cos(angle), -2 * np.sin(angle)),
                           np.where(c == 0, 1.0, sign)) / 2048.0
            m1[j, h] = fwd * same
            i2[j, h] = (inv * same).T
    jj, bb, c = (x.reshape(-1) for x in np.meshgrid(np.arange(8), bq, np.arange(2), indexing="ij"))
    b = 8 * bb + jj
    k2 = np.arange(64)
    ang = tau * b[:, None] * k2[None, :] / 64.0
    cb = c[:, None]
    m2g = np.concatenate([np.where(cb == 0, np.cos(ang), np.sin(ang)),
                          np.where(cb == 0, -np.sin(ang), np.cos(ang))], 1)
    i1g = np.concatenate([np.where(cb == 0, np.cos(ang), np.sin(ang)),
                          np.where(cb == 0, -np.sin(ang), np.cos(ang))], 1).T
    q = np.arange(32)
    ang0 = tau * b[:, None] * q[None, :] / 64.0
    ang16 = tau * b[:, None] * (16 + 32 * q[None, :]) / 2048.0
    is0, is16 = (c == 0)[:, None], (c == 1)[:, None]
    im0 = -np.sin(ang0) * is0
    im0[:, 0] = np.where(c == 0, np.where(b % 2, -1.0, 1.0), 0.0)
    m2s = np.concatenate([np.cos(ang0) * is0, np.cos(ang16) * is16, im0, -np.sin(ang16) * is16], 1)
    w_re = np.where(q == 0, 1.0, 2.0)[None, :]
    jm0 = -2 * np.sin(ang0) * is0
    jm0[:, 0] = np.where(c == 0, np.where(b % 2, -1.0, 1.0), 0.0)
    i1s = np.concatenate([w_re * np.cos(ang0) * is0, 2 * np.cos(ang16) * is16, jm0, -2 * np.sin(ang16) * is16], 1).T
    conj = np.where(np.arange(128) < 64, 1.0, -1.0)[None, :]
    conj_s = conj.copy()
    conj_s[0, 64] = 1.0
    mats = np.stack([m2s, m2g, m2s * conj_s, m2g * conj, i1s, i1g])
    dft = np.concatenate([m1.reshape(16, 128, 128), mats, i2.reshape(16, 128, 128)])
    dft = np.ascontiguousarray(dft.transpose(1, 0, 2)).astype(f32)

    L, bands = 1024, 16
    order = np.concatenate([times(j) for j in range(8)])
    t = (np.arange(L, dtype=f32) / f32(L - 1)).astype(f32)
    w = (f32(tau) * np.arange(L, dtype=f32) / f32(L)).astype(f32)
    f = np.linspace(1e-4, bands - 1, bands, dtype=f32)
    fw = (f[None, :] * w[:, None]).astype(f32).astype(np.float64)
    z = np.concatenate([t[:, None], np.cos(fw), -np.sin(fw)], 1)
    z_t = np.ascontiguousarray(z[order].T).astype(f32)
    lo, hi = math.log(1e-2) / 1.5, math.log(1e-2) / 0.3
    deltas = np.abs(np.linspace(lo, hi, 768, dtype=f32))
    decay = np.exp(-(t[:, None] * deltas[None, :]).astype(f32).astype(np.float64))
    decay = np.ascontiguousarray(decay[order].reshape(8, 128, 768).transpose(1, 0, 2)).astype(f32)

    slopes = 2.0 ** (-8.0 * np.arange(1, 9) / 8.0)
    qi = np.arange(128)[:, None]
    rel = qi + 64 - np.arange(256)[None, :]
    in_band = np.abs(rel) <= 64
    k = np.arange(128)[None, :]
    rel2 = qi // 2 - k // 2
    same2 = qi % 2 == k % 2
    parts = []
    for s in slopes:
        parts.append(np.concatenate([np.where(in_band, -s * np.abs(rel), -1e30),
                                     np.where(in_band, -s * 4 * np.abs(rel), -1e30),
                                     np.where(same2, -s * 16 * np.abs(rel2), -1e30)], 1))
    alibi = (8.0 * np.stack(parts)).reshape(4, 2, 128, 640).transpose(0, 2, 1, 3)
    alibi = np.ascontiguousarray(alibi).astype(f32)
    eye = np.eye(128, dtype=f32)
    pair = np.kron(np.eye(2), np.ones((64, 64))).astype(f32)
    squares = np.ascontiguousarray(np.stack([eye, pair], 1))
    return {"dft": dft, "z_t": z_t, "decay": decay, "alibi": alibi, "squares": squares}


_INS = ["x", "norm_g", "w_in", "b_in", "conv_w", "conv_b", "hf_w1", "hf_b1", "hf_w2", "hf_b2", "hf_w3", "hf_b3", "hf_w4",
        "hf_freq", "hy_skip", "q_norm_g", "k_norm_g", "w_hy_out", "w_at_out", "w_out"]
_TABLES = ["dft", "z_t", "decay", "alibi", "squares"]


def kernel(**inputs):
    import numpy as _np
    import concourse.bacc as _bacc
    from concourse import mybir as _mybir
    from concourse.bass_utils import run_bass_kernel_spmd as _run

    nc = _bacc.Bacc("TRN2", target_bir_lowering=False, num_devices=1)
    tables = shape_tables()
    arrays, args = {}, {}
    for name in _INS + _TABLES:
        a = _np.ascontiguousarray(inputs[name] if name in inputs else tables[name])
        arrays[f"in_{name}_dram"] = a
        args[name] = nc.dram_tensor(f"in_{name}_dram", a.shape, _mybir.dt.from_np(a.dtype), kind="ExternalInput").ap()
    args["out"] = nc.dram_tensor("out_0_dram", (1, 1024, 1024), _mybir.dt.float32, kind="ExternalOutput").ap()
    program(nc, **args)
    r = _run(nc, [arrays], core_ids=[0])
    return r.results[0]["out_0_dram"]
```

```python
from contextlib import ExitStack

import concourse.bass as bass
from concourse import mybir

F32 = mybir.dt.float32
ACT = mybir.ActivationFunctionType
ALU = mybir.AluOpType
AX = mybir.AxisListType
ds = bass.ds

P = 128
D = 1024
S = 1024
KT = D // P
HALF = 512
HY = 768
HYT = HY // P
HD = 64
PAIRS = 4
GROUPS = 3
COL_GATE_HY = 3 * HY
COL_QKV = 4 * HY
COL_GATE_AT = COL_QKV + 9 * 512
COL_MIX = COL_GATE_AT + 512
NB_IN = 80
EPS = 1e-6

ROW_CONV_W, ROW_CONV_B, ROW_QG, ROW_KG, ROW_HF = 0, 54, 72, 73, 74
ROWS_B = 78


def sbuf(ctx, nc, name, shape, dt=F32):
    return ctx.enter_context(nc.sbuf_tensor(name, shape, dt))


def sems(ctx, nc, *names):
    return [ctx.enter_context(nc.semaphore(n)) for n in names]


def count_from_one(nc, *counted):
    with nc.Block() as block:
        @block.sync
        def _(sync):
            for s in counted:
                sync.sem_inc(s, 1)


def wait_alone(eng, passed, sem, value):
    eng.wait_ge(sem, value)
    eng.sem_inc(passed, 1)


def w_view(w, k):
    return w.rearrange("(k p) n -> p k n", p=P) if k > 1 else w


def normalise(nc, ps, keep, x, norm_g, b_in, conv_w, conv_b, hf_b, q_g, k_g, squares):
    xn_t, sq, cols_in, cols_p = keep["xn_t"], keep["squares"], keep["cols_in"], keep["cols_p"]
    with ExitStack() as ctx:
        xt = sbuf(ctx, nc, "x_tok", [P, KT, D])
        xs = sbuf(ctx, nc, "x_scaled", [P, 2, D])
        junk = sbuf(ctx, nc, "x_squares", [P, 2, D])
        stat = sbuf(ctx, nc, "x_stat", [P, 4, KT])
        rows_in = sbuf(ctx, nc, "rows_in", [P, P])
        rows_p = sbuf(ctx, nc, "rows_p", [P, P])
        x_in = sems(ctx, nc, *[f"x_in{t}" for t in range(KT)])
        table_in, rows_clear, rows_ready, cols_done, cols_kept = sems(
            ctx, nc, "table_in", "rows_clear", "rows_ready", "cols_done", "cols_kept")
        squared, mean_done, root_done, rstd_done, scaled, turned, kept = sems(
            ctx, nc, "squared", "mean_done", "root_done", "rstd_done", "scaled", "turned", "kept")
        with nc.Block() as block:
            @block.sync
            def _(sync):
                for t in range(KT):
                    sync.dma_start(xt[:, t, :], x[t * P:(t + 1) * P, :]).then_inc(x_in[t], 16)

            @block.gpsimd
            def _(pool):
                pool.memset(rows_in[:], 0.0).then_inc(rows_clear, 1)
                pool.memset(rows_p[:], 0.0).then_inc(rows_clear, 1)

            @block.scalar
            def _(act):
                act.dma_start(sq[:], squares).then_inc(table_in, 16)
                act.wait_ge(rows_clear, 2)
                act.dma_start(rows_in[0:NB_IN, :], b_in.rearrange("a (c p) -> (a c) p", p=P)).then_inc(rows_ready, 16)
                act.dma_start(rows_in[NB_IN:NB_IN + KT, :], norm_g.rearrange("a (c p) -> (a c) p", p=P)).then_inc(rows_ready, 16)
                act.dma_start(rows_p[0:54, :], conv_w.rearrange("j (c p) -> (j c) p", p=P)).then_inc(rows_ready, 16)
                act.dma_start(rows_p[54:72, :], conv_b.rearrange("a (c p) -> (a c) p", p=P)).then_inc(rows_ready, 16)
                for e in range(2):
                    act.dma_start(rows_p[ROW_QG:ROW_QG + 1, e * HD:(e + 1) * HD], q_g).then_inc(rows_ready, 16)
                    act.dma_start(rows_p[ROW_KG:ROW_KG + 1, e * HD:(e + 1) * HD], k_g).then_inc(rows_ready, 16)
                for n, v in enumerate(hf_b):
                    act.dma_start(rows_p[ROW_HF + n:ROW_HF + n + 1, 0:HD], v).then_inc(rows_ready, 16)
                for t in range(KT):
                    act.wait_ge(x_in[t], 16)
                    if t >= 2:
                        act.wait_ge(squared, t - 1)
                    act.activation(junk[:, t % 2, :], xt[:, t, :], ACT.Square, accum_out=stat[:, 0, t:t + 1]).then_inc(squared, 1)
                act.wait_ge(mean_done, 1)
                act.activation(stat[:, 2, :], stat[:, 1, :], ACT.Sqrt).then_inc(root_done, 1)

            @block.vector
            def _(dve):
                dve.wait_ge(cols_done, 1)
                dve.tensor_copy(cols_in[:], ps[:, 0, 0:P]).then_inc(cols_kept, 1)
                dve.tensor_copy(cols_p[:], ps[:, 1, 0:P]).then_inc(cols_kept, 1)
                dve.wait_ge(squared, KT)
                dve.tensor_scalar(stat[:, 1, :], stat[:, 0, :], 1.0 / D, EPS, ALU.mult, ALU.add).then_inc(mean_done, 1)
                dve.wait_ge(root_done, 1)
                dve.reciprocal(stat[:, 3, :], stat[:, 2, :]).then_inc(rstd_done, 1)
                dve.wait_ge(rstd_done, 1)
                dve.wait_ge(cols_kept, 2)
                gain = cols_in[:, NB_IN:NB_IN + KT].unsqueeze(2).to_broadcast([P, KT, P])
                for t in range(KT):
                    for u in ([0, 1] if t == 0 else [t + 1] if t + 1 < KT else []):
                        if u >= 2:
                            dve.wait_ge(turned, u - 1)
                        dve.tensor_scalar(xs[:, u % 2, :], xt[:, u, :], stat[:, 3, u:u + 1], None, ALU.mult).then_inc(scaled, 1)
                    dve.wait_ge(turned, t + 1)
                    b = 4 * (t % 2)
                    for hh in range(2):
                        dve.tensor_tensor(xn_t[:, 4 * hh:4 * hh + 4, t * P:(t + 1) * P],
                                          ps[:, b + hh, :].rearrange("p (k n) -> p k n", n=P),
                                          gain[:, 4 * hh:4 * hh + 4, :], ALU.mult).then_inc(kept, 1)

            @block.tensor
            def _(pe):
                ident = sq[:, 0, :]
                pe.wait_ge(table_in, 16)
                pe.wait_ge(rows_ready, 16 * 12)
                pe.transpose(ps[:, 0, 0:P], rows_in[:], ident)
                pe.transpose(ps[:, 1, 0:P], rows_p[:], ident).then_inc(cols_done, 1)
                pe.wait_ge(cols_kept, 2)
                for t in range(KT):
                    pe.wait_ge(scaled, t + 1)
                    if t >= 2:
                        pe.wait_ge(kept, 2 * (t - 1))
                    for k in range(KT):
                        last = pe.transpose(ps[:, 4 * (t % 2) + k // 4, (k % 4) * P:(k % 4 + 1) * P],
                                            xs[:, t % 2, k * P:(k + 1) * P], ident)
                    last.then_inc(turned, 1)


def hyena_in(nc, ps, keep, w_in, v_tok, x1_tok, x2_t):
    xn_t, ident, cols_in, cols_p = keep["xn_t"], keep["squares"][:, 0, :], keep["cols_in"], keep["cols_p"]
    w_cols = w_view(w_in, KT)
    with ExitStack() as ctx:
        w = sbuf(ctx, nc, "w_hy", [P, 4, KT, P])
        z = sbuf(ctx, nc, "z_pad", [P, 3, S + 2])
        zc = sbuf(ctx, nc, "z_conv", [P, 3, S])
        gate = sbuf(ctx, nc, "hy_gate", [P, S])
        tok = sbuf(ctx, nc, "z_tok", [P, 2, 8, P])
        w_ready = sems(ctx, nc, *[f"w_ready{s}" for s in range(4)])
        tok_out = sems(ctx, nc, "tok_out0", "tok_out1")
        [x2_out] = sems(ctx, nc, "x2_out")
        proj_done, bank_free, z_ready, z_free, conv_step, conv_done, turned, turn_free, tok_ready, gate_ready, mul_done = sems(
            ctx, nc, "proj_done", "bank_free", "z_ready", "z_free", "conv_step", "conv_done", "turned", "turn_free",
            "tok_ready", "gate_ready", "mul_done")
        count_from_one(nc, *tok_out, turned, x2_out)

        with nc.Block() as block:
            @block.sync
            def _(sync):
                for s in range(4):
                    sync.dma_start(w[:, s], w_cols[:, :, s * HY:s * HY + P]).then_inc(w_ready[s], 16)
                with sync.Fori(1, HYT) as i:
                    for s in range(4):
                        sync.wait_ge(proj_done, i * 4 + (s - 3))
                        sync.dma_start(w[:, s], w_cols[:, :, ds(i * P + s * HY, P)]).then_inc(w_ready[s], 16)
                    sync.wait_ge(mul_done, i)
                    sync.dma_start(x2_t[ds(i * P - P, P), :], zc[:, 2, :]).then_inc(x2_out, 16)
                sync.wait_ge(mul_done, HYT)
                sync.dma_start(x2_t[(HYT - 1) * P:HYT * P, :], zc[:, 2, :]).then_inc(x2_out, 16)
                sync.wait_ge(x2_out, 1 + 16 * HYT)

            @block.tensor
            def _(pe):
                with pe.Fori(0, HYT) as i:
                    for s in range(4):
                        pe.wait_ge(w_ready[s], i * 16 + 16)
                        b = 2 * (s % 2)
                        pe.wait_ge(bank_free, i * 4 + s + 1)
                        for h in range(2):
                            for k in range(KT):
                                last = pe.matmul(ps[:, b + h, :], w[:, s, k, :], xn_t[:, k, h * HALF:(h + 1) * HALF],
                                                 start=(k == 0), stop=(k == KT - 1))
                        last.then_inc(proj_done, 1)
                        if s in (1, 2):
                            r = s - 1
                            pe.wait_ge(conv_done, i * 3 + r + 1)
                            pe.wait_ge(turn_free, i * 2 + r + 1)
                            rows = zc[:, r, :].rearrange("p (s j) -> p j s", j=8)
                            for j in range(8):
                                last = pe.transpose(ps[:, 4 + 2 * r + j // 4, (j % 4) * P:(j % 4 + 1) * P], rows[:, j], ident)
                            last.then_inc(turned, 1)

            @block.scalar
            def _(act):
                act.sem_inc(bank_free, 2)
                with act.Fori(0, HYT) as i:
                    for s in range(4):
                        b = 2 * (s % 2)
                        act.wait_ge(proj_done, i * 4 + s + 1)
                        bias = cols_in[:, ds(i + HYT * s, 1)]
                        src = ps[:, b:b + 2, :].rearrange("p a n -> p (a n)")
                        act.wait_ge(z_free, i * 4 + s + 1)
                        if s < 3:
                            act.activation(z[:, s, 1:S + 1], src, ACT.Identity, bias=bias).then_inc(z_ready, 1)
                            act.wait_ge(z_ready, i * 3 + s + 1)
                        else:
                            act.activation(gate[:], src, ACT.Silu, bias=bias).then_inc(gate_ready, 1)
                            act.wait_ge(gate_ready, i + 1)
                        act.sem_inc(bank_free, 1)
                        if s >= 2:
                            r = s - 2
                            act.wait_ge(turned, 1 + i * 2 + r + 1)
                            act.wait_ge(tok_out[r], 1 + i * 16)
                            act.activation(tok[:, r].rearrange("p j n -> p (j n)"),
                                           ps[:, 4 + 2 * r:6 + 2 * r, :].rearrange("p a n -> p (a n)"), ACT.Copy).then_inc(tok_ready, 1)
                            act.wait_ge(tok_ready, i * 2 + r + 1)
                            act.sem_inc(turn_free, 1)
                            dst = (v_tok, x1_tok)[r]
                            act.dma_start(dst[:, :, ds(i * P, P)].rearrange("j q c -> q j c"), tok[:, r]).then_inc(tok_out[r], 16)
                for r in range(2):
                    act.wait_ge(tok_out[r], 1 + 16 * HYT)

            @block.gpsimd
            def _(pool):
                pool.sem_inc(turn_free, 2)

            @block.vector
            def _(dve):
                dve.memset(z[:], 0.0).then_inc(conv_step, 1)
                dve.wait_ge(conv_step, 1)
                dve.sem_inc(z_free, 4)
                with dve.Fori(0, HYT) as i:
                    for s in range(3):
                        tap = [cols_p[:, ds(i + HYT * s + 18 * j, 1)] for j in range(3)]
                        shift = cols_p[:, ds(i + HYT * s + ROW_CONV_B, 1)]
                        dve.wait_ge(z_ready, i * 3 + s + 1)
                        if s < 2:
                            dve.wait_ge(turned, 1 + i * 2 + s)
                        else:
                            dve.wait_ge(x2_out, 1 + i * 16)
                        dve.tensor_scalar(zc[:, s, :], z[:, s, 0:S], tap[0], shift, ALU.mult, ALU.add).then_inc(conv_step, 1)
                        dve.wait_ge(conv_step, i * 6 + 2 * s + 2)
                        dve.scalar_tensor_tensor(zc[:, s, :], z[:, s, 1:S + 1], tap[1], zc[:, s, :], ALU.mult, ALU.add).then_inc(conv_step, 1)
                        dve.wait_ge(conv_step, i * 6 + 2 * s + 3)
                        dve.scalar_tensor_tensor(zc[:, s, :], z[:, s, 2:S + 2], tap[2], zc[:, s, :], ALU.mult, ALU.add).then_inc(conv_done, 1)
                        dve.wait_ge(conv_done, i * 3 + s + 1)
                        dve.sem_inc(z_free, 1)
                    dve.wait_ge(gate_ready, i + 1)
                    dve.tensor_tensor(zc[:, 2, :], zc[:, 2, :], gate[:], ALU.mult).then_inc(mul_done, 1)
                    dve.wait_ge(mul_done, i + 1)
                    dve.sem_inc(z_free, 1)


CH = 128
CHUNKS = HY // CH
NJ, NM = 8, 16
INV_2PI = 0.15915494309189535
ROUND = 12582912.0
TWO_PI = (6.28125, 0.0019350051879882812, 3.019916050e-07)
PI_BELOW = 3.1415925


def filter_mlp(nc, ps, keep, h_t, work, z_t, hf_w):
    cols_p = keep["cols_p"]
    with ExitStack() as ctx:
        feat = sbuf(ctx, nc, "features", [33, S])
        w = sbuf(ctx, nc, "hf_w", [HD, 3, HD])
        loaded, prod, arg, done = sems(ctx, nc, "mlp_loaded", "mlp_prod", "mlp_arg", "mlp_done")
        arg_x, turns = work[0:HD, 0:S], work[0:HD, S:2 * S]
        with nc.Block() as block:
            @block.sync
            def _(sync):
                sync.dma_start(feat[:], z_t).then_inc(loaded, 16)
                for n, v in enumerate(hf_w):
                    sync.dma_start(w[0:v.shape[0], n, :], v).then_inc(loaded, 16)

            @block.tensor
            def _(pe):
                pe.wait_ge(loaded, 64)
                for n in range(3):
                    if n:
                        pe.wait_ge(done, n)
                    for h in range(2):
                        src = feat[:, h * HALF:(h + 1) * HALF] if n == 0 else h_t[:, h * HALF:(h + 1) * HALF]
                        pe.matmul(ps[0:HD, h, :], w[0:33 if n == 0 else HD, n, :], src, start=True, stop=True).then_inc(prod, 1)

            @block.vector
            def _(dve):
                freq = cols_p[0:HD, ROW_HF + 3:ROW_HF + 4]
                step = 0
                for n in range(3):
                    dve.wait_ge(prod, 2 * n + 2)
                    src = ps[0:HD, 0:2, :].rearrange("p a n -> p (a n)")
                    dve.tensor_scalar(arg_x, src, cols_p[0:HD, ROW_HF + n:ROW_HF + n + 1], freq, ALU.add, ALU.mult).then_inc(arg, 1)
                    step += 1
                    dve.wait_ge(arg, step)
                    dve.tensor_scalar(turns, arg_x, INV_2PI, ROUND, ALU.mult, ALU.add).then_inc(arg, 1)
                    step += 1
                    dve.wait_ge(arg, step)
                    dve.tensor_scalar(turns, turns, -ROUND, None, ALU.add).then_inc(arg, 1)
                    step += 1
                    for part in TWO_PI:
                        dve.wait_ge(arg, step)
                        dve.scalar_tensor_tensor(arg_x, turns, -part, arg_x, ALU.mult, ALU.add).then_inc(arg, 1)
                        step += 1
                    dve.wait_ge(arg, step)
                    dve.tensor_scalar(arg_x, arg_x, PI_BELOW, -PI_BELOW, ALU.min, ALU.max).then_inc(arg, 1)
                    step += 1

            @block.scalar
            def _(act):
                for n in range(3):
                    act.wait_ge(arg, 7 * (n + 1))
                    act.wait_ge(prod, 2 * n + 2)
                    act.activation(h_t[:], arg_x, ACT.Sin).then_inc(done, 1)
                act.wait_ge(done, 3)


def hyena_mix(nc, ps, keep, v_tok, x1_tok, x2_t, y_t, dft, decay, skip, z_t, hf_w, w4):
    with ExitStack() as ctx:
        dft_sb = sbuf(ctx, nc, "dft_sb", [P, 38, P])
        h_t = sbuf(ctx, nc, "h_t", [HD, S])
        v = sbuf(ctx, nc, "v_chunk", [P, NJ, CH])
        x1 = sbuf(ctx, nc, "x1_chunk", [P, NJ, CH])
        x2 = sbuf(ctx, nc, "x2_chunk", [P, S])
        dec = sbuf(ctx, nc, "decay_chunk", [P, 2, NJ, CH])
        w4c = sbuf(ctx, nc, "w4_chunk", [HD, 2, 2, CH])
        skc = sbuf(ctx, nc, "skip_chunk", [1, 2, CH])
        taps = sbuf(ctx, nc, "filter_taps", [P, NJ, 2, CH])
        stage_f = sbuf(ctx, nc, "stage_filter", [P, 4, 2, 2, CH])
        stage_d = sbuf(ctx, nc, "stage_data", [P, 4, 2, CH])
        filt = sbuf(ctx, nc, "filter_mid", [P, NM, 2, CH])
        spec = sbuf(ctx, nc, "spectrum", [P, 2, NM, CH])
        spec_x = sbuf(ctx, nc, "spectrum_x", [P, 2, NM, CH])
        mid = sbuf(ctx, nc, "data_mid", [P, NM, CH])
        back = sbuf(ctx, nc, "data_back", [P, NJ, 2, CH])
        prod1 = sbuf(ctx, nc, "prod1", [P, 4, CH])
        prod2 = sbuf(ctx, nc, "prod2", [P, 4, CH])
        ybuf = sbuf(ctx, nc, "y_spec", [P, 2, 4, CH])
        work = sbuf(ctx, nc, "mlp_work", [HD, 2 * S])
        filter_mlp(nc, ps, keep, h_t, work, z_t, hf_w)

        m1 = lambda j, h: dft_sb[:, 2 * j + h, :]
        m2 = lambda m: dft_sb[:, 16 + (m > 0), :]
        m2c = lambda m: dft_sb[:, 18 + (m > 0), :]
        i1 = lambda m: dft_sb[:, 20 + (m > 0), :]
        i2 = lambda j, h: dft_sb[:, 22 + 2 * j + h, :]
        flat = lambda ap: ap.rearrange("p a c -> p (a c)") if len(ap.shape) == 3 else ap.rearrange("p a b c -> p (a b c)")

        dft_in, v_in, x1_in, x2_in, y_ready, y_out = sems(ctx, nc, "dft_in", "v_in", "x1_in", "x2_in", "y_ready", "y_out")
        filt_in = sems(ctx, nc, "filt_in0", "filt_in1")
        sent_f = sems(ctx, nc, *[f"sent_f{s}" for s in range(4)])
        sent_d = sems(ctx, nc, "sent_d0", "sent_d1")
        a_full, taps_step, taps_ready, f_full, f_kept, k_full, spec_ready, k_kept = sems(
            ctx, nc, "a_full", "taps_step", "taps_ready", "f_full", "f_kept", "k_full", "spec_ready", "k_kept")
        d_full, d_kept, x_full, x_used, prod_done, y_done, i_full, i_kept, back_in, r_full, r_used, pair_fixed = sems(
            ctx, nc, "d_full", "d_kept", "x_full", "x_used", "prod_done", "y_done", "i_full", "i_kept", "back_in", "r_full",
            "r_used", "pair_fixed")
        count_from_one(nc, taps_ready, *sent_f, *sent_d, f_kept, d_kept, x_used, i_kept, r_used, k_kept, y_out)

        with nc.Block() as block:
            def conv(c, o):
                return lambda k, b: c * (2 * k) + (o * k + b)

            def schedule(one_chunk, eng):
                with eng.Fori(0, CHUNKS - 1) as c:
                    one_chunk(c, False)
                one_chunk(CHUNKS - 1, True)

            @block.sync
            def _(sync):
                def load_filters(c, o):
                    at = conv(c, o)
                    sync.dma_start(w4c[:, o], w4.rearrange("k (o d c) -> k o d c", o=2, d=2)[:, o, :, ds(c * CH, CH)]).then_inc(filt_in[o], 16)
                    sync.dma_start(dec[:, o], decay[:, :, ds(c * CH, CH)]).then_inc(filt_in[o], 16)
                    sync.dma_start(skc[0:1, o, :], skip[:, o, ds(c * CH, CH)]).then_inc(filt_in[o], 16)

                def load_data(c):
                    sync.dma_start(v[:], v_tok.rearrange("j q c -> q j c")[:, :, ds(c * CH, CH)]).then_inc(v_in, 16)
                    sync.dma_start(x1[:], x1_tok.rearrange("j q c -> q j c")[:, :, ds(c * CH, CH)]).then_inc(x1_in, 16)

                def regroup_filters(c, o):
                    at = conv(c, o)
                    for j in range(NJ):
                        sync.wait_ge(f_kept, 1 + at(8, j + 1))
                        sync.dma_start(filt[16 * j:16 * j + 16].rearrange("q m d c -> q (m d c)"), flat(stage_f[:, j % 4])).then_inc(sent_f[j % 4], 16)

                def regroup_data(c, o):
                    at = conv(c, o)
                    for j in range(NJ):
                        if j % 2 == 0:
                            sync.wait_ge(d_kept, 1 + at(4, j // 2 + 1))
                        sync.dma_start(mid[16 * j:16 * j + 16].rearrange("q m c -> q (m c)"), stage_d[:, j % 4].rearrange("p h c -> p (h c)")).then_inc(sent_d[j // 2 % 2], 16)

                def regroup_back(c, o):
                    at = conv(c, o)
                    sync.wait_ge(i_kept, 1 + at(4, 4))
                    for j in range(NJ):
                        sync.dma_start(back[:, j].rearrange("p h c -> p (h c)"), mid[16 * j:16 * j + 16].rearrange("q m c -> q (m c)")).then_inc(back_in, 16)

                def one_chunk(c, last):
                    regroup_data(c, 0)
                    sync.wait_ge(y_out, 1 + c * 16)
                    sync.dma_start(x2[:], x2_t[ds(c * CH, CH), :]).then_inc(x2_in, 16)
                    regroup_filters(c, 1)
                    if not last:
                        load_filters(c + 1, 0)
                    regroup_back(c, 0)
                    regroup_data(c, 1)
                    if not last:
                        load_data(c + 1)
                        regroup_filters(c + 1, 0)
                        sync.wait_ge(taps_ready, 1 + c * 16 + 16)
                        load_filters(c + 1, 1)
                    regroup_back(c, 1)
                    sync.wait_ge(y_ready, c * 2 + 2)
                    sync.dma_start(y_t[ds(c * CH, CH), :], x2[:]).then_inc(y_out, 16)

                sync.dma_start(dft_sb[:], dft).then_inc(dft_in, 16)
                load_filters(0, 0)
                load_filters(0, 1)
                load_data(0)
                regroup_filters(0, 0)
                schedule(one_chunk, sync)
                sync.wait_ge(y_out, 1 + 16 * CHUNKS)

            @block.tensor
            def _(pe):
                def filter_taps(c, o, steps):
                    at = conv(c, o)
                    for j in steps:
                        if j == 0:
                            pe.wait_ge(filt_in[o], c * 48 + 48)
                        if j < NJ:
                            pe.wait_ge(taps_ready, 1 + at(8, j))
                            pe.matmul(ps[:, 0, 0:2 * CH], h_t[:, j * P:(j + 1) * P], w4c[:, o].rearrange("k d c -> k (d c)"),
                                      start=True, stop=True).then_inc(a_full, 1)
                        if j:
                            i = j - 1
                            pe.wait_ge(taps_ready, 1 + at(8, i + 1))
                            pe.wait_ge(f_kept, 1 + at(8, max(0, i - 1)))
                            for h in range(2):
                                last = pe.matmul(ps[:, 2 + i % 2, h * 2 * CH:(h + 1) * 2 * CH], m1(i, h), taps[:, i].rearrange("p d c -> p (d c)"),
                                                 start=True, stop=True)
                            last.then_inc(f_full, 1)

                def filter_spectrum(c, o):
                    at = conv(c, o)
                    for s in range(4):
                        pe.wait_ge(sent_f[s], 1 + at(32, 32))
                    for g in range(4):
                        if g >= 2:
                            pe.wait_ge(k_kept, 1 + at(4, g - 1))
                        for m in range(4 * g, 4 * g + 4):
                            out = ps[:, 4 + g % 2, (m % 4) * CH:(m % 4 + 1) * CH]
                            pe.matmul(out, m2(m), filt[:, m, 0, :], start=True, stop=False)
                            last = pe.matmul(out, m2c(m), filt[:, m, 1, :], start=False, stop=True)
                        last.then_inc(k_full, 1)

                def data_first(c, o):
                    at = conv(c, o)
                    if o == 0:
                        pe.wait_ge(v_in, c * 16 + 16)
                    for n in range(4):
                        if o == 1:
                            pe.wait_ge(r_used, 1 + c * 4 + (n // 2 + 1))
                        if n >= 2:
                            pe.wait_ge(d_kept, 1 + at(4, n - 1))
                        for j in (2 * n, 2 * n + 1):
                            for h in range(2):
                                last = pe.matmul(ps[:, 6 + n % 2, (2 * (j % 2) + h) * CH:(2 * (j % 2) + h + 1) * CH], m1(j, h), v[:, j, :],
                                                 start=True, stop=True)
                        last.then_inc(d_full, 1)

                def data_second(c, o, following):
                    at = conv(c, o)
                    for r in range(2):
                        pe.wait_ge(sent_d[r], 1 + at(64, 64))
                    pe.wait_ge(k_kept, 1 + at(4, 4))
                    for g in range(5):
                        if g < 4:
                            if g >= 2:
                                pe.wait_ge(x_used, 1 + at(4, g - 1))
                            for m in range(4 * g, 4 * g + 4):
                                last = pe.matmul(ps[:, 4 + g % 2, (m % 4) * CH:(m % 4 + 1) * CH], m2(m), mid[:, m, :], start=True, stop=True)
                            last.then_inc(x_full, 1)
                            if following:
                                filter_taps(*following, range(5 + g, 6 + g))
                        if g > 0:
                            k = g - 1
                            pe.wait_ge(y_done, at(8, 2 * k + 2))
                            if k >= 2:
                                pe.wait_ge(i_kept, 1 + at(4, k - 1))
                            for m in range(4 * k, 4 * k + 4):
                                last = pe.matmul(ps[:, 6 + k % 2, (m % 4) * CH:(m % 4 + 1) * CH], i1(m), ybuf[:, k % 2, m % 4, :], start=True, stop=True)
                            last.then_inc(i_full, 1)

                def data_last(c, o):
                    pe.wait_ge(back_in, conv(c, o)(128, 128))
                    for n in range(2):
                        for j in range(4 * n, 4 * n + 4):
                            out = ps[:, n, (j % 4) * P:(j % 4 + 1) * P]
                            for h in range(2):
                                if o:
                                    last = pe.matmul(out, back[:, j, h, :], i2(j, h), start=(h == 0), stop=(h == 1))
                                else:
                                    last = pe.matmul(out, i2(j, h), back[:, j, h, :], start=(h == 0), stop=(h == 1))
                        last.then_inc(r_full, 1)

                def one_chunk(c, last):
                    for o in range(2):
                        following = (c, 1) if o == 0 else None if last else (c + 1, 0)
                        data_first(c, o)
                        pe.wait_ge(r_used, 1 + conv(c, o)(2, 0))
                        if following:
                            filter_taps(*following, range(5))
                        data_second(c, o, following)
                        if following:
                            filter_spectrum(*following)
                        data_last(c, o)

                pe.wait_ge(dft_in, 16)
                filter_taps(0, 0, range(NJ + 1))
                filter_spectrum(0, 0)
                schedule(one_chunk, pe)

            @block.scalar
            def _(act):
                def filter_taps(c, o, steps):
                    at = conv(c, o)
                    for j in steps:
                        act.wait_ge(f_full, at(8, j + 1))
                        act.wait_ge(sent_f[j % 4], 1 + at(32, 16 * (j // 4)))
                        act.activation(flat(stage_f[:, j % 4]), ps[:, 2 + j % 2, :], ACT.Copy).then_inc(f_kept, 1)

                def filter_spectrum(c, o):
                    at = conv(c, o)
                    for g in range(4):
                        act.wait_ge(k_full, at(4, g + 1))
                        bank = ps[:, 4 + g % 2, :]
                        act.activation(flat(spec[:, o, 4 * g:4 * g + 4]), bank, ACT.Copy).then_inc(spec_ready, 1)
                        sx = flat(spec_x[:, o, 4 * g:4 * g + 4])
                        act.activation(sx[0:64], bank[64:128], ACT.Copy).then_inc(spec_ready, 1)
                        act.activation(sx[64:128], bank[0:64], ACT.Copy).then_inc(spec_ready, 1)
                        if g == 0:
                            act.wait_ge(spec_ready, at(13, 3))
                            act.activation(spec_x[64:65, o, 0, :], bank[64:65, 0:CH], ACT.Copy).then_inc(spec_ready, 1)
                        act.wait_ge(spec_ready, at(13, 3 * g + 4))
                        act.sem_inc(k_kept, 1)

                def data_first(c, o):
                    at = conv(c, o)
                    for n in range(4):
                        act.wait_ge(d_full, at(4, n + 1))
                        act.wait_ge(sent_d[n % 2], 1 + at(64, 32 * (n // 2)))
                        act.activation(flat(stage_d[:, 2 * (n % 2):2 * (n % 2) + 2]), ps[:, 6 + n % 2, :], ACT.Copy).then_inc(d_kept, 1)

                def data_second(c, o, following):
                    at = conv(c, o)
                    for g in range(5):
                        if g < 4 and following:
                            filter_taps(*following, [4 + g])
                        if g:
                            act.wait_ge(i_full, at(4, g))
                            act.activation(flat(mid[:, 4 * g - 4:4 * g]), ps[:, 6 + (g - 1) % 2, :], ACT.Copy).then_inc(i_kept, 1)

                def one_chunk(c, last):
                    for o in range(2):
                        following = (c, 1) if o == 0 else None if last else (c + 1, 0)
                        data_first(c, o)
                        if following:
                            filter_taps(*following, range(4))
                        data_second(c, o, following)
                        if following:
                            filter_spectrum(*following)

                filter_taps(0, 0, range(NJ))
                filter_spectrum(0, 0)
                schedule(one_chunk, act)

            @block.vector
            def _(dve):
                def filter_taps(c, o, steps):
                    at = conv(c, o)
                    for j in steps:
                        if j == 0:
                            dve.wait_ge(filt_in[o], c * 48 + 48)
                        dve.wait_ge(a_full, at(8, j + 1))
                        dve.tensor_tensor(taps[:, j], ps[:, 0, 0:2 * CH].rearrange("p (d c) -> p d c", d=2),
                                          dec[:, o, j, :].unsqueeze(1).to_broadcast([P, 2, CH]), ALU.mult).then_inc(taps_step, 1)
                        dve.wait_ge(taps_step, at(10, j + (3 if j else 1)))
                        if j == 0:
                            dve.memset(taps[0:1, 0, 1, :], 0.0).then_inc(taps_step, 1)
                            dve.tensor_tensor(taps[0:1, 0, 0, :], taps[0:1, 0, 0, :], skc[0:1, o, :], ALU.add).then_inc(taps_step, 1)
                            dve.wait_ge(taps_step, at(10, 3))
                        dve.sem_inc(taps_ready, 1)

                def data_second(c, o, following):
                    at = conv(c, o)
                    dve.wait_ge(spec_ready, at(13, 13))
                    dve.memset(spec[64:65, o, 0, :], 0.0).then_inc(pair_fixed, 1)
                    dve.memset(spec_x[0:1, o, 0, :], 0.0).then_inc(pair_fixed, 1)
                    dve.wait_ge(pair_fixed, at(2, 2))
                    for g in range(4):
                        dve.wait_ge(x_full, at(4, g + 1))
                        bank = ps[:, 4 + g % 2, :].rearrange("p (m c) -> p m c", m=4)
                        dve.tensor_tensor(prod1[:], bank, spec[:, o, 4 * g:4 * g + 4, :], ALU.mult).then_inc(prod_done, 1)
                        dve.tensor_tensor(prod2[:], bank, spec_x[:, o, 4 * g:4 * g + 4, :], ALU.mult).then_inc(prod_done, 1)
                        dve.wait_ge(prod_done, at(8, 2 * g + 2))
                        dve.sem_inc(x_used, 1)
                        if g >= 2:
                            dve.wait_ge(i_full, at(4, g - 1))
                        dve.tensor_tensor(ybuf[0:64, g % 2], prod1[0:64], prod1[64:128], ALU.subtract).then_inc(y_done, 1)
                        dve.wait_ge(y_done, at(8, 2 * g + 1))
                        dve.tensor_tensor(ybuf[64:128, g % 2], prod2[0:64], prod2[64:128], ALU.add).then_inc(y_done, 1)
                        dve.wait_ge(y_done, at(8, 2 * g + 2))
                        if following and g < 3:
                            filter_taps(*following, [5 + g])

                def data_last(c, o):
                    for n in range(2):
                        dve.wait_ge(r_full, conv(c, o)(2, n + 1))
                        if o == 0:
                            if n == 0:
                                dve.wait_ge(x1_in, c * 16 + 16)
                            dve.tensor_tensor(v[:, 4 * n:4 * n + 4, :], ps[:, n, :].rearrange("p (j c) -> p j c", j=4),
                                              x1[:, 4 * n:4 * n + 4, :], ALU.mult).then_inc(r_used, 1)
                        else:
                            if n == 0:
                                dve.wait_ge(x2_in, c * 16 + 16)
                            out = x2[:].rearrange("p (s j) -> p j s", j=8)[:, 4 * n:4 * n + 4, :]
                            dve.tensor_tensor(out, ps[:, n, :].rearrange("p (j s) -> p j s", j=4), out, ALU.mult).then_inc(y_ready, 1)
                            dve.wait_ge(y_ready, c * 2 + (n + 1))
                            dve.sem_inc(r_used, 1)

                def one_chunk(c, last):
                    for o in range(2):
                        following = (c, 1) if o == 0 else None if last else (c + 1, 0)
                        if following:
                            filter_taps(*following, range(5))
                        data_second(c, o, following)
                        data_last(c, o)

                filter_taps(0, 0, range(NJ))
                schedule(one_chunk, dve)


NV = 29


def score_tiles():
    tiles = []
    for t in range(8):
        k0, k1 = max(0, P * t - 64), min(S, P * t + 192)
        blocks = [(0, 64, 0), (64, 128, 1)] if t == 0 else [(0, 128, t), (128, 128 if t < 7 else 64, t + 1)]
        tiles.append(dict(g=0, q=(P * t, 1, P), k=(k0, 1, k1 - k0), w=k1 - k0, tab=64 if t == 0 else 0, blocks=blocks))
    for r in range(4):
        for t in range(2):
            blocks = [(0, 64, 9 + 3 * r), (64, 128, 10 + 3 * r)] if t == 0 else [(0, 128, 10 + 3 * r), (128, 64, 11 + 3 * r)]
            tiles.append(dict(g=1, q=(r + 512 * t, 4, P), k=(r + 256 * t, 4, 192), w=192,
                              tab=256 + (64 if t == 0 else 0), blocks=blocks))
    for r in range(8):
        tiles.append(dict(g=2, q=(r, 8, P), k=(r, 8, P), w=P, tab=512, blocks=[(0, P, 21 + r)]))
    off = 0
    for x in tiles:
        x["off"] = off
        off += x["w"]
    return tiles, off


def value_tiles():
    out = [(0, (0, 1, 64))] + [(0, (64 + P * n, 1, P)) for n in range(7)] + [(0, (960, 1, 64))]
    for r in range(4):
        out += [(1, (r, 4, 64)), (1, (r + 256, 4, P)), (1, (r + 768, 4, 64))]
    out += [(2, (r, 8, P)) for r in range(8)]
    return out


def tokens(ap, where):
    first, step, count = where
    return ap[:, first:first + step * (count - 1) + 1:step]


def attention(nc, ps, keep, w_in, alibi):
    xn_t, sq, cols_in, cols_p, att = keep["xn_t"], keep["squares"], keep["cols_in"], keep["cols_p"], keep["att_t"]
    ident, pair_ones = sq[:, 0, :], sq[:, 1, :]
    tiles, width = score_tiles()
    vts = value_tiles()
    NT = len(tiles)
    blocks = [(x, b) for x in tiles for b in x["blocks"]]
    NBLK = len(blocks)
    QUADS = NBLK // 4
    v_batches = [list(range(a, min(a + 4, b))) for a0, b in ((0, 9), (9, 21), (21, 29)) for a in range(a0, b, 4)]
    NVB = len(v_batches)
    w_cols = w_view(w_in, KT)
    with ExitStack() as ctx:
        w = sbuf(ctx, nc, "w_at", [P, 5, KT, P])
        qk = sbuf(ctx, nc, "qk", [P, 6, S])
        sqr = sbuf(ctx, nc, "qk_squares", [P, 4, HALF])
        rs = sbuf(ctx, nc, "qk_root", [P, 2, HALF])
        vt = sbuf(ctx, nc, "v_t", [P, S])
        vx = sbuf(ctx, nc, "v_tok_one", [P, NV, 2, HD + 1])
        gate = sbuf(ctx, nc, "at_gate", [P, S])
        table = sbuf(ctx, nc, "alibi_pair", [P, 2, 640])
        sc = sbuf(ctx, nc, "scores", [P, 2, width])
        mx = sbuf(ctx, nc, "tile_max", [P, 2, NT])
        mrow = sbuf(ctx, nc, "max_row", [1, S])
        nmx = sbuf(ctx, nc, "minus_max", [P, 2, NT])
        pts = sbuf(ctx, nc, "probs_t", [P, 2, 4, P])
        o_s = sbuf(ctx, nc, "out_t", [P, S])
        rden = sbuf(ctx, nc, "rden", [P, KT])
        diag = sbuf(ctx, nc, "rden_diag", [P, KT, P])
        normed = sbuf(ctx, nc, "out_normed", [P, S])
        small = sbuf(ctx, nc, "small", [P, 66])
        w_ready = sems(ctx, nc, *[f"aw_ready{s}" for s in range(5)])
        consts, table_in, p_full, p_free, evac, v_read, sq_ready, n_full, n_root, n_recip, qk_ready = sems(
            ctx, nc, "consts", "at_table_in", "at_p_full", "at_p_free", "at_evac", "at_v_read", "at_sq_ready", "at_n_full", "at_n_root",
            "at_n_recip", "at_qk_ready")
        sc_full, sc_ready, row_full, row_kept, row_ready, neg_full, neg_ready, exp_done = sems(
            ctx, nc, "sc_full", "sc_ready", "row_full", "row_kept", "row_ready", "neg_full", "neg_ready", "exp_done")
        vx_full, vx_ready, pt_full, pt_ready, pv_done, o_kept, den_full, rd_ready, bc_full, o_norm, o_done = sems(
            ctx, nc, "vx_full", "vx_ready", "pt_full", "pt_ready", "pv_done", "o_kept", "den_full", "rd_ready", "bc_full", "o_norm", "o_done")
        count_from_one(nc, n_root, row_kept, vx_ready, pt_ready, o_kept, o_norm, n_full, vx_full, o_done, n_recip)

        TILES10 = [(0, 0), (1, 0), (0, 1), (1, 1), (0, 2), (1, 2), (2, 0), (2, 1), (2, 2), None]

        def first_col(n):
            return COL_GATE_AT if TILES10[n] is None else COL_QKV + TILES10[n][0] * 1536 + TILES10[n][1] * 512

        def one_pair(step):
            for n in range(7):
                step("project", n, 0, 0, KT)
                if n:
                    step("norm", n - 1, 0)
                    step("norm", n - 1, 1)
                step("project", n, 1, 0, KT)
            step("project", 7, 0, 0, KT // 2)

            def fillers():
                def projection(n, first):
                    return [("project", n, u // KT, u % KT, u % KT + 2) for u in range(first, 2 * KT, 2)]
                p7, p8 = projection(7, KT // 2), projection(8, 0)
                yield from [("values", 0), p7[0], ("values", 1), p7[1], ("values", 2)] + p7[2:]
                yield from [("values", 3), p8[0], ("values", 4), p8[1], ("values", 5)] + p8[2:]
                yield from [("values", 6), ("values", 7)]

            fill = fillers()
            batches = 0

            def one_filler():
                nonlocal batches
                for f in fill:
                    if f[0] == "values":
                        step("values", f[1], shared)
                        batches += 1
                    else:
                        step(*f)
                    break

            shared = False
            for n in range(0, NT, 2):
                step("score", 0, n)
                step("score", 0, n + 1)
                one_filler()
            for n in range(0, NT, 2):
                step("score", 1, n)
                step("score", 1, n + 1)
                one_filler()
                if n // 2 < GROUPS:
                    step("max_row", 0, n // 2)
                if n // 2 == GROUPS:
                    step("max_cols", 0, batches)
                    shared = True
                if n // 2 > GROUPS:
                    step("exps", 0, 4 * (n // 2 - GROUPS - 1), min(NT, 4 * (n // 2 - GROUPS)))
            for _ in range(NVB):
                one_filler()
            for q in range(QUADS + 1):
                if q < QUADS:
                    step("turn", 0, q)
                if 1 <= q <= GROUPS:
                    step("max_row", 1, q - 1)
                if q == GROUPS + 1:
                    step("max_cols", 1, batches)
                    step("exps", 1, 0, NT)
                if q:
                    step("weigh", 0, q - 1)
            step("keep_out", 0)
            for q in range(QUADS + 1):
                if q < QUADS:
                    step("turn", 1, q)
                if q == 2:
                    step("denominator", 0)
                if q in (5, 7):
                    step("divide", 0, (q - 5) // 2)
                if q:
                    step("weigh", 1, q - 1)
            step("keep_out", 1)
            step("project", 9, 0, 0, KT)
            step("denominator", 1)
            step("project", 9, 1, 0, KT)
            step("divide", 1, 0)
            step("divide", 1, 1)
            step("gate")

        with nc.Block() as block:
            @block.sync
            def _(sync):
                for n in range(5):
                    sync.dma_start(w[:, n], w_cols[:, :, first_col(n):first_col(n) + P]).then_inc(w_ready[n], 16)
                sync.dma_start(table[:], alibi[0]).then_inc(table_in, 16)
                with sync.Fori(0, PAIRS - 1) as i:
                    for n in range(5, 15):
                        sync.wait_ge(p_full, i * 20 + 2 * (n - 5) + 2)
                        col = ds(i * P + (first_col(n % 10) + (P if n >= 10 else 0)), P)
                        sync.dma_start(w[:, n % 5], w_cols[:, :, col]).then_inc(w_ready[n % 5], 16)
                    sync.wait_ge(sc_ready, i * (2 * NT) + 2 * NT)
                    sync.dma_start(table[:], alibi[ds(i + 1, 1)].rearrange("a p h n -> p (a h) n")).then_inc(table_in, 16)
                for n in range(5, 10):
                    sync.wait_ge(p_full, 20 * (PAIRS - 1) + 2 * (n - 5) + 2)
                    col = (PAIRS - 1) * P + first_col(n)
                    sync.dma_start(w[:, n % 5], w_cols[:, :, col:col + P]).then_inc(w_ready[n % 5], 16)

            @block.gpsimd
            def _(pool):
                pool.memset(small[:, 0:1], EPS).then_inc(consts, 1)
                pool.memset(small[:, 1:65], 1.0).then_inc(consts, 1)
                pool.memset(small[:, 65:66], -1.0).then_inc(consts, 1)
                pool.memset(vx[:, :, :, HD:HD + 1], 1.0).then_inc(consts, 1)

            @block.tensor
            def _(pe):
                pe.wait_ge(consts, 4)
                with pe.Fori(0, PAIRS) as i:
                    def project(n, h, k0, k1):
                        if k0 == 0:
                            pe.wait_ge(w_ready[n % 5], i * 32 + (16 if n < 5 else 32))
                            pe.wait_ge(p_free, i * 20 + 2 * n + h + 1)
                            if n == 9 and h == 0:
                                pe.wait_ge(pt_ready, 1 + i * (2 * QUADS) + 2 * QUADS)
                        for k in range(k0, k1):
                            last = pe.matmul(ps[:, h, :], w[:, n % 5, k, :], xn_t[:, k, h * HALF:(h + 1) * HALF],
                                             start=(k == 0), stop=(k == KT - 1))
                        if k1 == KT:
                            last.then_inc(p_full, 1)

                    def norm(n, h):
                        m = 2 * n + h
                        pe.wait_ge(sq_ready, i * 12 + m + 1)
                        if m >= 2:
                            pe.wait_ge(n_root, 1 + i * 12 + (m - 1))
                        else:
                            pe.wait_ge(o_norm, 1 + i * 4)
                        pe.matmul(ps[:, 2 + h, :], pair_ones, sqr[:, m % 4, :], start=True, stop=True).then_inc(n_full, 1)

                    def score(e, n):
                        x, at = tiles[n], NT * e + n
                        rows = slice(64 * e, 64 * e + 64)
                        if at == 0:
                            pe.wait_ge(qk_ready, i * 12 + 12)
                        if at >= 2:
                            pe.wait_ge(sc_ready, i * (2 * NT) + (at - 1))
                        pe.matmul(ps[:, 4 + n % 2, 0:x["w"]], tokens(qk[rows, 2 * x["g"]], x["q"]),
                                  tokens(qk[rows, 2 * x["g"] + 1], x["k"]), start=True, stop=True).then_inc(sc_full, 1)

                    def max_row(e, g):
                        bank = 4 if e else 6
                        pe.wait_ge(sc_ready, i * (2 * NT) + (NT * e + NT))
                        if e == 0 and g == 0:
                            pe.wait_ge(o_kept, 1 + i * 2)
                        pe.wait_ge(row_kept, 1 + i * 6 + (3 * e + g))
                        for n, x in enumerate(tiles):
                            if x["g"] != g:
                                continue
                            col = mx[:, e, n:n + 1]
                            if g == 0:
                                last = pe.matmul(ps[0:1, bank + n // 4, (n % 4) * P:(n % 4 + 1) * P], col, ident, start=True, stop=True)
                            elif g == 1:
                                r, t = (n - 8) // 2, n % 2
                                last = pe.matmul(ps[0:1, bank + t, r:r + 4 * (P - 1) + 1:4], col, ident, start=True, stop=True)
                            else:
                                for t in range(2):
                                    last = pe.matmul(tokens(ps[0:1, bank + t, :], (n - 16, 8, 64)), col, ident[:, 64 * t:64 * t + 64],
                                                     start=True, stop=True)
                        last.then_inc(row_full, 1)

                    def max_cols(e, batches):
                        pe.wait_ge(row_ready, i * 2 + (e + 1))
                        pe.wait_ge(vx_ready, 1 + i * NVB + batches)
                        for n, x in enumerate(tiles):
                            last = pe.matmul(ps[:, 2, n:n + 1], tokens(mrow[:], x["q"]), small[0:1, 65:66], start=True, stop=True)
                        last.then_inc(neg_full, 1)

                    def values(n, shared):
                        batch = v_batches[n]
                        pe.wait_ge(evac, i * 20 + (12 + 2 * vts[batch[0]][0] + 2))
                        if shared:
                            pe.wait_ge(neg_ready, i * 2 + 1)
                        wait_alone(pe, keep["passed"], vx_ready, 1 + i * NVB + n)
                        for b, tile in enumerate(batch):
                            where = vts[tile][1]
                            keys = where[2]
                            last = pe.transpose(ps[0:keys, 2, b * P:(b + 1) * P], tokens(vt[:], where), ident)
                        last.then_inc(vx_full, 1)

                    def turn(e, qd):
                        t = QUADS * e + qd
                        wait_alone(pe, keep["passed"], exp_done, i * (2 * NT) + (NT * e + tiles.index(blocks[4 * qd + 3][0]) + 1))
                        if t == 1:
                            wait_alone(pe, keep["passed"], p_free, i * 20 + 19)
                        if t >= 2:
                            wait_alone(pe, keep["passed"], pt_ready, 1 + i * (2 * QUADS) + (t - 1))
                        for b in range(4):
                            x, (c, keys, _) = blocks[4 * qd + b]
                            last = pe.transpose(ps[0:keys, (3, 0)[t % 2], b * P:(b + 1) * P], sc[:, e, x["off"] + c:x["off"] + c + keys], ident)
                        last.then_inc(pt_full, 1)

                    def weigh(e, qd):
                        if qd == 0:
                            pe.wait_ge(o_kept, 1 + i * 2 + e)
                            pe.wait_ge(vx_ready, 1 + i * NVB + NVB)
                        pe.wait_ge(pt_ready, 1 + i * (2 * QUADS) + (QUADS * e + qd + 1))
                        for b in range(4):
                            x, (c, keys, tile) = blocks[4 * qd + b]
                            probs = pts[0:keys, qd % 2, b, :]
                            val = vx[0:keys, tile, e, :]
                            first, step, _ = x["q"]
                            if x["g"] < 2:
                                lo = first % HALF
                                last = pe.matmul(ps[0:HD + 1, 6 + first // HALF, lo:lo + step * (P - 1) + 1:step], val, probs,
                                                 start=(x["g"] == 0 and first % HALF == 0 and c == 0), stop=False, skip_group_check=True)
                            else:
                                for t in range(2):
                                    last = pe.matmul(tokens(ps[0:HD + 1, 6 + t, :], (first, 8, 64)), val, probs[:, 64 * t:64 * t + 64],
                                                     start=False, stop=(qd == QUADS - 1 and b == 3), skip_group_check=True)
                        last.then_inc(pv_done, 1)

                    def denominator(e):
                        pe.wait_ge(o_kept, 1 + i * 2 + (e + 1))
                        if e == 0:
                            pe.wait_ge(neg_ready, i * 2 + 2)
                        else:
                            pe.wait_ge(o_norm, 1 + i * 4 + 2)
                        for j in range(KT):
                            last = pe.matmul(ps[:, 2, j:j + 1], o_s[64:65, j * P:(j + 1) * P], small[64:65, 1:2], start=True, stop=True)
                        last.then_inc(den_full, 1)

                    def divide(e, h):
                        pe.wait_ge(rd_ready, i * 4 + (2 * e + 2))
                        pe.wait_ge(o_norm, 1 + i * 4 + (2 * e + h))
                        pe.matmul(ps[0:HD, 2, :], small[:, 1:65], diag[:, 4 * h:4 * h + 4, :].rearrange("p j n -> p (j n)"),
                                  start=True, stop=True).then_inc(bc_full, 1)

                    do = dict(project=project, norm=norm, score=score, max_row=max_row, max_cols=max_cols, values=values,
                              turn=turn, weigh=weigh, denominator=denominator, divide=divide)
                    one_pair(lambda name, *a: do[name](*a) if name in do else None)

            @block.scalar
            def _(act):
                act.sem_inc(p_free, 2)
                act.wait_ge(consts, 4)
                with act.Fori(0, PAIRS) as i:
                    def project(n, h, k0, k1):
                        if k1 < KT:
                            return
                        wait_alone(act, keep["passed"], p_full, i * 20 + 2 * n + h + 1)
                        half = slice(h * HALF, (h + 1) * HALF)
                        bias = cols_in[:, ds(i + first_col(n) // P, 1)]
                        if n < 6:
                            act.activation(qk[:, n, half], ps[:, h, :], ACT.Identity, bias=bias).then_inc(evac, 1)
                            wait_alone(act, keep["passed"], n_full, 1 + i * 12 + max(0, 2 * n + h - 3))
                            act.activation(sqr[:, (2 * n + h) % 4, :], ps[:, h, :], ACT.Square, bias=bias).then_inc(sq_ready, 1)
                            act.wait_ge(sq_ready, i * 12 + 2 * n + h + 1)
                        elif n < 9:
                            wait_alone(act, keep["passed"], vx_full, 1 + i * NVB + (0, 3, 6)[n - 6])
                            act.activation(vt[:, half], ps[:, h, :], ACT.Identity, bias=bias).then_inc(evac, 1)
                        else:
                            wait_alone(act, keep["passed"], o_done, 1 + i * 2)
                            act.activation(gate[:, half], ps[:, h, :], ACT.Silu, bias=bias).then_inc(evac, 1)
                        act.wait_ge(evac, i * 20 + 2 * n + h + 1)
                        act.sem_inc(p_free, 1)

                    def norm(n, h):
                        act.wait_ge(n_full, 1 + i * 12 + 2 * n + h + 1)
                        act.wait_ge(n_recip, 1 + i * 24 + 2 * max(0, 2 * n + h - 1))
                        act.activation(rs[:, h, :], ps[:, 2 + h, :], ACT.Sqrt, bias=small[:, 0:1], scale=1.0 / HD).then_inc(n_root, 1)

                    def exps(e, first, until):
                        act.wait_ge(neg_ready, i * 2 + (e + 1))
                        for n in range(first, until):
                            x = tiles[n]
                            s = sc[:, e, x["off"]:x["off"] + x["w"]]
                            act.activation(s, s, ACT.Exp, bias=nmx[:, e, n:n + 1]).then_inc(exp_done, 1)

                    def keep_out(e):
                        act.wait_ge(pv_done, i * (2 * QUADS) + QUADS * (e + 1))
                        act.wait_ge(o_norm, 1 + i * 4 + 2 * e)
                        act.activation(o_s[0:HD + 1, :], ps[0:HD + 1, 6:8, :].rearrange("p a n -> p (a n)"), ACT.Copy).then_inc(o_kept, 1)

                    do = dict(project=project, norm=norm, exps=exps, keep_out=keep_out)
                    one_pair(lambda name, *a: do[name](*a) if name in do else None)

            @block.vector
            def _(dve):
                with dve.Fori(0, PAIRS) as i:
                    def norm(n, h):
                        gain = cols_p[:, (ROW_QG, ROW_KG)[n % 2]:(ROW_QG, ROW_KG)[n % 2] + 1]
                        m = 2 * n + h
                        dve.wait_ge(n_root, 1 + i * 12 + m + 1)
                        dve.reciprocal(rs[:, h, :], rs[:, h, :]).then_inc(n_recip, 1)
                        dve.wait_ge(n_recip, 1 + i * 24 + 2 * m + 1)
                        x = qk[:, n, h * HALF:(h + 1) * HALF]
                        dve.scalar_tensor_tensor(x, x, gain, rs[:, h, :], ALU.mult, ALU.mult).then_inc(n_recip, 1)
                        dve.wait_ge(n_recip, 1 + i * 24 + 2 * m + 2)
                        dve.sem_inc(qk_ready, 1)

                    def score(e, n):
                        x = tiles[n]
                        if e == 0 and n == 0:
                            dve.wait_ge(table_in, i * 16 + 16)
                        wait_alone(dve, keep["passed"], sc_full, i * (2 * NT) + (NT * e + n + 1))
                        dve.tensor_tensor_reduce(sc[:, e, x["off"]:x["off"] + x["w"]], ps[:, 4 + n % 2, 0:x["w"]],
                                                 table[:, e, x["tab"]:x["tab"] + x["w"]], 0.125, -3e38, ALU.add, ALU.max,
                                                 mx[:, e, n:n + 1]).then_inc(sc_ready, 1)

                    def max_row(e, g):
                        bank = 4 if e else 6
                        src = ps[0:1, bank:bank + 2, :].rearrange("p a n -> p (a n)")
                        dve.wait_ge(row_full, i * 6 + (3 * e + g + 1))
                        if g == 0:
                            dve.tensor_copy(mrow[:], src).then_inc(row_kept, 1)
                        else:
                            dve.tensor_tensor(mrow[:], src, mrow[:], ALU.max).then_inc(row_kept, 1)
                        dve.wait_ge(row_kept, 1 + i * 6 + (3 * e + g + 1))
                        if g == GROUPS - 1:
                            dve.sem_inc(row_ready, 1)

                    def max_cols(e, batches):
                        dve.wait_ge(neg_full, i * 2 + (e + 1))
                        dve.tensor_copy(nmx[:, e, :], ps[:, 2, 0:NT]).then_inc(neg_ready, 1)

                    def values(n, shared):
                        batch = v_batches[n]
                        dve.wait_ge(vx_full, 1 + i * NVB + n + 1)
                        dve.tensor_copy(vx[:, batch[0]:batch[-1] + 1, :, 0:HD],
                                        ps[:, 2, 0:P * len(batch)].rearrange("p (b e d) -> p b e d", e=2, d=HD)).then_inc(vx_ready, 1)

                    def turn(e, qd):
                        t = QUADS * e + qd
                        dve.wait_ge(pt_full, i * (2 * QUADS) + (t + 1))
                        if t >= 2:
                            dve.wait_ge(pv_done, i * (2 * QUADS) + (t - 1))
                        dve.tensor_copy(pts[:, qd % 2].rearrange("p b n -> p (b n)"), ps[:, (3, 0)[t % 2], :]).then_inc(pt_ready, 1)

                    def denominator(e):
                        dve.wait_ge(den_full, i * 2 + (e + 1))
                        dve.reciprocal(rden[:], ps[:, 2, 0:KT]).then_inc(rd_ready, 1)
                        dve.wait_ge(rd_ready, i * 4 + (2 * e + 1))
                        dve.tensor_tensor(diag[:], ident.unsqueeze(1).to_broadcast([P, KT, P]), rden[:].unsqueeze(2).to_broadcast([P, KT, P]),
                                          ALU.mult).then_inc(rd_ready, 1)

                    def divide(e, h):
                        half = slice(h * HALF, (h + 1) * HALF)
                        dve.wait_ge(bc_full, i * 4 + (2 * e + h + 1))
                        dve.tensor_tensor(normed[64 * e:64 * e + 64, half], o_s[0:HD, half], ps[0:HD, 2, :], ALU.mult).then_inc(o_norm, 1)

                    def gated():
                        dve.wait_ge(o_norm, 1 + i * 4 + 4)
                        dve.wait_ge(evac, i * 20 + 20)
                        for h in range(2):
                            half = slice(h * HALF, (h + 1) * HALF)
                            dve.tensor_tensor(att[:, ds(i, 1), half], normed[:, half].unsqueeze(1), gate[:, half].unsqueeze(1),
                                              ALU.mult).then_inc(o_done, 1)
                        dve.wait_ge(o_done, 1 + i * 2 + 2)

                    do = dict(norm=norm, score=score, max_row=max_row, max_cols=max_cols, values=values, turn=turn,
                              denominator=denominator, divide=divide, gate=gated)
                    one_pair(lambda name, *a: do[name](*a) if name in do else None)


def merge(nc, ps, keep, w_in, w_hy, w_at, w_out, y_t, x, out):
    xn_t, cols_in, att = keep["xn_t"], keep["cols_in"], keep["att_t"]
    w_cols, hy_cols, at_cols, out_rows = w_view(w_in, KT), w_view(w_hy, HYT), w_view(w_at, PAIRS), w_view(w_out, KT)
    DT = D // P
    with ExitStack() as ctx:
        y = sbuf(ctx, nc, "y_gated", [P, HYT, S])
        merged = sbuf(ctx, nc, "merged", [P, DT, S])
        wg = sbuf(ctx, nc, "w_gates", [P, 2, 2, KT, P])
        wu = sbuf(ctx, nc, "w_up", [P, 2, HYT + PAIRS, P])
        wo = sbuf(ctx, nc, "w_out_sb", [P, KT, D])
        sig = sbuf(ctx, nc, "sigmoids", [P, 2, 2, HALF])
        part = sbuf(ctx, nc, "parts", [P, 2, HALF])
        xr = sbuf(ctx, nc, "x_again", [P, 2, D])
        w_ready = sems(ctx, nc, "mw_ready0", "mw_ready1")
        x_in = sems(ctx, nc, "xr_in0", "xr_in1")
        stored = sems(ctx, nc, "stored0", "stored1")
        y_in, wo_in, full, free, sig_ready, part_ready, merged_ready, o_full, o_ready = sems(
            ctx, nc, "m_y_in", "wo_in", "m_full", "m_free", "sig_ready", "part_ready", "merged_ready", "o_full", "o_ready")
        count_from_one(nc, part_ready)
        with nc.Block() as block:
            def load(eng, r, c_gate, c_up):
                for g in range(2):
                    eng.dma_start(wg[:, r, g], w_cols[:, :, c_gate(g)]).then_inc(w_ready[r], 16)
                eng.dma_start(wu[:, r, 0:HYT], hy_cols[:, :, c_up]).then_inc(w_ready[r], 16)
                eng.dma_start(wu[:, r, HYT:HYT + PAIRS], at_cols[:, :, c_up]).then_inc(w_ready[r], 16)

            @block.sync
            def _(sync):
                for r in range(2):
                    load(sync, r, lambda g: slice(COL_MIX + g * D + r * P, COL_MIX + g * D + r * P + P), slice(r * P, r * P + P))
                sync.dma_start(y[:], y_t.rearrange("(t q) n -> q t n", q=P)).then_inc(y_in, 16)
                with sync.Fori(1, DT // 2) as i:
                    for r in range(2):
                        sync.wait_ge(full, i * 4 + (2 * r - 2))
                        load(sync, r, lambda g: ds(i * (2 * P) + (COL_MIX + g * D + r * P), P), ds(i * (2 * P) + r * P, P))
                sync.dma_start(wo[:], out_rows).then_inc(wo_in, 16)
                for t in range(2):
                    sync.dma_start(xr[:, t, :], x[t * P:(t + 1) * P, :]).then_inc(x_in[t], 16)
                for t in range(KT):
                    sync.wait_ge(o_ready, 2 * t + 2)
                    sync.dma_start(out[t * P:(t + 1) * P, :], xr[:, t % 2, :]).then_inc(stored[t % 2], 16)
                    if t + 2 < KT:
                        sync.wait_ge(stored[t % 2], 16 * (t // 2 + 1))
                        sync.dma_start(xr[:, t % 2, :], x[(t + 2) * P:(t + 3) * P, :]).then_inc(x_in[t % 2], 16)
                for r in range(2):
                    sync.wait_ge(stored[r], 16 * (KT // 2))

            @block.tensor
            def _(pe):
                with pe.Fori(0, DT // 2) as i:
                    for r in range(2):
                        pe.wait_ge(w_ready[r], i * 64 + 64)
                        for h in range(2):
                            half = slice(h * HALF, (h + 1) * HALF)
                            pe.wait_ge(free, i * 4 + (2 * r + h + 1))
                            for g in range(2):
                                for k in range(KT):
                                    pe.matmul(ps[:, 4 * h + g, :], wg[:, r, g, k, :], xn_t[:, k, half], start=(k == 0), stop=(k == KT - 1))
                            if r == 0:
                                pe.wait_ge(y_in, 16)
                            for k in range(HYT):
                                pe.matmul(ps[:, 4 * h + 2, :], wu[:, r, k, :], y[:, k, half], start=(k == 0), stop=(k == HYT - 1))
                            for k in range(PAIRS):
                                last = pe.matmul(ps[:, 4 * h + 3, :], wu[:, r, HYT + k, :], att[:, k, half], start=(k == 0), stop=(k == PAIRS - 1))
                            last.then_inc(full, 1)
                pe.wait_ge(merged_ready, 2 * DT)
                pe.wait_ge(wo_in, 16)
                for t in range(KT):
                    for h in range(2):
                        n = 2 * t + h
                        if n >= 2:
                            pe.wait_ge(o_ready, n - 1)
                        for k in range(KT):
                            last = pe.matmul(ps[:, n % 2, :], merged[:, k, t * P:(t + 1) * P], wo[:, k, h * HALF:(h + 1) * HALF],
                                             start=(k == 0), stop=(k == KT - 1))
                        last.then_inc(o_full, 1)

            @block.scalar
            def _(act):
                with act.Fori(0, DT // 2) as i:
                    for r in range(2):
                        for h in range(2):
                            wait_alone(act, keep["passed"], full, i * 4 + (2 * r + h + 1))
                            wait_alone(act, keep["passed"], part_ready, 1 + i * 8 + max(0, 4 * r + 2 * h - 2))
                            for g in range(2):
                                bias = cols_in[:, ds(i * 2 + (COL_MIX // P + g * DT + r), 1)]
                                act.activation(sig[:, h, g, :], ps[:, 4 * h + g, :], ACT.Sigmoid, bias=bias).then_inc(sig_ready, 1)

            @block.vector
            def _(dve):
                dve.sem_inc(free, 2)
                with dve.Fori(0, DT // 2) as i:
                    for r in range(2):
                        for h in range(2):
                            n = 2 * r + h
                            for g in range(2):
                                dve.wait_ge(sig_ready, i * 8 + (2 * n + g + 1))
                                dve.tensor_tensor(part[:, g, :], sig[:, h, g, :], ps[:, 4 * h + 2 + g, :], ALU.mult).then_inc(part_ready, 1)
                            dve.wait_ge(part_ready, 1 + i * 8 + (2 * n + 2))
                            dve.sem_inc(free, 1)
                            dve.tensor_tensor(merged[:, ds(i * 2 + r, 1), h * HALF:(h + 1) * HALF], part[:, 0:1, :], part[:, 1:2, :],
                                              ALU.add).then_inc(merged_ready, 1)
                            dve.wait_ge(merged_ready, i * 4 + (n + 1))
                for t in range(KT):
                    dve.wait_ge(x_in[t % 2], 16 * (t // 2 + 1))
                    for h in range(2):
                        dve.wait_ge(o_full, 2 * t + h + 1)
                        dst = xr[:, t % 2, h * HALF:(h + 1) * HALF]
                        dve.tensor_tensor(dst, ps[:, h, :], dst, ALU.add).then_inc(o_ready, 1)


def program(nc, x, norm_g, w_in, b_in, conv_w, conv_b, hf_w1, hf_b1, hf_w2, hf_b2, hf_w3, hf_b3, hf_w4, hf_freq,
            hy_skip, q_norm_g, k_norm_g, w_hy_out, w_at_out, w_out, dft, z_t, decay, alibi, squares, out):
    v_tok = nc.dram_tensor("v_tok_d", (8, P, HY), F32).ap()
    x1_tok = nc.dram_tensor("x1_tok_d", (8, P, HY), F32).ap()
    x2_t = nc.dram_tensor("x2_t_d", (HY, S), F32).ap()
    y_t = nc.dram_tensor("y_t_d", (HY, S), F32).ap()
    with ExitStack() as ctx:
        ps = ctx.enter_context(nc.psum_tensor("psum", [P, 8, HALF], F32))
        keep = {"xn_t": sbuf(ctx, nc, "xn_t", [P, KT, S]), "squares": sbuf(ctx, nc, "squares_sb", [P, 2, P]),
                "cols_in": sbuf(ctx, nc, "cols_in", [P, P]), "cols_p": sbuf(ctx, nc, "cols_p", [P, P])}
        [keep["passed"]] = sems(ctx, nc, "passed")
        w = w_in[0]
        normalise(nc, ps, keep, x[0], norm_g, b_in, conv_w[0], conv_b, (hf_b1, hf_b2, hf_b3, hf_freq), q_norm_g, k_norm_g, squares)
        hyena_in(nc, ps, keep, w, v_tok, x1_tok, x2_t)
        hyena_mix(nc, ps, keep, v_tok, x1_tok, x2_t, y_t, dft, decay, hy_skip, z_t, (hf_w1[0], hf_w2[0], hf_w3[0]), hf_w4[0])
        keep["att_t"] = sbuf(ctx, nc, "att_t", [P, PAIRS, S])
        attention(nc, ps, keep, w, alibi)
        merge(nc, ps, keep, w, w_hy_out[0], w_at_out[0], w_out[0], y_t, x[0], out[0])


def shape_tables():
    import math
    import numpy as np

    f32 = np.float32
    a = np.arange(16)
    bq = np.arange(8)
    tau = 2.0 * np.pi

    def times(j):
        return (64 * a[:, None] + 8 * bq[None, :] + j).reshape(-1)

    col_b, col_c, col_m = (x.reshape(-1) for x in np.meshgrid(bq, np.arange(2), np.arange(8), indexing="ij"))
    m1 = np.zeros((8, 2, 128, 128))
    i2 = np.zeros((8, 2, 128, 128))
    for j in range(8):
        n = times(j)
        same = (n % 64 // 8)[:, None] == col_b[None, :]
        sign = np.where((n // 64) % 2, -1.0, 1.0)[:, None]
        for h in range(2):
            k1 = 2 * col_m[None, :] + h
            c = col_c[None, :]
            angle = tau * k1 * n[:, None] / 2048.0
            fwd = np.where(k1 > 0, np.where(c == 0, np.cos(angle), -np.sin(angle)), np.where(c == 0, 1.0, sign))
            inv = np.where(k1 > 0, np.where(c == 0, 2 * np.cos(angle), -2 * np.sin(angle)),
                           np.where(c == 0, 1.0, sign)) / 2048.0
            m1[j, h] = fwd * same
            i2[j, h] = (inv * same).T
    jj, bb, c = (x.reshape(-1) for x in np.meshgrid(np.arange(8), bq, np.arange(2), indexing="ij"))
    b = 8 * bb + jj
    k2 = np.arange(64)
    ang = tau * b[:, None] * k2[None, :] / 64.0
    cb = c[:, None]
    m2g = np.concatenate([np.where(cb == 0, np.cos(ang), np.sin(ang)),
                          np.where(cb == 0, -np.sin(ang), np.cos(ang))], 1)
    i1g = np.concatenate([np.where(cb == 0, np.cos(ang), np.sin(ang)),
                          np.where(cb == 0, -np.sin(ang), np.cos(ang))], 1).T
    q = np.arange(32)
    ang0 = tau * b[:, None] * q[None, :] / 64.0
    ang16 = tau * b[:, None] * (16 + 32 * q[None, :]) / 2048.0
    is0, is16 = (c == 0)[:, None], (c == 1)[:, None]
    im0 = -np.sin(ang0) * is0
    im0[:, 0] = np.where(c == 0, np.where(b % 2, -1.0, 1.0), 0.0)
    m2s = np.concatenate([np.cos(ang0) * is0, np.cos(ang16) * is16, im0, -np.sin(ang16) * is16], 1)
    w_re = np.where(q == 0, 1.0, 2.0)[None, :]
    jm0 = -2 * np.sin(ang0) * is0
    jm0[:, 0] = np.where(c == 0, np.where(b % 2, -1.0, 1.0), 0.0)
    i1s = np.concatenate([w_re * np.cos(ang0) * is0, 2 * np.cos(ang16) * is16, jm0, -2 * np.sin(ang16) * is16], 1).T
    conj = np.where(np.arange(128) < 64, 1.0, -1.0)[None, :]
    conj_s = conj.copy()
    conj_s[0, 64] = 1.0
    mats = np.stack([m2s, m2g, m2s * conj_s, m2g * conj, i1s, i1g])
    dft = np.concatenate([m1.reshape(16, 128, 128), mats, i2.reshape(16, 128, 128)])
    dft = np.ascontiguousarray(dft.transpose(1, 0, 2)).astype(f32)

    L, bands = 1024, 16
    order = np.concatenate([times(j) for j in range(8)])
    t = (np.arange(L, dtype=f32) / f32(L - 1)).astype(f32)
    w = (f32(tau) * np.arange(L, dtype=f32) / f32(L)).astype(f32)
    f = np.linspace(1e-4, bands - 1, bands, dtype=f32)
    fw = (f[None, :] * w[:, None]).astype(f32).astype(np.float64)
    z = np.concatenate([t[:, None], np.cos(fw), -np.sin(fw)], 1)
    z_t = np.ascontiguousarray(z[order].T).astype(f32)
    lo, hi = math.log(1e-2) / 1.5, math.log(1e-2) / 0.3
    deltas = np.abs(np.linspace(lo, hi, 768, dtype=f32))
    decay = np.exp(-(t[:, None] * deltas[None, :]).astype(f32).astype(np.float64))
    decay = np.ascontiguousarray(decay[order].reshape(8, 128, 768).transpose(1, 0, 2)).astype(f32)

    slopes = 2.0 ** (-8.0 * np.arange(1, 9) / 8.0)
    qi = np.arange(128)[:, None]
    rel = qi + 64 - np.arange(256)[None, :]
    in_band = np.abs(rel) <= 64
    k = np.arange(128)[None, :]
    rel2 = qi // 2 - k // 2
    same2 = qi % 2 == k % 2
    parts = []
    for s in slopes:
        parts.append(np.concatenate([np.where(in_band, -s * np.abs(rel), -1e30),
                                     np.where(in_band, -s * 4 * np.abs(rel), -1e30),
                                     np.where(same2, -s * 16 * np.abs(rel2), -1e30)], 1))
    alibi = (8.0 * np.stack(parts)).reshape(4, 2, 128, 640).transpose(0, 2, 1, 3)
    alibi = np.ascontiguousarray(alibi).astype(f32)
    eye = np.eye(128, dtype=f32)
    pair = np.kron(np.eye(2), np.ones((64, 64))).astype(f32)
    squares = np.ascontiguousarray(np.stack([eye, pair], 1))
    return {"dft": dft, "z_t": z_t, "decay": decay, "alibi": alibi, "squares": squares}


_INS = ["x", "norm_g", "w_in", "b_in", "conv_w", "conv_b", "hf_w1", "hf_b1", "hf_w2", "hf_b2", "hf_w3", "hf_b3", "hf_w4",
        "hf_freq", "hy_skip", "q_norm_g", "k_norm_g", "w_hy_out", "w_at_out", "w_out"]
_TABLES = ["dft", "z_t", "decay", "alibi", "squares"]


def kernel(**inputs):
    import numpy as _np
    import concourse.bacc as _bacc
    from concourse import mybir as _mybir
    from concourse.bass_utils import run_bass_kernel_spmd as _run

    nc = _bacc.Bacc("TRN2", target_bir_lowering=False, num_devices=1)
    tables = shape_tables()
    arrays, args = {}, {}
    for name in _INS + _TABLES:
        a = _np.ascontiguousarray(inputs[name] if name in inputs else tables[name])
        arrays[f"in_{name}_dram"] = a
        args[name] = nc.dram_tensor(f"in_{name}_dram", a.shape, _mybir.dt.from_np(a.dtype), kind="ExternalInput").ap()
    args["out"] = nc.dram_tensor("out_0_dram", (1, 1024, 1024), _mybir.dt.float32, kind="ExternalOutput").ap()
    program(nc, **args)
    r = _run(nc, [arrays], core_ids=[0])
    return r.results[0]["out_0_dram"]
```

```python
from contextlib import ExitStack

import concourse.bass as bass
from concourse import mybir

F32 = mybir.dt.float32
F32R = mybir.dt.float32r
ACT = mybir.ActivationFunctionType
ALU = mybir.AluOpType
ds = bass.ds

P = 128
D = 1024
S = 1024
KT = D // P
HALF = 512
HY = 768
HYT = HY // P
HD = 64
PAIRS = 4
GROUPS = 3
COL_GATE_HY = 3 * HY
COL_QKV = 4 * HY
COL_GATE_AT = COL_QKV + 9 * 512
COL_MIX = COL_GATE_AT + 512
NB_IN = 80
EPS = 1e-6
CH = 128
CHUNKS = HY // CH
NJ, NM = 8, 16

ROW_CONV_W, ROW_CONV_B, ROW_QG, ROW_KG, ROW_HF = 0, 54, 72, 73, 74
ROWS_B = 78


def sbuf(ctx, nc, name, shape, dt=F32):
    return ctx.enter_context(nc.sbuf_tensor(name, shape, dt))


def sems(ctx, nc, *names):
    return [ctx.enter_context(nc.semaphore(n)) for n in names]


def count_from_one(nc, *counted):
    with nc.Block() as block:
        @block.sync
        def _(sync):
            for s in counted:
                sync.sem_inc(s, 1)


def wait_alone(eng, passed, sem, value):
    eng.wait_ge(sem, value)
    eng.sem_inc(passed, 1)


def w_view(w, k):
    return w.rearrange("(k p) n -> p k n", p=P) if k > 1 else w


SPLIT = ((0, 0), (0, 1), (1, 0))


def normalise(nc, ps, keep, w_in, x, norm_g, b_in, conv_w, conv_b, hf_b, q_g, k_g, squares):
    xn_t, sq, cols_in, cols_p = keep["xn_t"], keep["squares"], keep["cols_in"], keep["cols_p"]
    with ExitStack() as ctx:
        xt = sbuf(ctx, nc, "x_tok", [P, KT, D])
        xs = sbuf(ctx, nc, "x_scaled", [P, 2, D])
        junk = sbuf(ctx, nc, "x_squares", [P, 2, D])
        stat = sbuf(ctx, nc, "x_stat", [P, 4, KT])
        rows_in = sbuf(ctx, nc, "rows_in", [P, P])
        rows_p = sbuf(ctx, nc, "rows_p", [P, P])
        x_in = sems(ctx, nc, *[f"x_in{t}" for t in range(KT)])
        table_in, rows_clear, rows_ready, cols_done, cols_kept = sems(
            ctx, nc, "table_in", "rows_clear", "rows_ready", "cols_done", "cols_kept")
        squared, mean_done, root_done, rstd_done, scaled, turned, kept = sems(
            ctx, nc, "squared", "mean_done", "root_done", "rstd_done", "scaled", "turned", "kept")
        with nc.Block() as block:
            @block.sync
            def _(sync):
                for t in range(KT):
                    sync.dma_start(xt[:, t, :], x[t * P:(t + 1) * P, :]).then_inc(x_in[t], 16)
                sync.wait_ge(x_in[KT - 1], 16)
                for s in range(4):
                    sync.dma_start(keep["w_hy"][:, s], w_view(w_in, KT)[:, :, s * HY:s * HY + P]).then_inc(keep["w_hy_ready"][s], 16)

            @block.gpsimd
            def _(pool):
                pool.memset(rows_in[:], 0.0).then_inc(rows_clear, 1)
                pool.memset(rows_p[:], 0.0).then_inc(rows_clear, 1)
                pool.dma_start(sq[:], squares).then_inc(table_in, 16)
                pool.wait_ge(rows_clear, 2)
                pool.dma_start(rows_in[0:NB_IN, :], b_in.rearrange("a (c p) -> (a c) p", p=P)).then_inc(rows_ready, 16)
                pool.dma_start(rows_in[NB_IN:NB_IN + KT, :], norm_g.rearrange("a (c p) -> (a c) p", p=P)).then_inc(rows_ready, 16)
                pool.dma_start(rows_p[0:54, :], conv_w.rearrange("j (c p) -> (j c) p", p=P)).then_inc(rows_ready, 16)
                pool.dma_start(rows_p[54:72, :], conv_b.rearrange("a (c p) -> (a c) p", p=P)).then_inc(rows_ready, 16)
                for e in range(2):
                    pool.dma_start(rows_p[ROW_QG:ROW_QG + 1, e * HD:(e + 1) * HD], q_g).then_inc(rows_ready, 16)
                    pool.dma_start(rows_p[ROW_KG:ROW_KG + 1, e * HD:(e + 1) * HD], k_g).then_inc(rows_ready, 16)
                for n, v in enumerate(hf_b):
                    pool.dma_start(rows_p[ROW_HF + n:ROW_HF + n + 1, 0:HD], v).then_inc(rows_ready, 16)

            @block.scalar
            def _(act):
                def root(t):
                    act.wait_ge(mean_done, t + 1)
                    act.activation(stat[:, 2, t:t + 1], stat[:, 1, t:t + 1], ACT.Sqrt).then_inc(root_done, 1)

                def scale(t):
                    act.wait_ge(rstd_done, t + 1)
                    if t >= 2:
                        act.wait_ge(turned, t - 1)
                    act.activation(xs[:, t % 2, :], xt[:, t, :], ACT.Identity, scale=stat[:, 3, t:t + 1]).then_inc(scaled, 1)

                for t in range(KT):
                    act.wait_ge(x_in[t], 16)
                    if t >= 2:
                        act.wait_ge(squared, t - 1)
                    act.activation(junk[:, t % 2, :], xt[:, t, :], ACT.Square, accum_out=stat[:, 0, t:t + 1]).then_inc(squared, 1)
                    root(t)
                    if t:
                        scale(t - 1)
                scale(KT - 1)

            @block.vector
            def _(dve):
                def mean(t):
                    dve.wait_ge(squared, t + 1)
                    dve.tensor_scalar(stat[:, 1, t:t + 1], stat[:, 0, t:t + 1], 1.0 / D, EPS, ALU.mult, ALU.add).then_inc(mean_done, 1)

                def one_over_root(t):
                    dve.wait_ge(root_done, t + 1)
                    dve.reciprocal(stat[:, 3, t:t + 1], stat[:, 2, t:t + 1]).then_inc(rstd_done, 1)

                mean(0)
                one_over_root(0)
                mean(1)
                dve.wait_ge(cols_done, 1)
                dve.tensor_copy(cols_in[:], ps[:, 2, 0:NB_IN + KT]).then_inc(cols_kept, 1)
                dve.tensor_copy(cols_p[:], ps[:, 3, 0:ROWS_B]).then_inc(cols_kept, 1)
                dve.wait_ge(cols_kept, 2)
                gain = cols_in[:, NB_IN:NB_IN + KT].unsqueeze(2).to_broadcast([P, KT, P])
                for t in range(KT):
                    if t + 1 < KT:
                        one_over_root(t + 1)
                    if t + 2 < KT:
                        mean(t + 2)
                    dve.wait_ge(turned, t + 1)
                    b = 4 * (t % 2)
                    for hh in range(2):
                        dve.tensor_tensor(xn_t[:, 4 * hh:4 * hh + 4, t * P:(t + 1) * P],
                                          ps[:, b + hh, :].rearrange("p (k n) -> p k n", n=P),
                                          gain[:, 4 * hh:4 * hh + 4, :], ALU.mult).then_inc(kept, 1)

            @block.tensor
            def _(pe):
                ident = sq[:, 0, :]
                pe.wait_ge(table_in, 16)
                for t in range(KT):
                    pe.wait_ge(scaled, t + 1)
                    if t >= 2:
                        pe.wait_ge(kept, 2 * (t - 1))
                    for k in range(KT):
                        last = pe.transpose(ps[:, 4 * (t % 2) + k // 4, (k % 4) * P:(k % 4 + 1) * P],
                                            xs[:, t % 2, k * P:(k + 1) * P], ident)
                    last.then_inc(turned, 1)
                    if t == 0:
                        pe.wait_ge(rows_ready, 16 * 12)
                        pe.transpose(ps[:, 2, 0:P], rows_in[:], ident)
                        pe.transpose(ps[:, 3, 0:P], rows_p[:], ident).then_inc(cols_done, 1)


INV_2PI = 0.15915494309189535
ROUND = 12582912.0
TWO_PI = (6.28125, 0.0019350051879882812, 3.019916050e-07)
PI_BELOW = 3.1415925


def load_filters(nc, eng, keep, c, o):
    w4, decay, skip = keep["filter_sources"]
    eng.dma_start(keep["w4c"][:, o], w4.rearrange("k (o d c) -> k o d c", o=2, d=2)[:, o, :, ds(c * CH, CH)]).then_inc(keep["filt_in"][o], 16)
    eng.dma_start(keep["dec"][:, o], decay[:, :, ds(c * CH, CH)]).then_inc(keep["filt_in"][o], 16)
    eng.dma_start(keep["skc"][0:1, o, :], skip[:, o, ds(c * CH, CH)]).then_inc(keep["filt_in"][o], 16)


def hyena_in(nc, ps, keep, w_in, v_tok, x1_tok, x2_t, z_t, hf_w, dft):
    h_t, dft_sb, dft_in = keep["h_t"], keep["dft_sb"], keep["dft_in"]
    xn_t, ident, cols_in, cols_p = keep["xn_t"], keep["squares"][:, 0, :], keep["cols_in"], keep["cols_p"]
    w_cols = w_view(w_in, KT)
    with ExitStack() as ctx:
        w, w_ready = keep["w_hy"], keep["w_hy_ready"]
        w2 = sbuf(ctx, nc, "w_hy_split", [P, 2, 2, KT, P], F32R)
        xs = keep["xn_high"], keep["xn_low"]
        z = sbuf(ctx, nc, "z_pad", [P, 3, S + 2])
        zc = sbuf(ctx, nc, "z_conv", [P, 3, S])
        gate = sbuf(ctx, nc, "hy_gate", [P, S])
        tok = sbuf(ctx, nc, "z_tok", [P, 2, 8, P])
        feat = sbuf(ctx, nc, "features", [33, S])
        hw = sbuf(ctx, nc, "hf_w", [HD, 3, HD])
        arg_x = sbuf(ctx, nc, "mlp_arg_x", [HD, S])
        turns = sbuf(ctx, nc, "mlp_turns", [HD, S])
        loaded, prod, arg, done = sems(ctx, nc, "mlp_loaded", "mlp_prod", "mlp_arg", "mlp_done")
        tok_out = sems(ctx, nc, "tok_out0", "tok_out1")
        x2_out, x_high, x_low, w_high, w_low = sems(ctx, nc, "x2_out", "x_high", "x_low", "w_high", "w_low")
        proj_done, bank_free, z_ready, z_free, conv_step, conv_done, turned, turn_free, tok_ready, gate_ready, mul_done = sems(
            ctx, nc, "proj_done", "bank_free", "z_ready", "z_free", "conv_step", "conv_done", "turned", "turn_free",
            "tok_ready", "gate_ready", "mul_done")
        count_from_one(nc, *tok_out, turned, x2_out, proj_done)

        with nc.Block() as block:
            def schedule(one_tile, layer, eng):
                for n, (first, until) in enumerate(((0, 2), (2, 4), (4, HYT - 1))):
                    with eng.Fori(first, until) as i:
                        one_tile(i, False)
                    layer(n)
                one_tile(HYT - 1, True)

            @block.sync
            def _(sync):
                sync.dma_start(feat[:], z_t).then_inc(loaded, 16)
                for n, v in enumerate(hf_w):
                    sync.dma_start(hw[0:v.shape[0], n, :], v).then_inc(loaded, 16)
                sync.dma_start(dft_sb[:], dft).then_inc(dft_in, 16)
                load_filters(nc, sync, keep, 0, 0)
                load_filters(nc, sync, keep, 0, 1)
                with sync.Fori(1, HYT) as i:
                    for s in range(4):
                        sync.wait_ge(w_low, i * 4 + (s - 3))
                        sync.dma_start(w[:, s], w_cols[:, :, ds(i * P + s * HY, P)]).then_inc(w_ready[s], 16)
                    sync.wait_ge(mul_done, i)
                    sync.dma_start(x2_t[ds(i * P - P, P), :], zc[:, 2, :]).then_inc(x2_out, 16)
                sync.wait_ge(mul_done, HYT)
                sync.dma_start(x2_t[(HYT - 1) * P:HYT * P, :], zc[:, 2, :]).then_inc(x2_out, 16)
                sync.wait_ge(x2_out, 1 + 16 * HYT)

            @block.tensor
            def _(pe):
                def one_tile(i, last):
                    for s in range(4):
                        pe.wait_ge(w_low, i * 4 + s + 1)
                        b = 2 * (s % 2)
                        pe.wait_ge(bank_free, i * 4 + s + 1)
                        for k in range(KT):
                            pe.wait_ge(x_low, k + 1)
                            for wp, xp in SPLIT:
                                for h in range(2):
                                    last = pe.matmul(ps[:, b + h, :], w2[:, s % 2, wp, k, :], xs[xp][:, k, h * HALF:(h + 1) * HALF],
                                                     start=(k == 0 and wp == xp), stop=(k == KT - 1 and wp == 1))
                        last.then_inc(proj_done, 1)
                        if s in (1, 2):
                            r = s - 1
                            pe.wait_ge(conv_done, i * 3 + r + 1)
                            pe.wait_ge(turn_free, i * 2 + r + 1)
                            rows = zc[:, r, :].rearrange("p (s j) -> p j s", j=8)
                            for j in range(8):
                                last = pe.transpose(ps[:, 4 + 2 * r + j // 4, (j % 4) * P:(j % 4 + 1) * P], rows[:, j], ident)
                            last.then_inc(turned, 1)

                def layer(n):
                    if n == 0:
                        pe.wait_ge(loaded, 64)
                    else:
                        pe.wait_ge(done, n)
                    pe.wait_ge(turn_free, 2 * (2, 4, 5)[n] + 1)
                    for h in range(2):
                        src = feat[:, h * HALF:(h + 1) * HALF] if n == 0 else h_t[:, h * HALF:(h + 1) * HALF]
                        pe.matmul(ps[0:HD, 4 + h, :], hw[0:33 if n == 0 else HD, n, :], src, start=True, stop=True).then_inc(prod, 1)

                schedule(one_tile, layer, pe)

            @block.scalar
            def _(act):
                def high_weights(i, s, first=False):
                    act.wait_ge(w_ready[s], i * 16 + 16)
                    if not first:
                        act.wait_ge(proj_done, i * 4 + s)
                    act.activation(w2[:, s % 2, 0], w[:, s], ACT.Copy).then_inc(w_high, 1)

                def one_part(i, s):
                    b = 2 * (s % 2)
                    act.wait_ge(proj_done, 1 + i * 4 + s + 1)
                    bias = cols_in[:, ds(i + HYT * s, 1)]
                    src = ps[:, b:b + 2, :].rearrange("p a n -> p (a n)")
                    act.wait_ge(z_free, i * 4 + s + 1)
                    if s < 3:
                        act.activation(z[:, s, 1:S + 1], src, ACT.Identity, bias=bias).then_inc(z_ready, 1)
                        act.wait_ge(z_ready, i * 3 + s + 1)
                    else:
                        act.activation(gate[:], src, ACT.Silu, bias=bias).then_inc(gate_ready, 1)
                        act.wait_ge(gate_ready, i + 1)
                    act.sem_inc(bank_free, 1)
                    if s >= 2:
                        r = s - 2
                        act.wait_ge(turned, 1 + i * 2 + r + 1)
                        act.wait_ge(tok_out[r], 1 + i * 16)
                        act.activation(tok[:, r].rearrange("p j n -> p (j n)"),
                                       ps[:, 4 + 2 * r:6 + 2 * r, :].rearrange("p a n -> p (a n)"), ACT.Copy).then_inc(tok_ready, 1)
                        act.wait_ge(tok_ready, i * 2 + r + 1)
                        act.sem_inc(turn_free, 1)
                        dst = (v_tok, x1_tok)[r]
                        act.dma_start(dst[:, :, ds(i * P, P)].rearrange("j q c -> q j c"), tok[:, r]).then_inc(tok_out[r], 16)

                def one_tile(i, last):
                    for s in range(4):
                        if s < 3:
                            high_weights(i, s + 1)
                        elif not last:
                            high_weights(i + 1, 0)
                        one_part(i, s)

                act.sem_inc(bank_free, 2)
                high_weights(0, 0, first=True)
                for k in range(KT):
                    act.activation(xs[0][:, k, :], xn_t[:, k, :], ACT.Copy).then_inc(x_high, 1)
                def layer(n):
                    act.wait_ge(arg, 7 * (n + 1))
                    act.wait_ge(prod, 2 * n + 2)
                    act.activation(h_t[:], arg_x[:], ACT.Sin).then_inc(done, 1)

                schedule(one_tile, layer, act)
                for r in range(2):
                    act.wait_ge(tok_out[r], 1 + 16 * HYT)

            @block.gpsimd
            def _(pool):
                pool.sem_inc(turn_free, 2)

            @block.vector
            def _(dve):
                def low_weights(i, s):
                    dve.wait_ge(w_high, i * 4 + s + 1)
                    dve.tensor_tensor(w2[:, s % 2, 1], w[:, s], w2[:, s % 2, 0].bitcast(F32), ALU.subtract).then_inc(w_low, 1)

                def one_tile(i, last):
                    for s in range(4):
                        if s < 3:
                            low_weights(i, s + 1)
                            tap = [cols_p[:, ds(i + HYT * s + 18 * j, 1)] for j in range(3)]
                            shift = cols_p[:, ds(i + HYT * s + ROW_CONV_B, 1)]
                            dve.wait_ge(z_ready, i * 3 + s + 1)
                            if s < 2:
                                dve.wait_ge(turned, 1 + i * 2 + s)
                            else:
                                dve.wait_ge(x2_out, 1 + i * 16)
                            dve.tensor_scalar(zc[:, s, :], z[:, s, 0:S], tap[0], shift, ALU.mult, ALU.add).then_inc(conv_step, 1)
                            dve.wait_ge(conv_step, i * 6 + 2 * s + 2)
                            dve.scalar_tensor_tensor(zc[:, s, :], z[:, s, 1:S + 1], tap[1], zc[:, s, :], ALU.mult, ALU.add).then_inc(conv_step, 1)
                            dve.wait_ge(conv_step, i * 6 + 2 * s + 3)
                            dve.scalar_tensor_tensor(zc[:, s, :], z[:, s, 2:S + 2], tap[2], zc[:, s, :], ALU.mult, ALU.add).then_inc(conv_done, 1)
                            dve.wait_ge(conv_done, i * 3 + s + 1)
                        else:
                            if not last:
                                low_weights(i + 1, 0)
                            dve.wait_ge(gate_ready, i + 1)
                            dve.tensor_tensor(zc[:, 2, :], zc[:, 2, :], gate[:], ALU.mult).then_inc(mul_done, 1)
                            dve.wait_ge(mul_done, i + 1)
                        dve.sem_inc(z_free, 1)

                low_weights(0, 0)
                for k in range(KT):
                    dve.wait_ge(x_high, k + 1)
                    dve.tensor_tensor(xs[1][:, k, :], xn_t[:, k, :], xs[0][:, k, :].bitcast(F32), ALU.subtract).then_inc(x_low, 1)
                dve.memset(z[:], 0.0).then_inc(conv_step, 1)
                dve.wait_ge(conv_step, 1)
                dve.sem_inc(z_free, 4)
                def layer(n):
                    def next_step(op):
                        op.then_inc(arg, 1)
                        step[0] += 1
                        dve.wait_ge(arg, step[0])

                    step = [7 * n]
                    dve.wait_ge(prod, 2 * n + 2)
                    src = ps[0:HD, 4:6, :].rearrange("p a n -> p (a n)")
                    next_step(dve.tensor_scalar(arg_x[:], src, cols_p[0:HD, ROW_HF + n:ROW_HF + n + 1], cols_p[0:HD, ROW_HF + 3:ROW_HF + 4],
                                                ALU.add, ALU.mult))
                    next_step(dve.tensor_scalar(turns[:], arg_x[:], INV_2PI, ROUND, ALU.mult, ALU.add))
                    next_step(dve.tensor_scalar(turns[:], turns[:], -ROUND, None, ALU.add))
                    for part in TWO_PI:
                        next_step(dve.scalar_tensor_tensor(arg_x[:], turns[:], -part, arg_x[:], ALU.mult, ALU.add))
                    next_step(dve.tensor_scalar(arg_x[:], arg_x[:], PI_BELOW, -PI_BELOW, ALU.min, ALU.max))

                schedule(one_tile, layer, dve)




def hyena_mix(nc, ps, keep, w_in, v_tok, x1_tok, x2_t, y_t):
    with ExitStack() as ctx:
        h_t, dft_sb, dft_in = keep["h_t"], keep["dft_sb"], keep["dft_in"]
        v = sbuf(ctx, nc, "v_chunk", [P, NJ, CH])
        x1 = sbuf(ctx, nc, "x1_chunk", [P, NJ, CH])
        x2 = sbuf(ctx, nc, "x2_chunk", [P, S])
        dec, w4c, skc, filt_in = keep["dec"], keep["w4c"], keep["skc"], keep["filt_in"]
        taps = sbuf(ctx, nc, "filter_taps", [P, 2, 2, CH])
        stage_f = sbuf(ctx, nc, "stage_filter", [P, 4, 2, 2, CH])
        stage_d = sbuf(ctx, nc, "stage_data", [P, 4, 2, CH])
        filt = sbuf(ctx, nc, "filter_mid", [P, NM, 2, CH])
        spectra = sbuf(ctx, nc, "spectra", [P, 2, 2, NM, CH])
        spec, spec_x = spectra[:, :, 0], spectra[:, :, 1]
        mid = sbuf(ctx, nc, "data_mid", [P, NM, CH])
        back = sbuf(ctx, nc, "data_back", [P, NJ, 2, CH])
        prods = sbuf(ctx, nc, "products", [P, 2, 4, CH])
        ybuf = sbuf(ctx, nc, "y_spec", [P, 2, 4, CH])

        m1 = lambda j, h: dft_sb[:, 2 * j + h, :]
        m2 = lambda m: dft_sb[:, 16 + (m > 0), :]
        m2c = lambda m: dft_sb[:, 18 + (m > 0), :]
        i1 = lambda m: dft_sb[:, 20 + (m > 0), :]
        i2 = lambda j, h: dft_sb[:, 22 + 2 * j + h, :]
        runs = lambda g: [(0, 1), (1, 4)] if g == 0 else [(4 * g, 4 * g + 4)]
        flat = lambda ap: ap.rearrange("p a c -> p (a c)") if len(ap.shape) == 3 else ap.rearrange("p a b c -> p (a b c)")

        v_in, x1_in, x2_in, y_ready, y_out = sems(ctx, nc, "v_in", "x1_in", "x2_in", "y_ready", "y_out")
        sent_f = sems(ctx, nc, *[f"sent_f{s}" for s in range(4)])
        sent_d = sems(ctx, nc, "sent_d0", "sent_d1")
        a_full, taps_step, taps_ready, f_full, f_kept, k_full, spec_ready, k_kept = sems(
            ctx, nc, "a_full", "taps_step", "taps_ready", "f_full", "f_kept", "k_full", "spec_ready", "k_kept")
        d_full, d_kept, x_full, x_used, prod_done, y_done, i_full, i_kept, back_in, r_full, r_used, pair_fixed = sems(
            ctx, nc, "d_full", "d_kept", "x_full", "x_used", "prod_done", "y_done", "i_full", "i_kept", "back_in", "r_full",
            "r_used", "pair_fixed")
        count_from_one(nc, taps_ready, *sent_f, *sent_d, f_kept, d_kept, x_used, i_kept, r_used, k_kept, y_out)

        with nc.Block() as block:
            def conv(c, o):
                return lambda k, b: c * (2 * k) + (o * k + b)

            def schedule(one_chunk, eng):
                with eng.Fori(0, CHUNKS - 1) as c:
                    one_chunk(c, False)
                one_chunk(CHUNKS - 1, True)

            @block.sync
            def _(sync):
                def load_data(c):
                    sync.dma_start(v[:], v_tok.rearrange("j q c -> q j c")[:, :, ds(c * CH, CH)]).then_inc(v_in, 16)
                    sync.dma_start(x1[:], x1_tok.rearrange("j q c -> q j c")[:, :, ds(c * CH, CH)]).then_inc(x1_in, 16)

                def regroup_filters(c, o):
                    at = conv(c, o)
                    for j in range(NJ):
                        sync.wait_ge(f_kept, 1 + at(8, j + 1))
                        sync.dma_start(filt[16 * j:16 * j + 16].rearrange("q m d c -> q (m d c)"), flat(stage_f[:, j % 4])).then_inc(sent_f[j % 4], 16)

                def regroup_data(c, o):
                    at = conv(c, o)
                    for j in range(NJ):
                        if j % 2 == 0:
                            sync.wait_ge(d_kept, 1 + at(4, j // 2 + 1))
                        sync.dma_start(mid[16 * j:16 * j + 16].rearrange("q m c -> q (m c)"), stage_d[:, j % 4].rearrange("p h c -> p (h c)")).then_inc(sent_d[j // 2 % 2], 16)

                def regroup_back(c, o):
                    at = conv(c, o)
                    sync.wait_ge(i_kept, 1 + at(4, 4))
                    for j in range(NJ):
                        sync.dma_start(back[:, j].rearrange("p h c -> p (h c)"), mid[16 * j:16 * j + 16].rearrange("q m c -> q (m c)")).then_inc(back_in, 16)

                def one_chunk(c, last):
                    regroup_data(c, 0)
                    sync.wait_ge(y_out, 1 + c * 16)
                    sync.dma_start(x2[:], x2_t[ds(c * CH, CH), :]).then_inc(x2_in, 16)
                    regroup_filters(c, 1)
                    if not last:
                        load_filters(nc, sync, keep, c + 1, 0)
                    regroup_back(c, 0)
                    regroup_data(c, 1)
                    if not last:
                        load_data(c + 1)
                        regroup_filters(c + 1, 0)
                        sync.wait_ge(taps_ready, 1 + c * 16 + 16)
                        load_filters(nc, sync, keep, c + 1, 1)
                    else:
                        for n in range(2):
                            col = COL_QKV + n * 1536
                            sync.dma_start(keep["w_at"][:, n], w_view(w_in, KT)[:, :, col:col + P]).then_inc(keep["w_at_ready"][n], 16)
                    regroup_back(c, 1)
                    sync.wait_ge(y_ready, c * 2 + 2)
                    sync.dma_start(y_t[ds(c * CH, CH), :], x2[:]).then_inc(y_out, 16)

                load_data(0)
                regroup_filters(0, 0)
                schedule(one_chunk, sync)
                sync.wait_ge(y_out, 1 + 16 * CHUNKS)

            @block.tensor
            def _(pe):
                def filter_taps(c, o, steps):
                    at = conv(c, o)
                    for j in steps:
                        if j == 0:
                            pe.wait_ge(filt_in[o], c * 48 + 48)
                        if j < NJ:
                            pe.wait_ge(taps_ready, 1 + at(8, j))
                            pe.matmul(ps[:, 0, 0:2 * CH], h_t[:, j * P:(j + 1) * P], w4c[:, o].rearrange("k d c -> k (d c)"),
                                      start=True, stop=True).then_inc(a_full, 1)
                        if j:
                            i = j - 1
                            pe.wait_ge(taps_ready, 1 + at(8, i + 1))
                            pe.wait_ge(f_kept, 1 + at(8, max(0, i - 1)))
                            for h in range(2):
                                last = pe.matmul(ps[:, 2 + i % 2, h * 2 * CH:(h + 1) * 2 * CH], m1(i, h), taps[:, i % 2].rearrange("p d c -> p (d c)"),
                                                 start=True, stop=True)
                            last.then_inc(f_full, 1)

                def filter_spectrum(c, o):
                    at = conv(c, o)
                    for s in range(4):
                        pe.wait_ge(sent_f[s], 1 + at(32, 32))
                    for g in range(4):
                        if g >= 2:
                            pe.wait_ge(k_kept, 1 + at(4, g - 1))
                        for m, end in runs(g):
                            out = ps[:, 4 + g % 2, (m % 4) * CH:(m % 4 + end - m) * CH].rearrange("p (m c) -> p m c", c=CH)
                            pe.matmul(out, m2(m), filt[:, m:end, 0, :], start=True, stop=False)
                            last = pe.matmul(out, m2c(m), filt[:, m:end, 1, :], start=False, stop=True)
                        last.then_inc(k_full, 1)

                def data_first(c, o, following):
                    at = conv(c, o)
                    if o == 0:
                        pe.wait_ge(v_in, c * 16 + 16)
                    for n in range(4):
                        if n == 2:
                            pe.wait_ge(r_used, 1 + at(2, 0))
                            if following:
                                filter_taps(*following, range(1))
                        if o == 1:
                            pe.wait_ge(r_used, 1 + c * 4 + (n // 2 + 1))
                        if n >= 2:
                            pe.wait_ge(d_kept, 1 + at(4, n - 1))
                        for j in (2 * n, 2 * n + 1):
                            for h in range(2):
                                last = pe.matmul(ps[:, 6 + n % 2, (2 * (j % 2) + h) * CH:(2 * (j % 2) + h + 1) * CH], m1(j, h), v[:, j, :],
                                                 start=True, stop=True)
                        last.then_inc(d_full, 1)

                def data_second(c, o, following):
                    at = conv(c, o)
                    for r in range(2):
                        pe.wait_ge(sent_d[r], 1 + at(64, 64))
                    pe.wait_ge(k_kept, 1 + at(4, 4))
                    for g in range(-1, 4):
                        for x in (0, 1) if g < 0 else (g + 2,) if g < 2 else ():
                            if x >= 2:
                                pe.wait_ge(x_used, 1 + at(4, x - 1))
                            for m, end in runs(x):
                                last = pe.matmul(ps[:, 4 + x % 2, (m % 4) * CH:(m % 4 + end - m) * CH], m2(m), flat(mid[:, m:end, :]), start=True, stop=True)
                            last.then_inc(x_full, 1)
                        if following and g < 3:
                            filter_taps(*following, range(6 + g, 7 + g))
                        if g >= 0:
                            pe.wait_ge(y_done, at(8, 2 * g + 2))
                            if g >= 2:
                                pe.wait_ge(i_kept, 1 + at(4, g - 1))
                            for m, end in runs(g):
                                last = pe.matmul(ps[:, 6 + g % 2, (m % 4) * CH:(m % 4 + end - m) * CH], i1(m),
                                                 flat(ybuf[:, g % 2, m % 4:m % 4 + end - m, :]), start=True, stop=True)
                            last.then_inc(i_full, 1)

                def data_last(c, o):
                    pe.wait_ge(back_in, conv(c, o)(128, 128))
                    for n in range(2):
                        for j in range(4 * n, 4 * n + 4):
                            out = ps[:, n, (j % 4) * P:(j % 4 + 1) * P]
                            for h in range(2):
                                if o:
                                    last = pe.matmul(out, back[:, j, h, :], i2(j, h), start=(h == 0), stop=(h == 1))
                                else:
                                    last = pe.matmul(out, i2(j, h), back[:, j, h, :], start=(h == 0), stop=(h == 1))
                        last.then_inc(r_full, 1)

                def one_chunk(c, last):
                    for o in range(2):
                        following = (c, 1) if o == 0 else None if last else (c + 1, 0)
                        data_first(c, o, following)
                        if following:
                            filter_taps(*following, range(1, 5))
                        data_second(c, o, following)
                        if following:
                            filter_spectrum(*following)
                        data_last(c, o)

                pe.wait_ge(dft_in, 16)
                filter_taps(0, 0, range(NJ + 1))
                filter_spectrum(0, 0)
                schedule(one_chunk, pe)

            @block.scalar
            def _(act):
                def filter_taps(c, o, steps):
                    at = conv(c, o)
                    for j in steps:
                        act.wait_ge(f_full, at(8, j + 1))
                        act.wait_ge(sent_f[j % 4], 1 + at(32, 16 * (j // 4)))
                        act.activation(flat(stage_f[:, j % 4]), ps[:, 2 + j % 2, :], ACT.Copy).then_inc(f_kept, 1)

                def filter_spectrum(c, o):
                    at = conv(c, o)
                    for g in range(4):
                        act.wait_ge(k_full, at(4, g + 1))
                        bank = ps[:, 4 + g % 2, :]
                        act.activation(flat(spec[:, o, 4 * g:4 * g + 4]), bank, ACT.Copy).then_inc(spec_ready, 1)
                        sx = flat(spec_x[:, o, 4 * g:4 * g + 4])
                        act.activation(sx[0:64], bank[64:128], ACT.Copy).then_inc(spec_ready, 1)
                        act.activation(sx[64:128], bank[0:64], ACT.Copy).then_inc(spec_ready, 1)
                        if g == 0:
                            act.wait_ge(spec_ready, at(13, 3))
                            act.activation(spec_x[64:65, o, 0, :], bank[64:65, 0:CH], ACT.Copy).then_inc(spec_ready, 1)
                        act.wait_ge(spec_ready, at(13, 3 * g + 4))
                        act.sem_inc(k_kept, 1)

                def data_first(c, o):
                    at = conv(c, o)
                    for n in range(4):
                        act.wait_ge(d_full, at(4, n + 1))
                        act.wait_ge(sent_d[n % 2], 1 + at(64, 32 * (n // 2)))
                        act.activation(flat(stage_d[:, 2 * (n % 2):2 * (n % 2) + 2]), ps[:, 6 + n % 2, :], ACT.Copy).then_inc(d_kept, 1)

                def data_second(c, o, following):
                    at = conv(c, o)
                    for g in range(5):
                        if g < 4 and following:
                            filter_taps(*following, [4 + g])
                        if g:
                            act.wait_ge(i_full, at(4, g))
                            act.activation(flat(mid[:, 4 * g - 4:4 * g]), ps[:, 6 + (g - 1) % 2, :], ACT.Copy).then_inc(i_kept, 1)

                def one_chunk(c, last):
                    for o in range(2):
                        following = (c, 1) if o == 0 else None if last else (c + 1, 0)
                        data_first(c, o)
                        if following:
                            filter_taps(*following, range(4))
                        data_second(c, o, following)
                        if following:
                            filter_spectrum(*following)

                filter_taps(0, 0, range(NJ))
                filter_spectrum(0, 0)
                schedule(one_chunk, act)

            @block.vector
            def _(dve):
                def filter_taps(c, o, steps):
                    at = conv(c, o)
                    for j in steps:
                        if j == 0:
                            dve.wait_ge(filt_in[o], c * 48 + 48)
                        dve.wait_ge(a_full, at(8, j + 1))
                        dve.tensor_tensor(taps[:, j % 2], ps[:, 0, 0:2 * CH].rearrange("p (d c) -> p d c", d=2),
                                          dec[:, o, j, :].unsqueeze(1).to_broadcast([P, 2, CH]), ALU.mult).then_inc(taps_step, 1)
                        dve.wait_ge(taps_step, at(10, j + (3 if j else 1)))
                        if j == 0:
                            dve.memset(taps[0:1, 0, 1, :], 0.0).then_inc(taps_step, 1)
                            dve.tensor_tensor(taps[0:1, 0, 0, :], taps[0:1, 0, 0, :], skc[0:1, o, :], ALU.add).then_inc(taps_step, 1)
                            dve.wait_ge(taps_step, at(10, 3))
                        dve.sem_inc(taps_ready, 1)

                def data_second(c, o, following):
                    at = conv(c, o)
                    dve.wait_ge(spec_ready, at(13, 13))
                    dve.memset(spec[64:65, o, 0, :], 0.0).then_inc(pair_fixed, 1)
                    dve.memset(spec_x[0:1, o, 0, :], 0.0).then_inc(pair_fixed, 1)
                    dve.wait_ge(pair_fixed, at(2, 2))
                    for g in range(4):
                        dve.wait_ge(x_full, at(4, g + 1))
                        dve.tensor_tensor(prods[:].rearrange("p s m c -> p s (m c)"), ps[:, 4 + g % 2, :].unsqueeze(1).to_broadcast([P, 2, 4 * CH]),
                                          spectra[:, o, :, 4 * g:4 * g + 4, :].rearrange("p s m c -> p s (m c)"), ALU.mult).then_inc(prod_done, 1)
                        dve.wait_ge(prod_done, at(4, g + 1))
                        dve.sem_inc(x_used, 1)
                        if following and g < 3:
                            filter_taps(*following, [5 + g])
                        if g >= 2:
                            dve.wait_ge(i_full, at(4, g - 1))
                        dve.tensor_tensor(ybuf[0:64, g % 2], prods[0:64, 0], prods[64:128, 0], ALU.subtract).then_inc(y_done, 1)
                        dve.wait_ge(y_done, at(8, 2 * g + 1))
                        dve.tensor_tensor(ybuf[64:128, g % 2], prods[0:64, 1], prods[64:128, 1], ALU.add).then_inc(y_done, 1)
                        dve.wait_ge(y_done, at(8, 2 * g + 2))

                def data_last(c, o):
                    for n in range(2):
                        dve.wait_ge(r_full, conv(c, o)(2, n + 1))
                        if o == 0:
                            if n == 0:
                                dve.wait_ge(x1_in, c * 16 + 16)
                            dve.tensor_tensor(v[:, 4 * n:4 * n + 4, :], ps[:, n, :].rearrange("p (j c) -> p j c", j=4),
                                              x1[:, 4 * n:4 * n + 4, :], ALU.mult).then_inc(r_used, 1)
                        else:
                            if n == 0:
                                dve.wait_ge(x2_in, c * 16 + 16)
                            out = x2[:].rearrange("p (s j) -> p j s", j=8)[:, 4 * n:4 * n + 4, :]
                            dve.tensor_tensor(out, ps[:, n, :].rearrange("p (j s) -> p j s", j=4), out, ALU.mult).then_inc(y_ready, 1)
                            dve.wait_ge(y_ready, c * 2 + (n + 1))
                            dve.sem_inc(r_used, 1)

                def one_chunk(c, last):
                    for o in range(2):
                        following = (c, 1) if o == 0 else None if last else (c + 1, 0)
                        if following:
                            filter_taps(*following, range(5))
                        data_second(c, o, following)
                        data_last(c, o)

                filter_taps(0, 0, range(NJ))
                schedule(one_chunk, dve)


NV = 29


def score_tiles():
    tiles = []
    for t in range(8):
        k0, k1 = max(0, P * t - 64), min(S, P * t + 192)
        blocks = [(0, 64, 0), (64, 128, 1)] if t == 0 else [(0, 128, t), (128, 128 if t < 7 else 64, t + 1)]
        tiles.append(dict(g=0, q=(P * t, 1, P), k=(k0, 1, k1 - k0), w=k1 - k0, tab=64 if t == 0 else 0, blocks=blocks))
    for r in range(4):
        for t in range(2):
            blocks = [(0, 64, 9 + 3 * r), (64, 128, 10 + 3 * r)] if t == 0 else [(0, 128, 10 + 3 * r), (128, 64, 11 + 3 * r)]
            tiles.append(dict(g=1, q=(r + 512 * t, 4, P), k=(r + 256 * t, 4, 192), w=192,
                              tab=256 + (64 if t == 0 else 0), blocks=blocks))
    for r in range(8):
        tiles.append(dict(g=2, q=(r, 8, P), k=(r, 8, P), w=P, tab=512, blocks=[(0, P, 21 + r)]))
    off = 0
    for x in tiles:
        x["off"] = off
        off += x["w"]
    return tiles, off


def value_tiles():
    out = [(0, (0, 1, 64))] + [(0, (64 + P * n, 1, P)) for n in range(7)] + [(0, (960, 1, 64))]
    for r in range(4):
        out += [(1, (r, 4, 64)), (1, (r + 256, 4, P)), (1, (r + 768, 4, 64))]
    out += [(2, (r, 8, P)) for r in range(8)]
    return out


def tokens(ap, where):
    first, step, count = where
    return ap[:, first:first + step * (count - 1) + 1:step]


def attention(nc, ps, keep, w_in, alibi, att_t):
    x_parts, sq, cols_in, cols_p = (keep["xn_high"], keep["xn_low"]), keep["squares"], keep["cols_in"], keep["cols_p"]
    ident, pair_ones = sq[:, 0, :], sq[:, 1, :]
    tiles, width = score_tiles()
    vts = value_tiles()
    NT = len(tiles)
    blocks = [(x, b) for x in tiles for b in x["blocks"]]
    NBLK = len(blocks)
    QUADS = NBLK // 4
    v_batches = [list(range(a, min(a + 4, b))) for a0, b in ((0, 9), (9, 21), (21, 29)) for a in range(a0, b, 4)]
    NVB = len(v_batches)
    w_cols = w_view(w_in, KT)
    with ExitStack() as ctx:
        w, w_ready = keep["w_at"], keep["w_at_ready"]
        w2 = sbuf(ctx, nc, "w_at_split", [P, 2, 2, KT, P], F32R)
        qk = sbuf(ctx, nc, "qk", [P, 6, S])
        sqr = sbuf(ctx, nc, "qk_squares", [P, HALF])
        sq_parts = [sbuf(ctx, nc, n, [P, 2, HALF], F32R) for n in ("qk_squares_high", "qk_squares_low")]
        ones_r = sbuf(ctx, nc, "pair_ones_r", [P, P], F32R)
        rs = sbuf(ctx, nc, "qk_root", [P, 2, HALF])
        vt = sbuf(ctx, nc, "v_t", [P, S])
        vx = sbuf(ctx, nc, "v_tok_one", [P, NV, 2, HD + 1])
        gate = sbuf(ctx, nc, "at_gate", [P, S])
        table = sbuf(ctx, nc, "alibi_pair", [P, 2, 640])
        sc = sbuf(ctx, nc, "scores", [P, 2, width])
        mx = sbuf(ctx, nc, "tile_max", [P, 2, NT])
        nmx = sbuf(ctx, nc, "minus_max", [P, NT, 2])
        pts = sbuf(ctx, nc, "probs_t", [P, 2, 4, P])
        o_s = sbuf(ctx, nc, "out_t", [P, S])
        rden = sbuf(ctx, nc, "rden", [P, KT])
        diag = sbuf(ctx, nc, "rden_diag", [P, KT, P])
        mrow = diag[0:2].rearrange("p j n -> p (j n)")
        normed = sbuf(ctx, nc, "out_normed", [P, S])
        small = sbuf(ctx, nc, "small", [P, 67])
        w_high, w_low, att_out, sq_high, sq_low = sems(ctx, nc, "aw_high", "aw_low", "att_out", "sq_high", "sq_low")
        consts, table_in, p_full, p_free, evac, sq_ready, n_full, n_root, n_recip, qk_ready = sems(
            ctx, nc, "consts", "at_table_in", "at_p_full", "at_p_free", "at_evac", "at_sq_ready", "at_n_full", "at_n_root",
            "at_n_recip", "at_qk_ready")
        sc_full, sc_ready, row_full, row_kept, row_ready, neg_full, neg_ready, exp_done = sems(
            ctx, nc, "sc_full", "sc_ready", "row_full", "row_kept", "row_ready", "neg_full", "neg_ready", "exp_done")
        vx_full, vx_ready, pt_full, pt_ready, pv_done, o_kept, den_full, rd_ready, bc_full, o_norm, o_done = sems(
            ctx, nc, "vx_full", "vx_ready", "pt_full", "pt_ready", "pv_done", "o_kept", "den_full", "rd_ready", "bc_full", "o_norm", "o_done")
        count_from_one(nc, n_root, row_kept, vx_ready, pt_ready, o_kept, o_norm, n_full, vx_full, o_done, n_recip, att_out, sq_low)

        TILES10 = [(0, 0), (1, 0), (0, 1), (1, 1), (0, 2), (1, 2), (2, 0), (2, 1), (2, 2), None]

        def first_col(n):
            return COL_GATE_AT if TILES10[n] is None else COL_QKV + TILES10[n][0] * 1536 + TILES10[n][1] * 512

        def one_pair(step, last):
            for n in range(7):
                step("project", n, 0, 0, KT)
                if n:
                    step("high", n + 1)
                    step("low", n + 1)
                    step("norm", n - 1, 0)
                    step("norm", n - 1, 1)
                step("project", n, 1, 0, KT)
            step("project", 7, 0, 0, KT)

            p7 = [("project", 7, 1, k, k + 2) for k in range(0, KT, 2)]
            p8 = [("project", 8, h, k, k + 2) for h in range(2) for k in range(0, KT, 2)]
            fill = [("values", 0), p7[0], ("values", 1), p7[1], ("values", 2)] + p7[2:]
            fill += [("values", 3), p8[0], ("values", 4), p8[1], ("values", 5)] + p8[2:] + [("values", 6), ("values", 7)]
            high_at = {fill.index(("values", 2)): 8, fill.index(("project", 8, 0, KT - 2, KT)): 9}
            for e in range(2):
                for n in range(0, NT, 2):
                    step("score", e, n)
                    step("score", e, n + 1)
                    at = (NT * e + n) // 2
                    if at < len(fill):
                        step(*fill[at])
                    if at in high_at:
                        step("high", high_at[at])
                    if at - 2 in high_at:
                        step("low", high_at[at - 2])
            for g in range(GROUPS):
                step("max_row", g)
                step("project", 9, 0, 2 * g, 2 * g + 2)
            step("max_cols")
            step("project", 9, 0, 6, KT)
            step("exps", 0, 0, NT)
            step("exps", 1, 0, NT // 2)
            for q in range(QUADS + 1):
                if q < QUADS:
                    step("turn", 0, q)
                if q:
                    step("weigh", 0, q - 1)
            step("keep_out", 0)
            step("exps", 1, NT // 2, NT)
            for q in range(QUADS + 1):
                if q < QUADS:
                    step("turn", 1, q)
                if q == 2:
                    step("denominator", 0)
                if q == 4 and not last:
                    step("high", 10)
                    step("low", 10)
                if q in (5, 7):
                    step("divide", 0, (q - 5) // 2)
                if q:
                    step("weigh", 1, q - 1)
            step("keep_out", 1)
            step("project", 9, 1, 0, KT // 2)
            step("denominator", 1)
            step("project", 9, 1, KT // 2, KT)
            step("divide", 1, 0)
            step("divide", 1, 1)
            step("gate")
            if not last:
                step("high", 11)
                step("low", 11)

        with nc.Block() as block:
            @block.sync
            def _(sync):
                sync.dma_start(table[:], alibi[0]).then_inc(table_in, 16)
                with sync.Fori(0, PAIRS - 1) as i:
                    for n in range(2, 12):
                        sync.wait_ge(w_low, i * 10 + n - 1)
                        col = ds(i * P + (first_col(n % 10) + (P if n >= 10 else 0)), P)
                        sync.dma_start(w[:, n % 2], w_cols[:, :, col]).then_inc(w_ready[n % 2], 16)
                    sync.wait_ge(sc_ready, i * (2 * NT) + 2 * NT)
                    sync.dma_start(table[:], alibi[ds(i + 1, 1)].rearrange("a p h n -> p (a h) n")).then_inc(table_in, 16)
                    sync.wait_ge(o_done, 1 + i * 2 + 2)
                    sync.dma_start(att_t[ds(i * P, P), :], normed[:]).then_inc(att_out, 16)
                for n in range(2, 10):
                    sync.wait_ge(w_low, 10 * (PAIRS - 1) + n - 1)
                    col = (PAIRS - 1) * P + first_col(n)
                    sync.dma_start(w[:, n % 2], w_cols[:, :, col:col + P]).then_inc(w_ready[n % 2], 16)
                sync.wait_ge(o_done, 1 + 2 * PAIRS)
                sync.dma_start(att_t[(PAIRS - 1) * P:PAIRS * P, :], normed[:]).then_inc(att_out, 16)
                sync.wait_ge(att_out, 1 + 16 * PAIRS)

            @block.gpsimd
            def _(pool):
                pool.memset(small[:, 0:1], EPS).then_inc(consts, 1)
                pool.memset(small[:, 1:65], 1.0).then_inc(consts, 1)
                pool.memset(vx[:, :, :, HD:HD + 1], 1.0).then_inc(consts, 1)
                with pool.Fori(0, PAIRS) as i:
                    for m in range(12):
                        pool.wait_ge(sq_high, i * 12 + m + 1)
                        pool.tensor_tensor(sq_parts[1][:, m % 2, :], sqr[:], sq_parts[0][:, m % 2, :].bitcast(F32),
                                           ALU.subtract).then_inc(sq_low, 1)

            @block.tensor
            def _(pe):
                pe.wait_ge(consts, 5)
                def pair(i, last):
                    def project(n, h, k0, k1):
                        if k0 == 0:
                            pe.wait_ge(w_low, i * 10 + n + 1)
                            pe.wait_ge(p_free, i * 20 + 2 * n + h + 1)
                            if n == 9 and h == 1:
                                pe.wait_ge(pt_ready, 1 + i * (2 * QUADS) + 2 * QUADS)
                        for k in range(k0, k1):
                            for wp, xp in SPLIT:
                                last = pe.matmul(ps[:, h, :], w2[:, n % 2, wp, k, :], x_parts[xp][:, k, h * HALF:(h + 1) * HALF],
                                                 start=(k == 0 and wp == xp), stop=(k == KT - 1 and wp == 1))
                        if k1 == KT:
                            last.then_inc(p_full, 1)

                    def norm(n, h):
                        m = 2 * n + h
                        pe.wait_ge(sq_low, 1 + i * 12 + m + 1)
                        if m >= 2:
                            pe.wait_ge(n_root, 1 + i * 12 + (m - 1))
                        else:
                            pe.wait_ge(o_norm, 1 + i * 4)
                        pe.matmul(ps[:, 2 + h, :], ones_r[:], sq_parts[0][:, h, :], start=True, stop=False)
                        pe.matmul(ps[:, 2 + h, :], ones_r[:], sq_parts[1][:, h, :], start=False, stop=True).then_inc(n_full, 1)

                    def score(e, n):
                        x, at = tiles[n], NT * e + n
                        rows = slice(64 * e, 64 * e + 64)
                        if at == 0:
                            pe.wait_ge(qk_ready, i * 12 + 12)
                        if at >= 2:
                            pe.wait_ge(sc_ready, i * (2 * NT) + (at - 1))
                        pe.matmul(ps[:, 4 + n % 2, 0:x["w"]], tokens(qk[rows, 2 * x["g"]], x["q"]),
                                  tokens(qk[rows, 2 * x["g"] + 1], x["k"]), start=True, stop=True).then_inc(sc_full, 1)

                    def max_row(g):
                        if g == 0:
                            pe.wait_ge(sc_ready, i * (2 * NT) + 2 * NT)
                            pe.wait_ge(o_kept, 1 + i * 2)
                        pe.wait_ge(row_kept, 1 + i * 3 + g)
                        for n, x in enumerate(tiles):
                            if x["g"] != g:
                                continue
                            cols = mx[:, :, n]
                            if g == 0:
                                last = pe.matmul(ps[0:2, 6 + n // 4, (n % 4) * P:(n % 4 + 1) * P], cols, ident, start=True, stop=True)
                            elif g == 1:
                                r, t = (n - 8) // 2, n % 2
                                last = pe.matmul(ps[0:2, 6 + t, r:r + 4 * (P - 1) + 1:4], cols, ident, start=True, stop=True)
                            else:
                                for t in range(2):
                                    last = pe.matmul(tokens(ps[0:2, 6 + t, :], (n - 16, 8, 64)), cols, ident[:, 64 * t:64 * t + 64],
                                                     start=True, stop=True)
                        last.then_inc(row_full, 1)

                    def max_cols():
                        pe.wait_ge(row_ready, i + 1)
                        pe.wait_ge(vx_ready, 1 + i * NVB + NVB)
                        for n, x in enumerate(tiles):
                            last = pe.matmul(ps[:, 2, 2 * n:2 * n + 2], tokens(mrow, x["q"]), small[0:2, 65:67], start=True, stop=True)
                        last.then_inc(neg_full, 1)

                    def values(n):
                        batch = v_batches[n]
                        pe.wait_ge(evac, i * 20 + (12 + 2 * vts[batch[0]][0] + 2))
                        wait_alone(pe, keep["passed"], vx_ready, 1 + i * NVB + n)
                        for b, tile in enumerate(batch):
                            where = vts[tile][1]
                            keys = where[2]
                            last = pe.transpose(ps[0:keys, 2, b * P:(b + 1) * P], tokens(vt[:], where), ident)
                        last.then_inc(vx_full, 1)

                    def turn(e, qd):
                        t = QUADS * e + qd
                        wait_alone(pe, keep["passed"], exp_done, i * (2 * NT) + (NT * e + tiles.index(blocks[4 * qd + 3][0]) + 1))
                        if t == 1:
                            wait_alone(pe, keep["passed"], p_free, i * 20 + 20)
                        if t >= 2:
                            wait_alone(pe, keep["passed"], pt_ready, 1 + i * (2 * QUADS) + (t - 1))
                        for b in range(4):
                            x, (c, keys, _) = blocks[4 * qd + b]
                            last = pe.transpose(ps[0:keys, (3, 1)[t % 2], b * P:(b + 1) * P], sc[:, e, x["off"] + c:x["off"] + c + keys], ident)
                        last.then_inc(pt_full, 1)

                    def weigh(e, qd):
                        if qd == 0:
                            pe.wait_ge(o_kept, 1 + i * 2 + e)
                            pe.wait_ge(vx_ready, 1 + i * NVB + NVB)
                        pe.wait_ge(pt_ready, 1 + i * (2 * QUADS) + (QUADS * e + qd + 1))
                        for b in range(4):
                            x, (c, keys, tile) = blocks[4 * qd + b]
                            probs = pts[0:keys, qd % 2, b, :]
                            val = vx[0:keys, tile, e, :]
                            first, step, _ = x["q"]
                            if x["g"] < 2:
                                lo = first % HALF
                                last = pe.matmul(ps[0:HD + 1, 6 + first // HALF, lo:lo + step * (P - 1) + 1:step], val, probs,
                                                 start=(x["g"] == 0 and first % HALF == 0 and c == 0), stop=False, skip_group_check=True)
                            else:
                                for t in range(2):
                                    last = pe.matmul(tokens(ps[0:HD + 1, 6 + t, :], (first, 8, 64)), val, probs[:, 64 * t:64 * t + 64],
                                                     start=False, stop=(qd == QUADS - 1 and b == 3), skip_group_check=True)
                        last.then_inc(pv_done, 1)

                    def denominator(e):
                        pe.wait_ge(o_kept, 1 + i * 2 + (e + 1))
                        if e == 0:
                            pe.wait_ge(neg_ready, i + 1)
                        else:
                            pe.wait_ge(o_norm, 1 + i * 4 + 2)
                        for j in range(KT):
                            last = pe.matmul(ps[:, 2, j:j + 1], o_s[64:65, j * P:(j + 1) * P], small[64:65, 1:2], start=True, stop=True)
                        last.then_inc(den_full, 1)

                    def divide(e, h):
                        pe.wait_ge(rd_ready, i * 4 + (2 * e + 2))
                        pe.wait_ge(o_norm, 1 + i * 4 + (2 * e + h))
                        pe.matmul(ps[0:HD, 2, :], small[:, 1:65], diag[:, 4 * h:4 * h + 4, :].rearrange("p j n -> p (j n)"),
                                  start=True, stop=True).then_inc(bc_full, 1)

                    do = dict(project=project, norm=norm, score=score, max_row=max_row, max_cols=max_cols, values=values,
                              turn=turn, weigh=weigh, denominator=denominator, divide=divide)
                    one_pair(lambda name, *a: do[name](*a) if name in do else None, last)

                with pe.Fori(0, PAIRS - 1) as i:
                    pair(i, False)
                pair(PAIRS - 1, True)

            @block.scalar
            def _(act):
                act.sem_inc(p_free, 2)
                act.activation(ones_r[:], pair_ones, ACT.Copy).then_inc(consts, 1)
                act.wait_ge(consts, 5)
                def pair(i, last):
                    def high(n):
                        act.wait_ge(w_ready[n % 2], i * 80 + 16 * (n // 2 + 1))
                        act.wait_ge(p_full, i * 20 + 2 * n - 2)
                        act.activation(w2[:, n % 2, 0], w[:, n % 2], ACT.Copy).then_inc(w_high, 1)

                    def project(n, h, k0, k1):
                        if k1 < KT or (n, h) == (9, 0):
                            return
                        for half in (0, 1) if n == 9 else (h,):
                            keep_half(n, half)

                    def keep_half(n, h):
                        wait_alone(act, keep["passed"], p_full, i * 20 + 2 * n + h + 1)
                        half = slice(h * HALF, (h + 1) * HALF)
                        bias = cols_in[:, ds(i + first_col(n) // P, 1)]
                        if n < 6:
                            act.activation(qk[:, n, half], ps[:, h, :], ACT.Identity, bias=bias).then_inc(evac, 1)
                            wait_alone(act, keep["passed"], n_full, 1 + i * 12 + max(0, 2 * n + h - 1))
                            wait_alone(act, keep["passed"], sq_low, 1 + i * 12 + 2 * n + h)
                            act.activation(sqr[:], ps[:, h, :], ACT.Square, bias=bias).then_inc(sq_ready, 1)
                            act.wait_ge(sq_ready, i * 12 + 2 * n + h + 1)
                            act.activation(sq_parts[0][:, h, :], sqr[:], ACT.Copy).then_inc(sq_high, 1)
                        elif n < 9:
                            wait_alone(act, keep["passed"], vx_full, 1 + i * NVB + (0, 3, 6)[n - 6])
                            act.activation(vt[:, half], ps[:, h, :], ACT.Identity, bias=bias).then_inc(evac, 1)
                        else:
                            wait_alone(act, keep["passed"], o_done, 1 + i * 2)
                            act.activation(gate[:, half], ps[:, h, :], ACT.Silu, bias=bias).then_inc(evac, 1)
                        act.wait_ge(evac, i * 20 + 2 * n + h + 1)
                        act.sem_inc(p_free, 1)

                    def norm(n, h):
                        act.wait_ge(n_full, 1 + i * 12 + 2 * n + h + 1)
                        act.wait_ge(n_recip, 1 + i * 24 + 2 * max(0, 2 * n + h - 1))
                        act.activation(rs[:, h, :], ps[:, 2 + h, :], ACT.Sqrt, bias=small[:, 0:1], scale=1.0 / HD).then_inc(n_root, 1)

                    def exps(e, first, until):
                        act.wait_ge(neg_ready, i + 1)
                        for n in range(first, until):
                            x = tiles[n]
                            s = sc[:, e, x["off"]:x["off"] + x["w"]]
                            act.activation(s, s, ACT.Exp, bias=nmx[:, n, e:e + 1]).then_inc(exp_done, 1)

                    def keep_out(e):
                        act.wait_ge(pv_done, i * (2 * QUADS) + QUADS * (e + 1))
                        act.wait_ge(o_norm, 1 + i * 4 + 2 * e)
                        act.activation(o_s[0:HD + 1, :], ps[0:HD + 1, 6:8, :].rearrange("p a n -> p (a n)"), ACT.Copy).then_inc(o_kept, 1)

                    do = dict(high=high, project=project, norm=norm, exps=exps, keep_out=keep_out)
                    one_pair(lambda name, *a: do[name](*a) if name in do else None, last)

                for n in range(2):
                    act.wait_ge(w_ready[n], 16)
                    act.activation(w2[:, n, 0], w[:, n], ACT.Copy).then_inc(w_high, 1)
                with act.Fori(0, PAIRS - 1) as i:
                    pair(i, False)
                pair(PAIRS - 1, True)

            @block.vector
            def _(dve):
                dve.tensor_scalar(small[0:2, 65:67], ident[0:2, 0:2], -1.0, None, ALU.mult).then_inc(consts, 1)
                def pair(i, last):
                    def low(n):
                        dve.wait_ge(w_high, i * 10 + n + 1)
                        dve.tensor_tensor(w2[:, n % 2, 1], w[:, n % 2], w2[:, n % 2, 0].bitcast(F32), ALU.subtract).then_inc(w_low, 1)

                    def norm(n, h):
                        gain = cols_p[:, (ROW_QG, ROW_KG)[n % 2]:(ROW_QG, ROW_KG)[n % 2] + 1]
                        m = 2 * n + h
                        dve.wait_ge(n_root, 1 + i * 12 + m + 1)
                        dve.reciprocal(rs[:, h, :], rs[:, h, :]).then_inc(n_recip, 1)
                        dve.wait_ge(n_recip, 1 + i * 24 + 2 * m + 1)
                        x = qk[:, n, h * HALF:(h + 1) * HALF]
                        dve.scalar_tensor_tensor(x, x, gain, rs[:, h, :], ALU.mult, ALU.mult).then_inc(n_recip, 1)
                        dve.wait_ge(n_recip, 1 + i * 24 + 2 * m + 2)
                        dve.sem_inc(qk_ready, 1)

                    def score(e, n):
                        x = tiles[n]
                        if e == 0 and n == 0:
                            dve.wait_ge(table_in, i * 16 + 16)
                        wait_alone(dve, keep["passed"], sc_full, i * (2 * NT) + (NT * e + n + 1))
                        dve.tensor_tensor_reduce(sc[:, e, x["off"]:x["off"] + x["w"]], ps[:, 4 + n % 2, 0:x["w"]],
                                                 table[:, e, x["tab"]:x["tab"] + x["w"]], 0.125, -3e38, ALU.add, ALU.max,
                                                 mx[:, e, n:n + 1]).then_inc(sc_ready, 1)

                    def max_row(g):
                        src = ps[0:2, 6:8, :].rearrange("p a n -> p (a n)")
                        dve.wait_ge(row_full, i * 3 + (g + 1))
                        if g == 0:
                            dve.tensor_copy(mrow, src).then_inc(row_kept, 1)
                        else:
                            dve.tensor_tensor(mrow, src, mrow, ALU.max).then_inc(row_kept, 1)
                        dve.wait_ge(row_kept, 1 + i * 3 + (g + 1))
                        if g == GROUPS - 1:
                            dve.sem_inc(row_ready, 1)

                    def max_cols():
                        dve.wait_ge(neg_full, i + 1)
                        dve.tensor_copy(nmx[:].rearrange("p n e -> p (n e)"), ps[:, 2, 0:2 * NT]).then_inc(neg_ready, 1)

                    def values(n):
                        batch = v_batches[n]
                        dve.wait_ge(vx_full, 1 + i * NVB + n + 1)
                        dve.tensor_copy(vx[:, batch[0]:batch[-1] + 1, :, 0:HD],
                                        ps[:, 2, 0:P * len(batch)].rearrange("p (b e d) -> p b e d", e=2, d=HD)).then_inc(vx_ready, 1)

                    def turn(e, qd):
                        t = QUADS * e + qd
                        dve.wait_ge(pt_full, i * (2 * QUADS) + (t + 1))
                        if t >= 2:
                            dve.wait_ge(pv_done, i * (2 * QUADS) + (t - 1))
                        dve.tensor_copy(pts[:, qd % 2].rearrange("p b n -> p (b n)"), ps[:, (3, 1)[t % 2], :]).then_inc(pt_ready, 1)

                    def denominator(e):
                        dve.wait_ge(den_full, i * 2 + (e + 1))
                        dve.reciprocal(rden[:], ps[:, 2, 0:KT]).then_inc(rd_ready, 1)
                        dve.wait_ge(rd_ready, i * 4 + (2 * e + 1))
                        dve.tensor_tensor(diag[:], ident.unsqueeze(1).to_broadcast([P, KT, P]), rden[:].unsqueeze(2).to_broadcast([P, KT, P]),
                                          ALU.mult).then_inc(rd_ready, 1)

                    def divide(e, h):
                        half = slice(h * HALF, (h + 1) * HALF)
                        dve.wait_ge(bc_full, i * 4 + (2 * e + h + 1))
                        dve.wait_ge(att_out, 1 + i * 16)
                        dve.tensor_tensor(normed[64 * e:64 * e + 64, half], o_s[0:HD, half], ps[0:HD, 2, :], ALU.mult).then_inc(o_norm, 1)

                    def gated():
                        dve.wait_ge(o_norm, 1 + i * 4 + 4)
                        dve.wait_ge(evac, i * 20 + 20)
                        for h in range(2):
                            half = slice(h * HALF, (h + 1) * HALF)
                            dve.tensor_tensor(normed[:, half], normed[:, half], gate[:, half], ALU.mult).then_inc(o_done, 1)
                        dve.wait_ge(o_done, 1 + i * 2 + 2)

                    do = dict(low=low, norm=norm, score=score, max_row=max_row, max_cols=max_cols, values=values, turn=turn,
                              denominator=denominator, divide=divide, gate=gated)
                    one_pair(lambda name, *a: do[name](*a) if name in do else None, last)

                for n in range(2):
                    dve.wait_ge(w_high, n + 1)
                    dve.tensor_tensor(w2[:, n, 1], w[:, n], w2[:, n, 0].bitcast(F32), ALU.subtract).then_inc(w_low, 1)
                with dve.Fori(0, PAIRS - 1) as i:
                    pair(i, False)
                pair(PAIRS - 1, True)


DT = D // P
UPT = PAIRS + HYT


def merge(nc, ps, keep, w_in, w_hy, w_at, w_out, y_t, att_t, x, out):
    with ExitStack() as ctx:
        share = {"gates": sbuf(ctx, nc, "gates", [P, 2, DT, S]), "raw": sbuf(ctx, nc, "to_split", [P, 2, S])}
        share["raw_in"] = sems(ctx, nc, "raw_in0", "raw_in1")
        share["raw_high"], share["raw_low"] = sems(ctx, nc, "raw_high", "raw_low")
        sources = [att_t[k * P:(k + 1) * P, :] for k in range(PAIRS)] + [y_t[k * P:(k + 1) * P, :] for k in range(HYT)]
        sources += [w_out[k * P:(k + 1) * P, :] for k in range(KT)]

        def load_raw(eng, chunk):
            if chunk >= 2:
                eng.wait_ge(share["raw_low"], chunk - 1)
            eng.dma_start(share["raw"][:, chunk % 2, :], sources[chunk]).then_inc(share["raw_in"][chunk % 2], 16)

        def high_of_raw(act, chunk, to):
            act.wait_ge(share["raw_in"][chunk % 2], 16 * (chunk // 2 + 1))
            act.activation(to, share["raw"][:, chunk % 2, :], ACT.Copy).then_inc(share["raw_high"], 1)

        def low_of_raw(dve, chunk, to, high):
            dve.wait_ge(share["raw_high"], chunk + 1)
            dve.tensor_tensor(to, share["raw"][:, chunk % 2, :], high.bitcast(F32), ALU.subtract).then_inc(share["raw_low"], 1)

        share["load_raw"], share["high_of_raw"], share["low_of_raw"] = load_raw, high_of_raw, low_of_raw
        with ExitStack() as up:
            share["wu"] = sbuf(up, nc, "w_up", [P, 2, UPT, P])
            share["att"] = [sbuf(up, nc, n, [P, PAIRS, S], F32R) for n in ("att_high", "att_low")]
            share["up_in"] = sems(up, nc, "up_in0", "up_in1")

            def load_up(eng, i, r):
                col = ds(i * (2 * P) + r * P, P)
                eng.dma_start(share["wu"][:, r, 0:PAIRS], w_view(w_at, PAIRS)[:, :, col]).then_inc(share["up_in"][r], 16)
                eng.dma_start(share["wu"][:, r, PAIRS:UPT], w_view(w_hy, HYT)[:, :, col]).then_inc(share["up_in"][r], 16)

            share["load_up"] = load_up
            merge_gates(nc, ps, keep, share, w_in)
            merge_branches(nc, ps, keep, share)
        merge_out(nc, ps, keep, share, x, out)


def merge_gates(nc, ps, keep, share, w_in):
    x_parts, cols_in, gates, att = (keep["xn_high"], keep["xn_low"]), keep["cols_in"], share["gates"], share["att"]
    w_cols = w_view(w_in, KT)
    with ExitStack() as ctx:
        wg = sbuf(ctx, nc, "w_gates", [P, 2, KT, P])
        wg2 = sbuf(ctx, nc, "w_gates_split", [P, 2, 2, KT, P], F32R)
        w_ready = sems(ctx, nc, "gw_ready0", "gw_ready1")
        w_high, w_low, full, free, ready = sems(ctx, nc, "gw_high", "gw_low", "gate_full", "gate_free", "gate_ready")
        count_from_one(nc, full)
        with nc.Block() as block:
            def schedule(one_tile, eng):
                with eng.Fori(0, DT // 2 - 1) as i:
                    one_tile(i, 0, False)
                    one_tile(i, 1, False)
                one_tile(DT // 2 - 1, 0, False)
                one_tile(DT // 2 - 1, 1, True)

            def following(i, r, g):
                return (i, r, 1) if g == 0 else (i, 1, 0) if r == 0 else (i + 1, 0, 0)

            @block.sync
            def _(sync):
                def load(i, r, g, first=False):
                    if not first:
                        sync.wait_ge(w_low, i * 4 + (2 * r + g - 1))
                    sync.dma_start(wg[:, g], w_cols[:, :, ds(i * (2 * P) + (COL_MIX + g * D + r * P), P)]).then_inc(w_ready[g], 16)

                load(0, 0, 0, first=True)
                load(0, 0, 1, first=True)
                load(0, 1, 0)
                load(0, 1, 1)
                share["load_up"](sync, 0, 0)
                share["load_up"](sync, 0, 1)
                share["load_raw"](sync, 0)
                share["load_raw"](sync, 1)
                with sync.Fori(1, DT // 2) as i:
                    for r in range(2):
                        for g in range(2):
                            load(i, r, g)
                for chunk in range(2, PAIRS + 2):
                    share["load_raw"](sync, chunk)

            @block.tensor
            def _(pe):
                def one_tile(i, r, last):
                    for g in range(2):
                        pe.wait_ge(w_low, i * 4 + (2 * r + g + 1))
                        pe.wait_ge(free, i * 4 + (2 * r + g + 1))
                        for k in range(KT):
                            for wp, xp in SPLIT:
                                for h in range(2):
                                    mm = pe.matmul(ps[:, 4 * r + 2 * g + h, :], wg2[:, g, wp, k, :], x_parts[xp][:, k, h * HALF:(h + 1) * HALF],
                                                   start=(k == 0 and wp == xp), stop=(k == KT - 1 and wp == 1))
                        mm.then_inc(full, 1)

                schedule(one_tile, pe)

            @block.scalar
            def _(act):
                def high_weights(i, r, g, first=False):
                    act.wait_ge(w_ready[g], i * 32 + (16 * r + 16))
                    if not first:
                        act.wait_ge(full, i * 4 + (2 * r + g))
                    act.activation(wg2[:, g, 0], wg[:, g], ACT.Copy).then_inc(w_high, 1)

                def one_tile(i, r, last):
                    for g in range(2):
                        if not (last and g == 1):
                            high_weights(*following(i, r, g))
                        n = 2 * r + g
                        wait_alone(act, keep["passed"], full, 1 + i * 4 + n + 1)
                        bias = cols_in[:, ds(i * 2 + (COL_MIX // P + g * DT + r), 1)]
                        act.activation(gates[:, g, ds(i * 2 + r, 1), :], ps[:, 4 * r + 2 * g:4 * r + 2 * g + 2, :].rearrange("p a n -> p (a n)").unsqueeze(1),
                                       ACT.Sigmoid, bias=bias).then_inc(ready, 1)
                        act.wait_ge(ready, i * 4 + (n + 1))
                        act.sem_inc(free, 1)
                        if isinstance(i, int) and r == 0:
                            for chunk in (2 * g, 2 * g + 1):
                                share["high_of_raw"](act, chunk, att[0][:, chunk, :])

                act.sem_inc(free, 4)
                high_weights(0, 0, 0, first=True)
                schedule(one_tile, act)

            @block.vector
            def _(dve):
                def low_weights(i, r, g):
                    dve.wait_ge(w_high, i * 4 + (2 * r + g + 1))
                    dve.tensor_tensor(wg2[:, g, 1], wg[:, g], wg2[:, g, 0].bitcast(F32), ALU.subtract).then_inc(w_low, 1)

                def one_tile(i, r, last):
                    for g in range(2):
                        if not (last and g == 1):
                            low_weights(*following(i, r, g))
                        if isinstance(i, int) and r == 0:
                            for chunk in (2 * g, 2 * g + 1):
                                share["low_of_raw"](dve, chunk, att[1][:, chunk, :], att[0][:, chunk, :])

                low_weights(0, 0, 0)
                schedule(one_tile, dve)


def merge_branches(nc, ps, keep, share):
    gates, wu, att, up_in = share["gates"], share["wu"], share["att"], share["up_in"]
    with ExitStack() as ctx:
        y = [nc.alloc_sbuf_tensor_at(n, [P, HYT, S], F32R, offset=keep[at]) for n, at in (("y_high", "xn_low_at"), ("y_low", "xn_high_at"))]
        wu2 = sbuf(ctx, nc, "w_up_split", [P, 2, 2, UPT, P], F32R)
        part = sbuf(ctx, nc, "part", [P, 1, S])
        w_high, w_low, att_full, y_full, free, part_ready, scaled, merged_ready = sems(
            ctx, nc, "uw_high", "uw_low", "u_att_full", "u_y_full", "u_free", "part_ready", "gate_scaled", "merged_ready")
        count_from_one(nc, y_full)
        with nc.Block() as block:
            def schedule(one_tile, eng):
                with eng.Fori(0, DT // 2 - 1) as i:
                    one_tile(i, 0, False)
                    one_tile(i, 1, False)
                one_tile(DT // 2 - 1, 0, False)
                one_tile(DT // 2 - 1, 1, True)

            @block.sync
            def _(sync):
                for chunk in range(PAIRS + 2, UPT + 2):
                    share["load_raw"](sync, chunk)
                with sync.Fori(1, DT // 2) as i:
                    for r in range(2):
                        wait_alone(sync, keep["passed"], w_low, i * 2 + (r - 1))
                        share["load_up"](sync, i, r)

            @block.tensor
            def _(pe):
                def one_tile(i, r, last):
                    pe.wait_ge(w_low, i * 2 + (r + 1))
                    pe.wait_ge(free, i * 2 + (r + 1))
                    for first, n_k, parts, bank, done in ((0, PAIRS, att, 4 * r + 2, att_full), (PAIRS, HYT, y, 4 * r, y_full)):
                        for k in range(n_k):
                            pe.wait_ge(share["raw_low"], first + k + 1)
                            for wp, xp in SPLIT:
                                for h in range(2):
                                    mm = pe.matmul(ps[:, bank + h, :], wu2[:, r, wp, first + k, :], parts[xp][:, k, h * HALF:(h + 1) * HALF],
                                                   start=(k == 0 and wp == xp), stop=(k == n_k - 1 and wp == 1))
                        mm.then_inc(done, 1)

                schedule(one_tile, pe)

            @block.scalar
            def _(act):
                def high_weights(i, r, first=False):
                    act.wait_ge(up_in[r], i * 32 + 32)
                    if not first:
                        act.wait_ge(y_full, i * 2 + r)
                    act.activation(wu2[:, r, 0], wu[:, r], ACT.Copy).then_inc(w_high, 1)

                high_weights(0, 0, first=True)
                for k in range(HYT):
                    share["high_of_raw"](act, PAIRS + k, y[0][:, k, :])
                with act.Fori(0, DT // 2 - 1) as i:
                    high_weights(i, 1)
                    high_weights(i + 1, 0)
                high_weights(DT // 2 - 1, 1)

            @block.vector
            def _(dve):
                def low_weights(i, r):
                    dve.wait_ge(w_high, i * 2 + (r + 1))
                    dve.tensor_tensor(wu2[:, r, 1], wu[:, r], wu2[:, r, 0].bitcast(F32), ALU.subtract).then_inc(w_low, 1)

                def one_tile(i, r, last):
                    if not last:
                        low_weights(*((i, 1) if r == 0 else (i + 1, 0)))
                    u = lambda bank: ps[:, bank:bank + 2, :].rearrange("p a n -> p (a n)").unsqueeze(1)
                    here = ds(i * 2 + r, 1)
                    dve.wait_ge(att_full, i * 2 + (r + 1))
                    dve.tensor_tensor(part[:], gates[:, 1, here, :], u(4 * r + 2), ALU.mult).then_inc(part_ready, 1)
                    dve.wait_ge(y_full, 1 + i * 2 + (r + 1))
                    dve.tensor_tensor(gates[:, 0, here, :], gates[:, 0, here, :], u(4 * r), ALU.mult).then_inc(scaled, 1)
                    dve.wait_ge(scaled, i * 2 + (r + 1))
                    dve.wait_ge(part_ready, i * 2 + (r + 1))
                    dve.sem_inc(free, 1)
                    dve.tensor_tensor(gates[:, 0, here, :], gates[:, 0, here, :], part[:], ALU.add).then_inc(merged_ready, 1)
                    dve.wait_ge(merged_ready, i * 2 + (r + 1))

                dve.sem_inc(free, 2)
                low_weights(0, 0)
                for k in range(HYT):
                    share["low_of_raw"](dve, PAIRS + k, y[1][:, k, :], y[0][:, k, :])
                schedule(one_tile, dve)


def merge_out(nc, ps, keep, share, x, out):
    merged, xr = share["gates"][:, 0], share["gates"][:, 1]
    with ExitStack() as ctx:
        m_parts = [sbuf(ctx, nc, n, [P, DT, S], F32R) for n in ("merged_high", "merged_low")]
        wo = [nc.alloc_sbuf_tensor_at(n, [P, KT, D], F32R, offset=keep[at]) for n, at in (("w_out_high", "xn_low_at"), ("w_out_low", "xn_high_at"))]
        x_in = sems(ctx, nc, *[f"xr_in{t}" for t in range(KT)])
        m_high, m_low, o_full, o_ready, stored = sems(ctx, nc, "merged_high_done", "merged_low_done", "o_full", "o_ready", "stored")
        with nc.Block() as block:
            @block.sync
            def _(sync):
                for k in range(2, KT):
                    share["load_raw"](sync, UPT + k)
                for t in range(KT):
                    sync.dma_start(xr[:, t, :], x[t * P:(t + 1) * P, :]).then_inc(x_in[t], 16)
                for t in range(KT):
                    sync.wait_ge(o_ready, 2 * t + 2)
                    sync.dma_start(out[t * P:(t + 1) * P, :], xr[:, t, :]).then_inc(stored, 16)
                sync.wait_ge(stored, 16 * KT)

            @block.tensor
            def _(pe):
                for t0 in range(0, KT, 4):
                    for k in range(KT):
                        if t0 == 0:
                            pe.wait_ge(share["raw_low"], UPT + k + 1)
                            pe.wait_ge(m_low, k + 1)
                        for t in range(t0, t0 + 4):
                            if t0 and k == 0:
                                pe.wait_ge(o_ready, 2 * (t - 4) + 2)
                            for mp, wp in SPLIT:
                                for h in range(2):
                                    mm = pe.matmul(ps[:, 2 * (t - t0) + h, :], m_parts[mp][:, k, t * P:(t + 1) * P], wo[wp][:, k, h * HALF:(h + 1) * HALF],
                                                   start=(k == 0 and mp == wp), stop=(k == KT - 1 and mp == 1))
                            if k == KT - 1:
                                mm.then_inc(o_full, 1)

            @block.scalar
            def _(act):
                for k in range(KT):
                    share["high_of_raw"](act, UPT + k, wo[0][:, k, :])
                    act.activation(m_parts[0][:, k, :], merged[:, k, :], ACT.Copy).then_inc(m_high, 1)

            @block.vector
            def _(dve):
                for k in range(KT):
                    share["low_of_raw"](dve, UPT + k, wo[1][:, k, :], wo[0][:, k, :])
                    dve.wait_ge(m_high, k + 1)
                    dve.tensor_tensor(m_parts[1][:, k, :], merged[:, k, :], m_parts[0][:, k, :].bitcast(F32), ALU.subtract).then_inc(m_low, 1)
                for t in range(KT):
                    dve.wait_ge(x_in[t], 16)
                    dve.wait_ge(o_full, t + 1)
                    for h in range(2):
                        dst = xr[:, t, h * HALF:(h + 1) * HALF]
                        dve.tensor_tensor(dst, ps[:, 2 * (t % 4) + h, :], dst, ALU.add).then_inc(o_ready, 1)


def program(nc, x, norm_g, w_in, b_in, conv_w, conv_b, hf_w1, hf_b1, hf_w2, hf_b2, hf_w3, hf_b3, hf_w4, hf_freq,
            hy_skip, q_norm_g, k_norm_g, w_hy_out, w_at_out, w_out, dft, z_t, decay, alibi, squares, out):
    v_tok = nc.dram_tensor("v_tok_d", (8, P, HY), F32).ap()
    x1_tok = nc.dram_tensor("x1_tok_d", (8, P, HY), F32).ap()
    x2_t = nc.dram_tensor("x2_t_d", (HY, S), F32).ap()
    y_t = nc.dram_tensor("y_t_d", (HY, S), F32).ap()
    att_t = nc.dram_tensor("att_t_d", (PAIRS * P, S), F32).ap()
    with ExitStack() as ctx:
        ps = ctx.enter_context(nc.psum_tensor("psum", [P, 8, HALF], F32))
        keep = {"xn_t": sbuf(ctx, nc, "xn_t", [P, KT, S])}
        keep["xn_low_at"] = nc.sbuf_base - KT * S * 4
        keep |= {"squares": sbuf(ctx, nc, "squares_sb", [P, 2, P]),
                "cols_in": sbuf(ctx, nc, "cols_in", [P, NB_IN + KT]), "cols_p": sbuf(ctx, nc, "cols_p", [P, ROWS_B])}
        [keep["passed"]] = sems(ctx, nc, "passed")
        keep["xn_high"] = sbuf(ctx, nc, "xn_high", [P, KT, S], F32R)
        keep["xn_high_at"] = nc.sbuf_base - KT * S * 4
        keep["xn_low"] = nc.alloc_sbuf_tensor_at("xn_low", [P, KT, S], F32R, offset=keep["xn_low_at"])
        keep["filter_sources"] = hf_w4[0], decay, hy_skip
        w = w_in[0]
        with ExitStack() as mixers:
            keep["w_at"] = sbuf(mixers, nc, "w_at", [P, 2, KT, P])
            keep["w_at_ready"] = sems(mixers, nc, "aw_ready0", "aw_ready1")
            with ExitStack() as hyena:
                keep["h_t"] = sbuf(hyena, nc, "h_t", [HD, S])
                keep["dft_sb"] = sbuf(hyena, nc, "dft_sb", [P, 38, P])
                keep["dec"] = sbuf(hyena, nc, "decay_chunk", [P, 2, NJ, CH])
                keep["w4c"] = sbuf(hyena, nc, "w4_chunk", [HD, 2, 2, CH])
                keep["skc"] = sbuf(hyena, nc, "skip_chunk", [1, 2, CH])
                keep["filt_in"] = sems(hyena, nc, "filt_in0", "filt_in1")
                [keep["dft_in"]] = sems(hyena, nc, "dft_in")
                with ExitStack() as first:
                    keep["w_hy"] = sbuf(first, nc, "w_hy", [P, 4, KT, P])
                    keep["w_hy_ready"] = sems(first, nc, *[f"w_hy_ready{s}" for s in range(4)])
                    normalise(nc, ps, keep, w, x[0], norm_g, b_in, conv_w[0], conv_b, (hf_b1, hf_b2, hf_b3, hf_freq), q_norm_g, k_norm_g, squares)
                    hyena_in(nc, ps, keep, w, v_tok, x1_tok, x2_t, z_t, (hf_w1[0], hf_w2[0], hf_w3[0]), dft)
                hyena_mix(nc, ps, keep, w, v_tok, x1_tok, x2_t, y_t)
            attention(nc, ps, keep, w, alibi, att_t)
        merge(nc, ps, keep, w, w_hy_out[0], w_at_out[0], w_out[0], y_t, att_t, x[0], out[0])


def shape_tables():
    import math
    import numpy as np

    f32 = np.float32
    a = np.arange(16)
    bq = np.arange(8)
    tau = 2.0 * np.pi

    def times(j):
        return (64 * a[:, None] + 8 * bq[None, :] + j).reshape(-1)

    col_b, col_c, col_m = (x.reshape(-1) for x in np.meshgrid(bq, np.arange(2), np.arange(8), indexing="ij"))
    m1 = np.zeros((8, 2, 128, 128))
    i2 = np.zeros((8, 2, 128, 128))
    for j in range(8):
        n = times(j)
        same = (n % 64 // 8)[:, None] == col_b[None, :]
        sign = np.where((n // 64) % 2, -1.0, 1.0)[:, None]
        for h in range(2):
            k1 = 2 * col_m[None, :] + h
            c = col_c[None, :]
            angle = tau * k1 * n[:, None] / 2048.0
            fwd = np.where(k1 > 0, np.where(c == 0, np.cos(angle), -np.sin(angle)), np.where(c == 0, 1.0, sign))
            inv = np.where(k1 > 0, np.where(c == 0, 2 * np.cos(angle), -2 * np.sin(angle)),
                           np.where(c == 0, 1.0, sign)) / 2048.0
            m1[j, h] = fwd * same
            i2[j, h] = (inv * same).T
    jj, bb, c = (x.reshape(-1) for x in np.meshgrid(np.arange(8), bq, np.arange(2), indexing="ij"))
    b = 8 * bb + jj
    k2 = np.arange(64)
    ang = tau * b[:, None] * k2[None, :] / 64.0
    cb = c[:, None]
    m2g = np.concatenate([np.where(cb == 0, np.cos(ang), np.sin(ang)),
                          np.where(cb == 0, -np.sin(ang), np.cos(ang))], 1)
    i1g = np.concatenate([np.where(cb == 0, np.cos(ang), np.sin(ang)),
                          np.where(cb == 0, -np.sin(ang), np.cos(ang))], 1).T
    q = np.arange(32)
    ang0 = tau * b[:, None] * q[None, :] / 64.0
    ang16 = tau * b[:, None] * (16 + 32 * q[None, :]) / 2048.0
    is0, is16 = (c == 0)[:, None], (c == 1)[:, None]
    im0 = -np.sin(ang0) * is0
    im0[:, 0] = np.where(c == 0, np.where(b % 2, -1.0, 1.0), 0.0)
    m2s = np.concatenate([np.cos(ang0) * is0, np.cos(ang16) * is16, im0, -np.sin(ang16) * is16], 1)
    w_re = np.where(q == 0, 1.0, 2.0)[None, :]
    jm0 = -2 * np.sin(ang0) * is0
    jm0[:, 0] = np.where(c == 0, np.where(b % 2, -1.0, 1.0), 0.0)
    i1s = np.concatenate([w_re * np.cos(ang0) * is0, 2 * np.cos(ang16) * is16, jm0, -2 * np.sin(ang16) * is16], 1).T
    conj = np.where(np.arange(128) < 64, 1.0, -1.0)[None, :]
    conj_s = conj.copy()
    conj_s[0, 64] = 1.0
    mats = np.stack([m2s, m2g, m2s * conj_s, m2g * conj, i1s, i1g])
    dft = np.concatenate([m1.reshape(16, 128, 128), mats, i2.reshape(16, 128, 128)])
    dft = np.ascontiguousarray(dft.transpose(1, 0, 2)).astype(f32)

    L, bands = 1024, 16
    order = np.concatenate([times(j) for j in range(8)])
    t = (np.arange(L, dtype=f32) / f32(L - 1)).astype(f32)
    w = (f32(tau) * np.arange(L, dtype=f32) / f32(L)).astype(f32)
    f = np.linspace(1e-4, bands - 1, bands, dtype=f32)
    fw = (f[None, :] * w[:, None]).astype(f32).astype(np.float64)
    z = np.concatenate([t[:, None], np.cos(fw), -np.sin(fw)], 1)
    z_t = np.ascontiguousarray(z[order].T).astype(f32)
    lo, hi = math.log(1e-2) / 1.5, math.log(1e-2) / 0.3
    deltas = np.abs(np.linspace(lo, hi, 768, dtype=f32))
    decay = np.exp(-(t[:, None] * deltas[None, :]).astype(f32).astype(np.float64))
    decay = np.ascontiguousarray(decay[order].reshape(8, 128, 768).transpose(1, 0, 2)).astype(f32)

    slopes = 2.0 ** (-8.0 * np.arange(1, 9) / 8.0)
    qi = np.arange(128)[:, None]
    rel = qi + 64 - np.arange(256)[None, :]
    in_band = np.abs(rel) <= 64
    k = np.arange(128)[None, :]
    rel2 = qi // 2 - k // 2
    same2 = qi % 2 == k % 2
    parts = []
    for s in slopes:
        parts.append(np.concatenate([np.where(in_band, -s * np.abs(rel), -1e30),
                                     np.where(in_band, -s * 4 * np.abs(rel), -1e30),
                                     np.where(same2, -s * 16 * np.abs(rel2), -1e30)], 1))
    alibi = (8.0 * np.stack(parts)).reshape(4, 2, 128, 640).transpose(0, 2, 1, 3)
    alibi = np.ascontiguousarray(alibi).astype(f32)
    eye = np.eye(128, dtype=f32)
    pair = np.kron(np.eye(2), np.ones((64, 64))).astype(f32)
    squares = np.ascontiguousarray(np.stack([eye, pair], 1))
    return {"dft": dft, "z_t": z_t, "decay": decay, "alibi": alibi, "squares": squares}


_INS = ["x", "norm_g", "w_in", "b_in", "conv_w", "conv_b", "hf_w1", "hf_b1", "hf_w2", "hf_b2", "hf_w3", "hf_b3", "hf_w4",
        "hf_freq", "hy_skip", "q_norm_g", "k_norm_g", "w_hy_out", "w_at_out", "w_out"]
_TABLES = ["dft", "z_t", "decay", "alibi", "squares"]


def kernel(**inputs):
    import numpy as _np
    import concourse.bacc as _bacc
    from concourse import mybir as _mybir
    from concourse.bass_utils import run_bass_kernel_spmd as _run

    nc = _bacc.Bacc("TRN2", target_bir_lowering=False, num_devices=1)
    tables = shape_tables()
    arrays, args = {}, {}
    for name in _INS + _TABLES:
        a = _np.ascontiguousarray(inputs[name] if name in inputs else tables[name])
        arrays[f"in_{name}_dram"] = a
        args[name] = nc.dram_tensor(f"in_{name}_dram", a.shape, _mybir.dt.from_np(a.dtype), kind="ExternalInput").ap()
    args["out"] = nc.dram_tensor("out_0_dram", (1, 1024, 1024), _mybir.dt.float32, kind="ExternalOutput").ap()
    program(nc, **args)
    r = _run(nc, [arrays], core_ids=[0])
    return r.results[0]["out_0_dram"]
```
